# Optimizing a Trainium2 kernel written in Bass

```python
import jax, jax.numpy as jnp
from jax import lax
import numpy as np

D_MODEL = 1024
BATCH = 1
SEQ = 128
DEPTH = 1
DEC_BATCH = 1
DEC_SEQ = 256
PAST_LEN = 128

GRID_W = 64
N_MIXERS = 2
N_SSM_LAYERS = (DEPTH + N_MIXERS - 1) // N_MIXERS
N_FNET_LAYERS = DEPTH // N_MIXERS
SSM_WIDTH = D_MODEL
SSM_GROUP = 16
SSM_GROUPS = SSM_WIDTH // SSM_GROUP
STATE_DIM = 64
FNET_GROUPS = 8
FNET_GROUP = D_MODEL // FNET_GROUPS
N_EXPERTS = 16
N_EXPERT_GROUPS = 4
EXPERTS_PER_GROUP = N_EXPERTS // N_EXPERT_GROUPS
TOP_K = 2
D_EXPERT = 1024
N_MOD = 6
EPS = 1e-6
DT_MIN = 1e-3
DT_MAX = 1e-1

kernel_name = "hybrid_s5_fnet_moe_diffusion_step"

def rms_norm(x, g):
    xf = x.astype(jnp.float32)
    y = xf * lax.rsqrt(jnp.mean(xf * xf, axis=-1, keepdims=True) + EPS)
    return (y * g.astype(jnp.float32)).astype(x.dtype)

def _linrec_combine(left, right):
    a1r, a1i, b1r, b1i = left
    a2r, a2i, b2r, b2i = right
    return (a2r * a1r - a2i * a1i,
            a2r * a1i + a2i * a1r,
            a2r * b1r - a2i * b1i + b2r,
            a2r * b1i + a2i * b1r + b2i)

def zoh_discretize(lam_re, lam_im, log_dt, b_re, b_im):
    f32 = jnp.float32
    lr = lam_re.astype(f32)
    li = lam_im.astype(f32)
    dt = jnp.exp(log_dt.astype(f32))[:, None]
    mag = jnp.exp(lr * dt)
    a_re = mag * jnp.cos(li * dt)
    a_im = mag * jnp.sin(li * dt)
    den = lr * lr + li * li
    nr = a_re - 1.0
    f_re = ((nr * lr + a_im * li) / den)[..., None]
    f_im = ((a_im * lr - nr * li) / den)[..., None]
    br = b_re.astype(f32)
    bi = b_im.astype(f32)
    return a_re, a_im, f_re * br - f_im * bi, f_re * bi + f_im * br

def ssm_scan(u_g, a_re, a_im, bb_re, bb_im, c_re, c_im, h0_re, h0_im, reverse):
    f32 = jnp.float32
    seq = u_g.shape[1]
    x_re = jnp.einsum("blgh,gph->blgp", u_g, bb_re)
    x_im = jnp.einsum("blgh,gph->blgp", u_g, bb_im)
    first, last = (-1, 0) if reverse else (0, -1)
    h0r = h0_re.astype(f32)
    h0i = h0_im.astype(f32)
    x_re = x_re.at[:, first].add(a_re * h0r - a_im * h0i)
    x_im = x_im.at[:, first].add(a_re * h0i + a_im * h0r)
    shape = (1, seq) + a_re.shape
    _, _, h_re, h_im = lax.associative_scan(
        _linrec_combine,
        (jnp.broadcast_to(a_re, shape), jnp.broadcast_to(a_im, shape), x_re, x_im),
        reverse=reverse, axis=1)
    y = (jnp.einsum("blgp,ghp->blgh", h_re, c_re.astype(f32))
         - jnp.einsum("blgp,ghp->blgh", h_im, c_im.astype(f32)))
    return y, h_re[:, last], h_im[:, last]

def ssm_mixer(h, w_in, lam_re, lam_im, log_dt, b_re, b_im, c_re, c_im, d_skip, w_glu,
              h0_re, h0_im):
    bsz, seq, _ = h.shape
    u = (h @ w_in).astype(jnp.float32)
    u_g = u.reshape(bsz, seq, SSM_GROUPS, SSM_GROUP)
    y = u * d_skip.astype(jnp.float32)
    fin_re, fin_im = [], []
    for d in range(2):
        a_re, a_im, bb_re, bb_im = zoh_discretize(lam_re[d], lam_im[d], log_dt[d],
                                                  b_re[d], b_im[d])
        y_d, f_re, f_im = ssm_scan(u_g, a_re, a_im, bb_re, bb_im, c_re[d], c_im[d],
                                   h0_re[:, d], h0_im[:, d], reverse=(d == 1))
        y = y + y_d.reshape(bsz, seq, SSM_WIDTH)
        fin_re.append(f_re)
        fin_im.append(f_im)
    val, gate = jnp.split(jax.nn.gelu(y).astype(h.dtype) @ w_glu, 2, axis=-1)
    return val * jax.nn.sigmoid(gate), jnp.stack(fin_re, axis=1), jnp.stack(fin_im, axis=1)

def fourier_mixer(h, w_out):
    bsz, seq, _ = h.shape
    u = h.astype(jnp.float32).reshape(bsz, seq, FNET_GROUPS, FNET_GROUP)
    f = jnp.fft.fft2(u, axes=(1, 3), norm="ortho")
    y = jnp.real(f).reshape(bsz, seq, D_MODEL).astype(h.dtype)
    return y @ w_out

def moe(h, router_w, router_b, w_gate, w_up, w_down):
    bsz, seq, dm = h.shape
    t = h.reshape(-1, dm)
    scores = jax.nn.sigmoid((t @ router_w).astype(jnp.float32))
    biased = scores + router_b.astype(jnp.float32)
    grp = biased.reshape(-1, N_EXPERT_GROUPS, EXPERTS_PER_GROUP)
    grp_score = lax.top_k(grp, TOP_K)[0].sum(-1)
    best = jnp.argmax(grp_score, axis=-1)
    mask = jnp.repeat(jax.nn.one_hot(best, N_EXPERT_GROUPS, dtype=jnp.bool_),
                      EXPERTS_PER_GROUP, axis=-1)
    _, top_idx = lax.top_k(jnp.where(mask, biased, -jnp.inf), TOP_K)
    top_w = jnp.take_along_axis(scores, top_idx, axis=-1)
    top_w = top_w / jnp.sum(top_w, axis=-1, keepdims=True)
    combine = jnp.einsum("nk,nke->ne", top_w,
                         jax.nn.one_hot(top_idx, N_EXPERTS, dtype=jnp.float32))
    g = jnp.einsum("nd,edf->nef", t, w_gate)
    u = jnp.einsum("nd,edf->nef", t, w_up)
    a = jax.nn.silu(g) * u * combine[:, :, None].astype(t.dtype)
    y = jnp.einsum("nef,efd->nd", a, w_down)
    return y.reshape(bsz, seq, dm)

def run_stream(x, cond, h0_re, h0_im, p):
    fin_re, fin_im = [], []
    for i in range(DEPTH):
        mod = (jax.nn.silu(cond) @ p["w_ada"][i] + p["b_ada"][i])[:, None, :]
        sh1, sc1, g1, sh2, sc2, g2 = jnp.split(mod, N_MOD, axis=-1)
        h = rms_norm(x, p["norm_mix"][i]) * (1 + sc1) + sh1
        j = i // N_MIXERS
        if i % N_MIXERS == 0:
            m, f_re, f_im = ssm_mixer(
                h, p["ssm_w_in"][j], p["ssm_lam_re"][j], p["ssm_lam_im"][j],
                p["ssm_log_dt"][j], p["ssm_b_re"][j], p["ssm_b_im"][j],
                p["ssm_c_re"][j], p["ssm_c_im"][j], p["ssm_d"][j], p["ssm_w_glu"][j],
                h0_re[:, j], h0_im[:, j])
            fin_re.append(f_re)
            fin_im.append(f_im)
        else:
            m = fourier_mixer(h, p["fnet_w_out"][j])
        x = x + g1 * m
        h = rms_norm(x, p["norm_ffn"][i]) * (1 + sc2) + sh2
        x = x + g2 * moe(h, p["router_w"], p["router_b"], p["moe_w_gate"][i],
                         p["moe_w_up"][i], p["moe_w_down"][i])
    return rms_norm(x, p["norm_final"]), jnp.stack(fin_re, axis=1), jnp.stack(fin_im, axis=1)

def setup_inputs(seed: int = 0) -> dict:
    key = jax.random.key(seed)
    ks = iter(jax.random.split(key, 40))
    f32 = jnp.float32

    def nrm(shape, scale):
        return scale * jax.random.normal(next(ks), shape, f32)

    st_shape = (DEC_BATCH, N_SSM_LAYERS, 2, SSM_GROUPS, STATE_DIM)
    n_idx = jnp.arange(STATE_DIM, dtype=f32)
    lam_shape = (N_SSM_LAYERS, 2, SSM_GROUPS, STATE_DIM)
    return {
        "x_prompt": nrm((BATCH, SEQ, D_MODEL), 1.0),
        "x_sample": nrm((DEC_BATCH, DEC_SEQ, D_MODEL), 1.0),
        "c": nrm((DEC_BATCH, D_MODEL), 1.0),
        "state_ssm_re": nrm(st_shape, 0.3),
        "state_ssm_im": nrm(st_shape, 0.3),
        "c_ctx": nrm((D_MODEL,), 1.0),
        "norm_mix": 1.0 + nrm((DEPTH, D_MODEL), 0.02),
        "norm_ffn": 1.0 + nrm((DEPTH, D_MODEL), 0.02),
        "w_ada": nrm((DEPTH, D_MODEL, N_MOD * D_MODEL), 0.5 * D_MODEL ** -0.5),
        "b_ada": nrm((DEPTH, N_MOD * D_MODEL), 0.02),
        "ssm_w_in": nrm((N_SSM_LAYERS, D_MODEL, SSM_WIDTH), D_MODEL ** -0.5),
        "ssm_lam_re": -0.5 + nrm(lam_shape, 0.01),
        "ssm_lam_im": jnp.pi * n_idx + nrm(lam_shape, 0.01),
        "ssm_log_dt": jax.random.uniform(next(ks), (N_SSM_LAYERS, 2, SSM_GROUPS), f32,
                                         np.log(DT_MIN), np.log(DT_MAX)),
        "ssm_b_re": nrm((N_SSM_LAYERS, 2, SSM_GROUPS, STATE_DIM, SSM_GROUP), (2 * SSM_GROUP) ** -0.5),
        "ssm_b_im": nrm((N_SSM_LAYERS, 2, SSM_GROUPS, STATE_DIM, SSM_GROUP), (2 * SSM_GROUP) ** -0.5),
        "ssm_c_re": nrm((N_SSM_LAYERS, 2, SSM_GROUPS, SSM_GROUP, STATE_DIM), STATE_DIM ** -0.5),
        "ssm_c_im": nrm((N_SSM_LAYERS, 2, SSM_GROUPS, SSM_GROUP, STATE_DIM), STATE_DIM ** -0.5),
        "ssm_d": nrm((N_SSM_LAYERS, SSM_WIDTH), 1.0),
        "ssm_w_glu": nrm((N_SSM_LAYERS, SSM_WIDTH, 2 * D_MODEL), SSM_WIDTH ** -0.5),
        "fnet_w_out": nrm((N_FNET_LAYERS, D_MODEL, D_MODEL), D_MODEL ** -0.5),
        "router_w": nrm((D_MODEL, N_EXPERTS), D_MODEL ** -0.5),
        "router_b": nrm((N_EXPERTS,), 0.01),
        "moe_w_gate": nrm((DEPTH, N_EXPERTS, D_MODEL, D_EXPERT), D_MODEL ** -0.5),
        "moe_w_up": nrm((DEPTH, N_EXPERTS, D_MODEL, D_EXPERT), D_MODEL ** -0.5),
        "moe_w_down": nrm((DEPTH, N_EXPERTS, D_EXPERT, D_MODEL), D_EXPERT ** -0.5),
        "norm_final": 1.0 + nrm((D_MODEL,), 0.02),
    }

def reference(x_prompt, x_sample, c, state_ssm_re, state_ssm_im, c_ctx,
              norm_mix, norm_ffn, w_ada, b_ada,
              ssm_w_in, ssm_lam_re, ssm_lam_im, ssm_log_dt, ssm_b_re, ssm_b_im,
              ssm_c_re, ssm_c_im, ssm_d, ssm_w_glu,
              fnet_w_out, router_w, router_b, moe_w_gate, moe_w_up, moe_w_down,
              norm_final):
    p = dict(norm_mix=norm_mix, norm_ffn=norm_ffn, w_ada=w_ada, b_ada=b_ada,
             ssm_w_in=ssm_w_in, ssm_lam_re=ssm_lam_re, ssm_lam_im=ssm_lam_im,
             ssm_log_dt=ssm_log_dt, ssm_b_re=ssm_b_re, ssm_b_im=ssm_b_im,
             ssm_c_re=ssm_c_re, ssm_c_im=ssm_c_im, ssm_d=ssm_d, ssm_w_glu=ssm_w_glu,
             fnet_w_out=fnet_w_out, router_w=router_w, router_b=router_b,
             moe_w_gate=moe_w_gate, moe_w_up=moe_w_up, moe_w_down=moe_w_down,
             norm_final=norm_final)
    zeros = jnp.zeros((x_prompt.shape[0], N_SSM_LAYERS, 2, SSM_GROUPS, STATE_DIM), jnp.float32)
    y_prompt, new_state_re, new_state_im = run_stream(x_prompt, c_ctx[None, :], zeros, zeros, p)
    y_sample, _, _ = run_stream(x_sample, c, state_ssm_re, state_ssm_im, p)
    return (y_prompt, y_sample, new_state_re, new_state_im)


_drawn_inputs = setup_inputs


def setup_inputs(seed=0):
    import zlib

    import numpy as np

    out = dict(_drawn_inputs(seed))
    spreads = {}
    factors = {'norm_mix': 3.237, 'ssm_lam_re': 14.291, 'norm_final': 7.795, 'norm_ffn': 3.336}
    for name, (base, spread) in spreads.items():
        noise = np.random.default_rng([zlib.crc32(name.encode()), seed]).standard_normal(out[name].shape)
        drawn = base * np.exp(spread * noise) if base else spread * noise
        out[name] = __import__('jax').numpy.asarray(drawn.astype(out[name].dtype))
    for name, factor in factors.items():
        out[name] = (out[name] * factor).astype(out[name].dtype)
    return out
```

```python
from contextlib import ExitStack
import math

import concourse.bass as bass
from concourse import mybir

F32 = mybir.dt.float32
I32 = mybir.dt.int32
U32 = mybir.dt.uint32
ALU = mybir.AluOpType
ACT = mybir.ActivationFunctionType
AX = mybir.AxisListType

P = 128
D = 1024
KT = D // P
T_CTX, T_LAT = 128, 256
T = T_CTX + T_LAT
NT = T // P
G, GS, NS = 64, 16, 64
GP = G // 2
DG = 2 * GP
L = 4
CC, CL = T_CTX // L, T_LAT // L
C = CC + CL
CX = C + 1
SLOTS = CX + 1
NP_V = L + 1
NE, NGRP, EPG = 16, 4, 4
FE = 1024
CAP = 96
TT = CAP // 32
ROUNDS = T // CAP
EPS = 1e-6
OOB = 1 << 20
UNIT = 2048
NU = 12
MAGIC = 12582912.0
LOG2E = 1.4426950408889634
LN2_HI, LN2_LO = 0.693359375, -2.12194440e-4
INV_2PI = 1.0 / (2.0 * math.pi)
TP1 = 6.28125
TP2 = 0.0019350051879882812
TP3 = 2.0 * math.pi - TP1 - TP2
PI_SAFE = 3.1415925
EXP_C = [1.0 / 5040, 1.0 / 720, 1.0 / 120, 1.0 / 24, 1.0 / 6, 0.5, 1.0]


def build(nc, x_prompt, x_sample, c, state_re, state_im, c_ctx, norm_mix, norm_ffn, w_ada, b_ada,
          w_in, lam_re, lam_im, log_dt, b_re, b_im, c_re, c_im, ssm_d, w_glu, router_w, router_b,
          w_gate, w_up, w_down, norm_final, y_prompt, y_sample, new_re, new_im):
    h2_d = nc.dram_tensor("h2_scratch", [T, D], F32, kind="Internal").ap()
    y2_d = nc.dram_tensor("y2_scratch", [2 * T, D], F32, kind="Internal").ap()
    list_d = nc.dram_tensor("slot_list", [NE * T, 2], I32, kind="Internal").ap()

    ctx = ExitStack()
    with ctx:
        def sb(name, shape, dt=F32):
            return ctx.enter_context(nc.sbuf_tensor(name, shape, dt))

        def sem(name):
            return ctx.enter_context(nc.semaphore(name))

        ring = sb("ring", [P, NU, UNIT])
        sreg = sb("sreg", [P, 2 * SLOTS * DG])
        vreg = sb("vreg", [P, 2 * DG * NP_V * GS])
        tmat = sb("tmat", [P, GP, L * GS])
        ada = sb("ada", [P, 3, 512])
        gains = sb("gains", [P, 512])
        ident = sb("ident", [P, P])
        bsel = sb("bsel", [P, 2, P])
        a4r = sb("a4r", [P, DG])
        a4i = sb("a4i", [P, 2, DG])
        h0 = sb("h0", [P, P])
        silu_c = sb("silu_c", [P, KT, 32])
        stat = sb("stat", [P, 16])
        scan_t = sb("scan_t", [P, 2, 2, P])
        cmb = sb("cmb", [P, 2, NT])
        dtab = sb("dtab", [P, 2, 8])
        i16 = sb("i16", [P, GS])
        sloti = sb("sloti", [P, 2, NT], U32)
        cmax = sb("cmax", [P, 1])
        cmaxi = sb("cmaxi", [P, 1], I32)
        gidx = sb("gidx", [P, 2], U32)
        sidx = sb("sidx", [P, 2], U32)
        pool_tick = sb("pool_tick", [1, 3])

        tab = tmat[:, :, :].rearrange("p g n -> p (g n)").rearrange("p (n g) -> p n g", g=DG)
        dskip = scan_t[:, :, :, :].rearrange("p a b n -> p (a b n)")[:, 0:256].rearrange(
            "p (a q h) -> p a q h", a=2, q=8)
        fins = scan_t[:, :, :, :].rearrange("p a b n -> p (a b n)")[0:2 * GP, 0:2 * P].rearrange(
            "p (d n) -> p d n", d=2)

        ada_w = ring[:, 0:2, :]
        uT = ring[:, 0:2, :].rearrange("p a b -> p (a b)")[:, 0:GP * CX].rearrange("p (g c) -> p g c", c=CX)
        w_pow = ring[:, 2:4, :].rearrange("p a (g k h) -> p a g k h", k=L, h=GS)
        u_c = ring[:, 2:4, :].rearrange("p a b -> p (a b)").rearrange("p (g i h) -> p g i h", i=L, h=GS)
        y_c = ring[:, 2:4, :].rearrange("p a b -> p (a b)").rearrange("p (i n) -> p i n", i=L)
        win = ring[:, 4:8, :].rearrange("p a b -> p (a b)").rearrange("p (k n) -> p k n", k=KT)
        pt = ring[:, 8:12, :].rearrange("p a b -> p (a b)").rearrange("p (g r s) -> p g r s", r=2, s=NS)

        S = sreg[:, :].rearrange("p (d c r g) -> p d c r g", d=2, c=SLOTS, r=2)
        off = [0]

        def cut(region, n):
            a = region[:, off[0]:off[0] + n]
            off[0] += n
            return a
        bs3 = cut(sreg, 3 * DG * GS).rearrange("p (r g h) -> p r g h", r=3, g=DG)
        cs3 = cut(sreg, 3 * DG * GS).rearrange("p (r g h) -> p r g h", r=3, g=DG)
        t2 = cut(sreg, GP * NP_V * GS)
        hT = cut(sreg, KT * T).rearrange("p (k t) -> p k t", k=KT)
        kpad = t2[:, 0:16 * 112].rearrange("p (a q w) -> p a q w", a=2, q=8)
        off[0] = 0
        bnat = cut(vreg, UNIT)
        cnat = cut(vreg, UNIT)
        lnat = cut(vreg, P)
        hnat = cut(vreg, P)
        dtnat = cut(vreg, 2)
        dtexp = cut(vreg, P)
        rows = cut(vreg, P)
        scr = cut(vreg, D)
        off[0] = 2 * DG * NP_V * GS - NT * D
        x_sb = cut(vreg, NT * D).rearrange("p (t n) -> p t n", t=NT)
        V = vreg[:, :].rearrange("p (g r k h) -> p g r k h", r=2, k=NP_V, h=GS)

        off[0] = 0
        yT = cut(sreg, KT * T).rearrange("p (k t) -> p k t", k=KT)
        x1 = cut(sreg, NT * D).rearrange("p (t n) -> p t n", t=NT)
        h2 = cut(sreg, NT * D).rearrange("p (t n) -> p t n", t=NT)
        rw = cut(sreg, KT * NE).rearrange("p (k e) -> p k e", k=KT)
        rb = cut(sreg, NE)
        route = cut(sreg, 24 * NT * NE).rearrange("p (a t e) -> p a t e", a=24, t=NT)
        e384 = cut(sreg, NT * NE).rearrange("p (t e) -> p t e", t=NT)
        rank = cut(sreg, NT * NE).rearrange("p (t e) -> p t e", t=NT)
        grank = cut(sreg, NT * NGRP).rearrange("p (t e) -> p t e", t=NT)
        tokv = cut(sreg, 4 * NT).bitcast(I32).rearrange("p (k t v) -> p k t v", k=2, t=NT)
        listi = cut(sreg, NE * T * 2 // P).bitcast(I32)
        iotas = cut(sreg, NT * NE).bitcast(I32).rearrange("p (t e) -> p t e", t=NT)
        tri = cut(sreg, 2 * P).rearrange("p (a n) -> p a n", a=2)
        assert off[0] <= 2 * SLOTS * DG
        off[0] = 0
        xg = cut(vreg, D)
        xgT = cut(vreg, KT * CAP).rearrange("p (k t) -> p k t", k=KT)
        sg = cut(vreg, TT * 256).rearrange("p (t n) -> p t n", t=TT)
        act_a = cut(vreg, TT * 256).rearrange("p (t n) -> p t n", t=TT)
        aT = cut(vreg, TT * 2 * P).rearrange("p (t c n) -> p t c n", t=TT, c=2)
        yrow = cut(vreg, D)
        h2T = cut(vreg, KT * T).rearrange("p (k t) -> p k t", k=KT)
        sig = cut(vreg, 512)
        prod = cut(vreg, 512)
        gfin = cut(vreg, D)
        assert off[0] <= 2 * DG * NP_V * GS
        yo = yT.rearrange("p k t -> p (k t)").rearrange("p (t n) -> p t n", t=NT)
        y2c = ring[:, 4:7, :].rearrange("p a b -> p (a b)").rearrange("p (k t n) -> p k t n", k=2, t=NT)
        m_out = h2

        ps = [ctx.enter_context(nc.psum_tensor(f"ps{i}", [P, 512], F32)) for i in range(8)]

        ld_cond, ld_x, ld_lam, ld_bc, ld_rows, ld_dtab = (sem(n) for n in (
            "ld_cond", "ld_x", "ld_lam", "ld_bc", "ld_rows", "ld_dtab"))
        ld_ada = [sem(f"ld_ada{i}") for i in range(2)]
        ld_win, ld_tmat, ld_glu, ld_xagain, ld_route, ld_y2 = (sem(n) for n in (
            "ld_win", "ld_tmat", "ld_glu", "ld_xagain", "ld_route", "ld_y2"))
        ld_unit = [sem(f"ld_unit{u}") for u in range(NU)]
        pool_zero, pool_const, pool_late = (sem(n) for n in ("pool_zero", "pool_const", "pool_late"))
        pe_tr, pe_ada, pe_bc, pe_w, pe_mod, pe_hT, pe_u, pe_uT, pe_k, pe_p, pe_y, pe_fin, pe_yT = (
            sem(n) for n in ("pe_tr", "pe_ada", "pe_bc", "pe_w", "pe_mod", "pe_hT", "pe_u", "pe_uT",
                             "pe_k", "pe_p", "pe_y", "pe_fin", "pe_yT"))
        pe_glu, pe_g1, pe_mod2, pe_h2T, pe_logit, pe_pos, pe_g2 = (sem(n) for n in (
            "pe_glu", "pe_g1", "pe_mod2", "pe_h2T", "pe_logit", "pe_pos", "pe_g2"))
        act_silu, act_sq, act_rt, act_trig, act_bc, act_pt, act_hT, act_u, act_uT, act_p, act_gelu = (
            sem(n) for n in ("act_silu", "act_sq", "act_rt", "act_trig", "act_bc", "act_pt", "act_hT",
                             "act_u", "act_uT", "act_p", "act_gelu"))
        act_yT, act_sig, act_h2T, act_score, act_fin, act_h0 = (sem(n) for n in (
            "act_yT", "act_sig", "act_h2T", "act_score", "act_fin", "act_h0"))
        dve_done = sem("dve_done")
        dve_dt, dve_trig, dve_bbar, dve_cs, dve_w, dve_v, dve_ms, dve_ada, dve_h, dve_k, dve_uT, dve_p = (
            sem(n) for n in ("dve_dt", "dve_trig", "dve_bbar", "dve_cs", "dve_w", "dve_v", "dve_ms",
                             "dve_ada", "dve_h", "dve_k", "dve_uT", "dve_p"))
        dve_h0, dve_scan, dve_x1, dve_h2, dve_mask, dve_slot, dve_cmax, dve_x2, dve_out = (sem(n) for n in (
            "dve_h0", "dve_scan", "dve_x1", "dve_h2", "dve_mask", "dve_slot", "dve_cmax", "dve_x2", "dve_out"))
        st_list, st_h2, st_out, st_scatter = (sem(n) for n in ("st_list", "st_h2", "st_out", "st_scatter"))
        unit_free, ld_idx, ld_xg, xt_ps, xt_ev, silu_done, prod_done, at_ps, at_ev, y_ev, ld_sidx, y_sent = (
            sem(n) for n in ("unit_free", "ld_idx", "ld_xg", "xt_ps", "xt_ev", "silu_done", "prod_done",
                             "at_ps", "at_ev", "y_ev", "ld_sidx", "y_sent"))

        y_free = sem("y_free")
        ticks = [sem("gather_tick"), sem("send_tick"), y_free]

        flat_s = sreg[:, :]
        FS = 2 * SLOTS * DG

        def chunk_states(d0, slot0, dslot, swap):
            first = slot0 * DG + (GP if swap else 0)
            return bass.AP(flat_s.tensor, flat_s.offset + first,
                           [[FS, P], [(SLOTS + dslot) * DG, 2], [-GP if swap else GP, 2], [1, GP]])

        def lam_rows(a):
            return a.rearrange("a d (g i) s -> (a d g) (i s)", i=2)

        block = ctx.enter_context(nc.Block())

        @block.sync
        def _(sp):
            def ada_piece(n):
                b, k = divmod(n, KT)
                if n >= 2:
                    sp.wait_ge(pe_ada, n - 1)
                sp.dma_start(ada_w[:, n % 2, :],
                             w_ada[0, k * P:(k + 1) * P, b * UNIT:(b + 1) * UNIT]).then_inc(ld_ada[n % 2], 16)
            for t in range(NT):
                src = x_prompt[0] if t == 0 else x_sample[0, (t - 1) * P:t * P, :]
                sp.dma_start(x_sb[:, t, :], src).then_inc(ld_x, 16)
            for n in range(KT):
                ada_piece(n)
            for k in range(KT):
                sp.dma_start(win[:, k, :], w_in[0, k * P:(k + 1) * P, :]).then_inc(ld_win, 16)
            for n in range(KT, 3 * KT):
                ada_piece(n)
            for k in range(KT):
                if k == 0:
                    sp.wait_ge(pe_u, 8)
                if k == 4:
                    sp.wait_ge(dve_k, 1)
                    for i in range(2):
                        for j in range(L):
                            for q in range(4):
                                dst = tmat[64 * i + 16 * j:64 * i + 16 * j + 16, q:GP:4, :]
                                sp.dma_start(dst, kpad[32 * q:32 * q + 16, i, :, (3 - j) * GS:(7 - j) * GS]
                                             ).then_inc(ld_tmat, 16)
                    sp.wait_ge(pe_p, 32)
                sp.dma_start(ring[:, 4 + k, :], w_glu[0, k * P:(k + 1) * P, :]).then_inc(ld_glu, 16)
            for r, dst in ((0, new_re), (1, new_im)):
                for d in range(2):
                    if r == 0:
                        sp.wait_ge(act_fin, d + 1)
                    sp.dma_start(dst[0, 0, d].rearrange("(g i) s -> g (i s)", i=2),
                                 fins[r * GP:(r + 1) * GP, d, :]).then_inc(st_out, 16)
            sp.wait_ge(pe_y, 8)
            for t in range(NT):
                src = x_prompt[0] if t == 0 else x_sample[0, (t - 1) * P:t * P, :]
                sp.dma_start(x1[:, t, :], src).then_inc(ld_xagain, 16)
            sp.dma_start(rw, router_w.rearrange("(k p) e -> p k e", p=P)).then_inc(ld_route, 16)
            sp.dma_start(rb, router_b.rearrange("(a e) -> a e", a=1).broadcast_to((P, NE))).then_inc(ld_route, 16)
            sp.dma_start(gfin, norm_final.rearrange("(a e) -> a e", a=1).broadcast_to((P, D))).then_inc(ld_route, 16)

            def load_unit(u, e):
                if u < KT:
                    for h, w in enumerate((w_gate, w_up)):
                        sp.dma_start(ring[:, u, h * D:(h + 1) * D],
                                     w[0, bass.ds(e, 1), u * P:(u + 1) * P, :].rearrange("a p n -> (a p) n")
                                     ).then_inc(ld_unit[u], 16)
                else:
                    for h in range(2):
                        k = 2 * (u - KT) + h
                        sp.dma_start(ring[:, u, h * D:(h + 1) * D],
                                     w_down[0, bass.ds(e, 1), k * P:(k + 1) * P, :].rearrange("a p n -> (a p) n")
                                     ).then_inc(ld_unit[u], 16)

            sp.wait_ge(pe_glu, 12)
            for u in range(NU):
                load_unit(u, 0)
            with sp.Fori(1, NE) as e:
                for u in range(NU):
                    sp.wait_ge(unit_free, e * NU + (u + 1 - NU))
                    load_unit(u, e)
            sp.wait_ge(y_sent, 16 * NE)
            v = sp.value_load(cmaxi[0:1, 0:1], min_val=0, max_val=T)
            with sp.If(v > CAP):
                with sp.Fori(1, ROUNDS) as r:
                    with sp.Fori(0, NE) as e:
                        for u in range(NU):
                            sp.wait_ge(unit_free, r * (NE * NU) + e * NU + (u + 1 - NU))
                            load_unit(u, e)
                sp.wait_ge(y_sent, 16 * NE * ROUNDS)
            sp.nop()
            for k in range(2):
                sp.dma_start(y2c[:, k, :, :], y2_d[k * T:(k + 1) * T, :].rearrange("(t p) n -> p t n", p=P)
                             ).then_inc(ld_y2, 16)
            for t in range(NT):
                sp.wait_ge(dve_out, t + 1)
                dst = y_prompt[0] if t == 0 else y_sample[0, (t - 1) * P:t * P, :]
                sp.dma_start(dst, yo[:, t, :]).then_inc(st_out, 16)
            sp.wait_ge(st_out, 16 * (4 + NT))
            sp.wait_ge(st_h2, 16 * NT)
            sp.wait_ge(st_list, 16)
            sp.wait_ge(st_scatter, 16 * 2 * NT)

        @block.gpsimd
        def _(pool):
            n = [0]

            def after(ins):
                n[0] += 1
                ins.then_inc(pool_const, 1)
                pool.wait_ge(pool_const, n[0])
            pool.memset(ada[:], 0.0).then_inc(pool_zero, 1)
            pool.memset(gains[:], 0.0).then_inc(pool_zero, 1)
            pool.memset(dtab[:], 0.0).then_inc(pool_zero, 1)
            pool.memset(silu_c[:], 0.0).then_inc(pool_zero, 1)
            after(pool.memset(ident[:], 0.0))
            after(pool.affine_select(out=ident[:], in_=ident[:], compare_op=ALU.not_equal, fill=1.0, base=0,
                                     pattern=[[-1, P]], channel_multiplier=1))
            after(pool.memset(bsel[:], 0.0))
            for cond in range(2):
                for j in range(4):
                    after(pool.affine_select(out=bsel[:, cond, :], in_=bsel[:, cond, :], compare_op=ALU.not_equal,
                                             fill=1.0, base=-(32 * j + cond), pattern=[[0, P]],
                                             channel_multiplier=1))
            assert n[0] == 11
            pool.wait_ge(pe_y, 8)
            pool.wait_ge(pe_fin, 2)
            n[0] = 0

            def late(ins):
                n[0] += 1
                ins.then_inc(pool_late, 1)
                pool.wait_ge(pool_late, n[0])
            late(pool.memset(tri, 1.0))
            late(pool.affine_select(out=tri[:, 0, :], in_=tri[:, 0, :], compare_op=ALU.is_gt, fill=0.0, base=0,
                                    pattern=[[1, P]], channel_multiplier=-1))
            late(pool.iota(iotas, pattern=[[0, NT], [T, NE]], base=0, channel_multiplier=0))
            late(pool.tensor_copy(e384, iotas))
            late(pool.iota(iotas, pattern=[[0, NT], [-1, NE]], base=NE, channel_multiplier=0))
            late(pool.tensor_copy(rank, iotas))
            late(pool.iota(iotas[:, :, 0:NGRP], pattern=[[0, NT], [-1, NGRP]], base=NGRP, channel_multiplier=0))
            late(pool.tensor_copy(grank, iotas[:, :, 0:NGRP]))
            for k in range(2):
                late(pool.iota(tokv[:, k, :, 0], pattern=[[P, NT]], base=0, channel_multiplier=1))
                late(pool.iota(tokv[:, k, :, 1], pattern=[[P, NT]], base=k * T, channel_multiplier=1))
            late(pool.memset(listi, OOB))
            assert n[0] == 13
            pool.dma_start(list_d.rearrange("(p a) v -> p (a v)", p=P), listi).then_inc(st_list, 16)
            pool.wait_ge(dve_scan, 1)
            pool.wait_ge(pe_y, 8)
            pool.memset(xg, 0.0).then_inc(pool_late, 1)
            pool.wait_ge(pool_late, 14)
            pool.wait_ge(st_list, 16)
            pool.wait_ge(dve_slot, 1)
            for k in range(2):
                for t in range(NT):
                    pool.indirect_dma_start(out=list_d, out_offset=bass.IndirectOffsetOnAxis(
                        ap=sloti[:, k, t:t + 1], axis=0), in_=tokv[:, k, t, :], in_offset=None,
                        bounds_check=NE * T - 1, oob_is_err=False).then_inc(st_scatter, 16)
            pool.wait_ge(st_scatter, 16 * 2 * NT)
            pool.wait_ge(st_h2, 16 * NT)
            pool.wait_ge(dve_cmax, 1)
            last_token = pool.to_reg(T - 1)
            last_row = pool.to_reg(2 * T - 1)

            def carry_waits(which, before):
                pool.wait_ge(ticks[which], before + 1)
                pool.tensor_tensor(pool_tick[:, which:which + 1], ident[0:1, 0:1], ident[0:1, 0:1], ALU.mult
                                   ).then_inc(ticks[which], 1)

            def gather(base, nth, used):
                if used is not None:
                    pool.wait_ge(ld_xg, nth * 16)
                pool.dma_start(gidx[0:CAP, :], list_d[bass.ds(base, CAP), :].bitcast(U32)).then_inc(ld_idx, 16)
                pool.wait_ge(ld_idx, nth * 16 + 16)
                if used is not None:
                    pool.wait_ge(xt_ps, used)
                carry_waits(0, nth)
                pool.indirect_dma_start(out=xg[0:CAP, :], out_offset=None, in_=h2_d,
                                        in_offset=bass.IndirectOffsetOnAxis(ap=gidx[0:CAP, 0:1], axis=0),
                                        bounds_check=last_token, oob_is_err=False).then_inc(ld_xg, 16)

            def send(base, it):
                pool.dma_start(sidx[0:CAP, :], list_d[bass.ds(base, CAP), :].bitcast(U32)).then_inc(ld_sidx, 16)
                pool.wait_ge(ld_sidx, it * 16 + 16)
                pool.wait_ge(y_ev, it * 12 + 24)
                carry_waits(1, it)
                pool.indirect_dma_start(out=y2_d, out_offset=bass.IndirectOffsetOnAxis(
                    ap=sidx[0:CAP, 1:2], axis=0), in_=yrow[0:CAP, :], in_offset=None,
                    bounds_check=last_row, oob_is_err=False).then_inc(y_sent, 16)
                pool.wait_ge(y_sent, it * 16 + 16)
                carry_waits(2, it)

            for which in range(3):
                pool.sem_inc(ticks[which], 1)
            gather(0, 0, None)
            with pool.Fori(0, NE - 1) as e:
                gather(e * T + T, e + 1, e + 1)
                send(e * T, e)
            send((NE - 1) * T, NE - 1)
            v = pool.value_load(cmaxi[0:1, 0:1], min_val=0, max_val=T)
            with pool.If(v > CAP):
                with pool.Fori(1, ROUNDS) as r:
                    gather(r * CAP, r * NE, r * NE)
                    with pool.Fori(0, NE - 1) as e:
                        gather(e * T + T + r * CAP, r * NE + e + 1, r * NE + e + 1)
                        send(e * T + r * CAP, r * NE + e)
                    send((NE - 1) * T + r * CAP, r * NE + NE - 1)
            pool.nop()

        @block.scalar
        def _(act):
            act.dma_start(rows[0:8, :], c_ctx.rearrange("(k p) -> k p", p=P)).then_inc(ld_cond, 16)
            act.dma_start(rows[8:16, :], c[0].rearrange("(k p) -> k p", p=P)).then_inc(ld_cond, 16)
            act.dma_start(lnat[0:DG, :], lam_rows(lam_re)).then_inc(ld_lam, 16)
            act.dma_start(lnat[DG:P, :], lam_rows(lam_im)).then_inc(ld_lam, 16)
            act.dma_start(dtnat[0:DG, :], log_dt.rearrange("a d (g i) -> (a d g) i", i=2)).then_inc(ld_lam, 16)
            act.dma_start(hnat[0:DG, :], state_re[0].rearrange("a d (g i) s -> (a d g) (i s)", i=2)).then_inc(ld_lam, 16)
            act.dma_start(hnat[DG:P, :], state_im[0].rearrange("a d (g i) s -> (a d g) (i s)", i=2)).then_inc(ld_lam, 16)
            for r, (b, cc) in enumerate(((b_re, c_re), (b_im, c_im))):
                act.dma_start(bnat[r * DG:(r + 1) * DG, :], b.rearrange("a d (g i) s h -> (a d g) (i s h)", i=2)
                              ).then_inc(ld_bc, 16)
                for i in range(2):
                    act.dma_start(cnat[r * DG:(r + 1) * DG, :].rearrange("p (h i s) -> p i h s", h=GS, i=2)[:, i],
                                  cc.rearrange("a d (g i) h s -> i (a d g) h s", i=2)[i]).then_inc(ld_bc, 16)
            act.wait_ge(pool_zero, 4)
            rows_b = b_ada.rearrange("o (b j n) -> o b j n", b=3, n=512)
            for j in range(4):
                for cond in range(2):
                    r = 32 * j + cond
                    act.dma_start(ada[r:r + 1, :, :], rows_b[:, :, j, :]).then_inc(ld_rows, 16)
                    gain = (norm_ffn if j < 2 else norm_mix)[0:1, (j % 2) * 512:(j % 2 + 1) * 512]
                    act.dma_start(gains[r:r + 1, :], gain).then_inc(ld_rows, 16)
            for q in range(4):
                for i in range(2):
                    act.dma_start(dtab[32 * q:32 * q + 16, i, :], ssm_d[0].rearrange(
                        "(m q i h) -> q i h m", m=8, q=4, i=2)[q, i], allow_slow_non_contiguous=True
                        ).then_inc(ld_dtab, 16)

            act.wait_ge(pe_tr, 1)
            act.activation(silu_c[:, :, 0:2].rearrange("p k c -> p c k"),
                           ps[3][:, 0:16].rearrange("p (c k) -> p c k", c=2), ACT.Silu).then_inc(act_silu, 1)
            act.wait_ge(pe_tr, 2)
            act.activation(h0[:], ps[4][:, 0:P], ACT.Copy).then_inc(act_h0, 1)
            braw = t2[:, 0:2 * DG * GS].rearrange("p (r g h) -> p r g h", r=2, h=GS)
            for m in range(4):
                act.wait_ge(pe_bc, m + 1)
                act.activation(braw[:, :, :, 4 * m:4 * m + 4],
                               ps[5 + m % 2][:, :].rearrange("p (h r g) -> p r g h", h=4, r=2), ACT.Copy
                               ).then_inc(act_bc, 1)
            act.wait_ge(dve_trig, 1)
            act.activation(tab[:, 7, :], tab[:, 5, :], ACT.Sin).then_inc(act_trig, 1)
            act.activation(tab[:, 8, :], tab[:, 6, :], ACT.Sin).then_inc(act_trig, 1)
            for m in range(4):
                act.wait_ge(pe_bc, 5 + m)
                src = ps[5 + m % 2][:, :].rearrange("p (h r g) -> p r g h", h=4, r=2)
                act.activation(cs3[:, 0, :, 4 * m:4 * m + 4], src[:, 0], ACT.Copy)
                act.activation(cs3[:, 1, :, 4 * m:4 * m + 4], src[:, 1], ACT.Copy, scale=-1.0)
                act.activation(cs3[:, 2, :, 4 * m:4 * m + 4], src[:, 0], ACT.Copy, scale=-1.0).then_inc(act_bc, 1)
            act.wait_ge(ld_x, 16 * NT)
            for t in range(NT):
                if t:
                    act.wait_ge(act_sq, t)
                act.activation(scr, x_sb[:, t, :], ACT.Square, accum_out=stat[:, t:t + 1]).then_inc(act_sq, 1)
            act.wait_ge(dve_ms, 1)
            act.activation(stat[:, 4:4 + NT], stat[:, 4:4 + NT], ACT.Sqrt).then_inc(act_rt, 1)
            for m in range(16):
                r = (m // 4) % 2
                g0 = (m // 8) * GP + (m % 4) * 8
                act.wait_ge(pe_w, m + 1)
                for i in range(2):
                    bank = ps[3 + 2 * (m % 2) + i]
                    act.activation(pt[64 * i:64 * i + 64, g0:g0 + 8, r, :],
                                   bank[64 * i:64 * i + 64, :].rearrange("p (g s) -> p g s", s=NS), ACT.Copy
                                   ).then_inc(act_pt, 1)
            for m in range(2 * NT):
                t, k0 = m // 2, 4 * (m % 2)
                act.wait_ge(pe_hT, m + 1)
                act.activation(hT[:, k0:k0 + 4, t * P:(t + 1) * P],
                               ps[4 + m % 2][:, :].rearrange("p (k n) -> p k n", k=4), ACT.Copy).then_inc(act_hT, 1)
            for m in range(8):
                i, half = m // 2, m % 2
                act.wait_ge(pe_u, m + 1)
                act.activation(u_c[0:C, 32 * half:32 * half + 32, i, :],
                               ps[4 + m % 2][0:C, :].rearrange("p (g h) -> p g h", h=GS), ACT.Copy
                               ).then_inc(act_u, 1)
            for m in range(0, 8, 2):
                act.wait_ge(pe_uT, m + 1)
                src = ps[4 + m % 4][:, 0:4 * C].rearrange("p (g c) -> p g c", c=C)
                act.activation(uT[:, 4 * m:4 * m + 4, 0:CC], src[:, :, 0:CC], ACT.Copy)
                act.activation(uT[:, 4 * m:4 * m + 4, CC + 1:CX], src[:, :, CC:C], ACT.Copy).then_inc(act_uT, 1)
            for m in range(32):
                d, g0 = m // 16, 2 * (m % 16)
                act.wait_ge(pe_p, m + 1)
                if m == 0:
                    act.wait_ge(dve_k, 1)
                    act.wait_ge(ld_tmat, 16 * 32)
                act.activation(S[0:64, d, 1 - d:1 - d + CX, :, g0:g0 + 2].rearrange("p c r g -> p g r c"),
                               ps[2 * (m % 4)][0:64, 0:4 * CX].rearrange("p (g r c) -> p g r c", g=2, r=2),
                               ACT.Copy).then_inc(act_p, 1)
            for d in range(2):
                act.wait_ge(pe_fin, d + 1)
                act.activation(fins[:, d, :], ps[6 + d][0:2 * GP, 0:P], ACT.Copy).then_inc(act_fin, 1)
            for m in range(8):
                gb, i = m // 2, m % 2
                act.wait_ge(pe_y, m + 1)
                dst = y_c[0:CX, :, :].rearrange("p i (b g a h) -> p b g a i h", b=4, a=2, h=GS)[:, gb, :, i]
                act.activation(dst, ps[m % 4][0:CX, :].rearrange("p (g i h) -> p g i h", g=8, i=L),
                               ACT.Gelu_apprx_tanh).then_inc(act_gelu, 1)
            for k in range(KT):
                act.wait_ge(pe_yT, k + 1)
                src = ps[4 + k % 4][:, 0:L * CX].rearrange("p (i c) -> p c i", i=L)
                dst = yT[:, k, :].rearrange("p (c i) -> p c i", i=L)
                act.activation(dst[:, 0:CC, :], src[:, 0:CC, :], ACT.Copy)
                act.activation(dst[:, CC:C, :], src[:, CC + 1:CX, :], ACT.Copy).then_inc(act_yT, 1)
            for m in range(6):
                act.wait_ge(pe_glu, 2 * m + 2)
                if m:
                    act.wait_ge(dve_x1, m)
                act.activation(sig, ps[2 * (m % 2) + 1][:, :], ACT.Sigmoid).then_inc(act_sig, 1)
            act.wait_ge(dve_x1, 6)
            for t in range(NT):
                if t:
                    act.wait_ge(act_sq, NT + t)
                act.activation(yrow, x1[:, t, :], ACT.Square, accum_out=stat[:, t:t + 1]).then_inc(act_sq, 1)
            act.wait_ge(dve_ms, 2)
            act.activation(stat[:, 4:4 + NT], stat[:, 4:4 + NT], ACT.Sqrt).then_inc(act_rt, 1)
            for m in range(2 * NT):
                t, k0 = m // 2, 4 * (m % 2)
                act.wait_ge(pe_h2T, m + 1)
                act.activation(h2T[:, k0:k0 + 4, t * P:(t + 1) * P],
                               ps[4 + m % 2][:, :].rearrange("p (k n) -> p k n", k=4), ACT.Copy).then_inc(act_h2T, 1)
                if m % 2:
                    act.wait_ge(dve_h2, t + 1)
                    act.dma_start(h2_d[t * P:(t + 1) * P, :], h2[:, t, :]).then_inc(st_h2, 16)
            act.wait_ge(pe_logit, NT)
            act.activation(route[:, 0], ps[6][:, 0:NT * NE].rearrange("p (t e) -> p t e", t=NT), ACT.Sigmoid
                           ).then_inc(act_score, 1)

            def expert(it):
                for t in range(TT):
                    act.wait_ge(unit_free, it * NU + KT)
                    act.activation(sg[:, t, :], ps[t][:, 0:256], ACT.Silu).then_inc(silu_done, 1)
                act.wait_ge(at_ps, it * TT + 2)
                act.activation(aT[:, 0:2, :, :], ps[7][:, :].rearrange("p (t c n) -> p t c n", t=2, c=2), ACT.Copy
                               ).then_inc(at_ev, 1)
                act.wait_ge(at_ps, it * TT + 3)
                act.activation(aT[:, 2, :, :], ps[4][:, 256:512].rearrange("p (c n) -> p c n", c=2), ACT.Copy
                               ).then_inc(at_ev, 1)
                act.wait_ge(unit_free, it * NU + NU)
                act.wait_ge(y_free, it + 1)
                for t in range(TT):
                    for j in range(2):
                        src = ps[3 + t // 2][32 * j:32 * j + 32, 256 * (t % 2):256 * (t % 2) + 256]
                        act.activation(yrow[32 * t:32 * t + 32, 256 * j:256 * j + 256], src, ACT.Copy
                                       ).then_inc(y_ev, 1)
            act.wait_ge(dve_cmax, 1)
            with act.Fori(0, NE) as e:
                expert(e)
            v = act.value_load(cmaxi[0:1, 0:1], min_val=0, max_val=T)
            with act.If(v > CAP):
                with act.Fori(1, ROUNDS) as r:
                    with act.Fori(0, NE) as e:
                        expert(r * NE + e)
            act.nop()
            for t in range(NT):
                act.wait_ge(dve_x2, t + 1)
                act.activation(h2[:, t, :], x1[:, t, :], ACT.Square, accum_out=stat[:, t:t + 1]).then_inc(act_sq, 1)
                act.wait_ge(dve_ms, 3 + t)
                act.activation(stat[:, 4 + t:5 + t], stat[:, 4 + t:5 + t], ACT.Sqrt).then_inc(act_rt, 1)

        @block.tensor
        def _(pe):
            def ada_piece(n):
                b, k = divmod(n, KT)
                pe.wait_ge(ld_ada[n % 2], 16 * (n // 2 + 1))
                for j in range(4):
                    last = pe.matmul(ps[b][32 * j:32 * j + 32, :], silu_c[:, k, :],
                                     ada_w[:, n % 2, j * 512:(j + 1) * 512], start=(k == 0), stop=(k == KT - 1))
                last.then_inc(pe_ada, 1)

            def spread(bank, b, j, cond):
                return pe.matmul(bank[:, :], bsel[32 * j:32 * j + 32, cond, :], ada[32 * j:32 * j + 32, b, :],
                                 start=True, stop=True)

            pe.wait_ge(pool_const, 11)
            pe.wait_ge(ld_cond, 32)
            pe.transpose(ps[3][:, 0:16], rows[0:16, :], ident[0:16, 0:16]).then_inc(pe_tr, 1)
            pe.wait_ge(ld_lam, 16 * 5)
            pe.wait_ge(dve_dt, 1)
            pe.transpose(ps[4][:, 0:P], hnat, ident[:])
            pe.transpose(ps[7][:, 0:P], lnat, ident[:])
            pe.transpose(ps[7][:, P:P + DG], dtexp[0:DG, :], ident[0:DG, 0:DG]).then_inc(pe_tr, 1)
            pe.wait_ge(ld_bc, 16 * 6)
            for m in range(8):
                nat = bnat if m < 4 else cnat
                if m >= 2:
                    pe.wait_ge(act_bc, m - 1)
                for h in range(4 * (m % 4), 4 * (m % 4) + 4):
                    if m < 4:
                        src = nat.rearrange("p (n h) -> p n h", h=GS)[:, :, h]
                    else:
                        src = nat[:, h * P:(h + 1) * P]
                    last = pe.transpose(ps[5 + m % 2][:, (h % 4) * P:(h % 4 + 1) * P], src, ident[:])
                last.then_inc(pe_bc, 1)
            pe.wait_ge(act_silu, 1)
            for n in range(KT):
                ada_piece(n)
            for m in range(16):
                batch = m // 4
                if m >= 2:
                    pe.wait_ge(act_pt, 2 * (m - 1))
                pe.wait_ge(dve_w, batch + 1)
                for g in range(8 * (m % 4), 8 * (m % 4) + 8):
                    for i in range(2):
                        last = pe.matmul(ps[3 + 2 * (m % 2) + i][64 * i:64 * i + 64, (g % 8) * NS:(g % 8 + 1) * NS],
                                         w_pow[64 * i:64 * i + 64, batch % 2, g, :, :].rearrange("p k h -> p (k h)"),
                                         ident[64 * i:64 * i + 64, 64 * i:64 * i + 64], start=True, stop=True)
                last.then_inc(pe_w, 1)
            pe.wait_ge(act_pt, 32)
            pe.wait_ge(dve_ada, 1)
            for cond in range(2):
                if cond:
                    pe.wait_ge(dve_h, 1)
                for b in range(2):
                    spread(ps[b], 0, 2 + b, cond)
                    last = spread(ps[2 + b], 0, b, cond)
                last.then_inc(pe_mod, 1)
            for m in range(2 * NT):
                t, k0 = m // 2, 4 * (m % 2)
                pe.wait_ge(dve_h, t + 1)
                if m >= 2:
                    pe.wait_ge(act_hT, m - 1)
                for k in range(k0, k0 + 4):
                    last = pe.transpose(ps[4 + m % 2][:, (k % 4) * P:(k % 4 + 1) * P],
                                        x_sb[:, t, k * P:(k + 1) * P], ident[:])
                last.then_inc(pe_hT, 1)
            pe.wait_ge(act_hT, 6)
            pe.wait_ge(ld_win, 16 * KT)
            for m in range(8):
                i, half = m // 2, m % 2
                if m >= 2:
                    pe.wait_ge(act_u, m - 1)
                for k in range(KT):
                    last = pe.matmul(ps[4 + m % 2][0:C, :], hT[:, k, i:T:L], win[:, k, half * 512:(half + 1) * 512],
                                     start=(k == 0), stop=(k == KT - 1))
                last.then_inc(pe_u, 1)
                ada_piece(KT + 2 * m)
                ada_piece(KT + 2 * m + 1)
            pe.wait_ge(act_u, 8)
            for m in range(8):
                if m >= 4:
                    pe.wait_ge(act_uT if m % 2 == 0 else dve_uT, (m - 4) // 2 + (1 if m % 2 == 0 else 2))
                for g in range(4 * m, 4 * m + 4):
                    src = u_c[0:C, 2 * g:2 * g + 2, :, :].rearrange("p i j h -> p (i j h)")
                    last = pe.transpose(ps[4 + m % 4][:, (g % 4) * C:(g % 4 + 1) * C], src, ident[0:C, 0:C])
                last.then_inc(pe_uT, 1)
            pe.wait_ge(dve_v, 4)
            for i in range(2):
                for mq in range(2):
                    bank = ps[2 * i + mq]
                    for m4 in range(4):
                        for q in range(4):
                            g = 4 * (4 * mq + m4) + q
                            out = bank[32 * q:32 * q + 32, 112 * m4:112 * m4 + 112]
                            for d in range(2):
                                for r in range(2):
                                    o = ((1 + r) * DG + d * GP + g) * GS
                                    lhs = flat_s[64 * i:64 * i + 64, o:o + 32]
                                    rhs = V[64 * i:64 * i + 64, d * GP + g, r, d:d + 4, :].rearrange("p k h -> p (k h)")
                                    last = pe.matmul(out[:, 48:112] if d == 0 else out[:, 0:64], lhs, rhs,
                                                     start=(m4 == 0 and d == 0 and r == 0), stop=True,
                                                     skip_group_check=True)
                    last.then_inc(pe_k, 1)
            pe.wait_ge(act_uT, 4)
            pe.wait_ge(dve_uT, 5)
            pe.wait_ge(dve_k, 1)
            for m in range(32):
                d, g0 = m // 16, 2 * (m % 16)
                if m >= 4:
                    pe.wait_ge(act_p, m - 3)
                    pe.wait_ge(dve_p, m - 3)
                for gi in range(2):
                    for r in range(2):
                        for i in range(2):
                            a = slice(64 * i, 64 * i + 64)
                            o = (2 * gi + r) * CX
                            last = pe.matmul(ps[2 * (m % 4) + i][a, o:o + CX], pt[a, d * GP + g0 + gi, r, :],
                                             uT[a, g0 + gi, :], start=True, stop=True)
                last.then_inc(pe_p, 1)
            pe.wait_ge(dve_scan, 1)
            for d in range(2):
                slot = CC if d == 0 else 0
                pe.transpose(ps[6 + d][0:2 * GP, 0:P], S[:, d, slot, :, :].rearrange("p r g -> p (r g)"), ident[:]
                             ).then_inc(pe_fin, 1)
            pe.wait_ge(ld_tmat, 16 * 32)
            for gb in range(4):
                if gb >= 2:
                    pe.wait_ge(act_gelu, 2 * (gb - 1))
                for g8 in range(8):
                    g = 8 * gb + g8
                    for i in range(2):
                        a = slice(64 * i, 64 * i + 64)
                        out = ps[2 * (gb % 2) + i][0:CX, g8 * 64:(g8 + 1) * 64]
                        pe.matmul(out, uT[a, g, :], tmat[a, g, :], start=True, stop=False)
                        for d in range(2):
                            for r in range(2):
                                last = pe.matmul(out, S[a, d, d:d + CX, r, g],
                                                 V[a, d * GP + g, r, 1 - d:5 - d, :].rearrange("p k h -> p (k h)"),
                                                 start=False, stop=(d == 1 and r == 1))
                        if g8 == 7:
                            last.then_inc(pe_y, 1)
            pe.wait_ge(act_gelu, 8)
            pe.wait_ge(act_fin, 2)
            for k in range(KT):
                if k >= 4:
                    pe.wait_ge(act_yT, k - 3)
                for i in range(L):
                    last = pe.transpose(ps[4 + k % 4][:, i * CX:(i + 1) * CX], y_c[0:CX, i, k * P:(k + 1) * P],
                                        ident[0:CX, 0:CX])
                last.then_inc(pe_yT, 1)
            pe.wait_ge(act_yT, 8)
            pe.wait_ge(dve_ada, 3)
            pe.wait_ge(ld_glu, 16 * KT)
            for m in range(6):
                t, half = m // 2, m % 2
                if m in (0, 2):
                    if m:
                        pe.wait_ge(dve_x1, 2)
                    spread(ps[6], 1, 0, m // 2)
                    spread(ps[7], 1, 1, m // 2).then_inc(pe_g1, 1)
                if m >= 2:
                    pe.wait_ge(dve_x1, m - 1)
                for part in range(2):
                    col = part * D + half * 512
                    for k in range(KT):
                        last = pe.matmul(ps[2 * (m % 2) + part][:, :], yT[:, k, t * P:(t + 1) * P],
                                         ring[:, 4 + k, col:col + 512], start=(k == 0), stop=(k == KT - 1))
                    last.then_inc(pe_glu, 1)
            pe.wait_ge(dve_x1, 6)
            for cond in range(2):
                if cond:
                    pe.wait_ge(dve_h2, 1)
                for b in range(2):
                    spread(ps[b], 2, b, cond)
                    last = spread(ps[2 + b], 1, 2 + b, cond)
                last.then_inc(pe_mod2, 1)
            for m in range(2 * NT):
                t, k0 = m // 2, 4 * (m % 2)
                pe.wait_ge(dve_h2, t + 1)
                if m >= 2:
                    pe.wait_ge(act_h2T, m - 1)
                for k in range(k0, k0 + 4):
                    last = pe.transpose(ps[4 + m % 2][:, (k % 4) * P:(k % 4 + 1) * P],
                                        h2[:, t, k * P:(k + 1) * P], ident[:])
                last.then_inc(pe_h2T, 1)
            pe.wait_ge(act_h2T, 6)
            pe.wait_ge(ld_route, 48)
            for t in range(NT):
                for k in range(KT):
                    last = pe.matmul(ps[6][:, t * NE:(t + 1) * NE], h2T[:, k, t * P:(t + 1) * P], rw[:, k, :],
                                     start=(k == 0), stop=(k == KT - 1))
                last.then_inc(pe_logit, 1)
            pe.wait_ge(dve_mask, 1)
            pe.wait_ge(pool_late, 13)
            for t in range(NT + 1):
                out = ps[7][:, t * NE:(t + 1) * NE]
                for u in range(min(t + 1, NT)):
                    last = pe.matmul(out, tri[:, 0 if u == t else 1, :], route[:, 20, u, :],
                                     start=(u == 0), stop=(u == min(t, NT - 1)))
            last.then_inc(pe_pos, 1)

            def transpose_x(nth):
                pe.wait_ge(ld_xg, nth * 16 + 16)
                for k in range(KT):
                    bank, col = (ps[5], k) if k < 5 else (ps[6], k - 5)
                    last = pe.transpose(bank[:, col * CAP:(col + 1) * CAP], xg[0:CAP, k * P:(k + 1) * P],
                                        ident[0:CAP, 0:CAP])
                last.then_inc(xt_ps, 1)

            def expert(it, last_of_round):
                pe.wait_ge(xt_ev, it * 2 + 2)
                pe.wait_ge(prod_done, it * TT + TT)
                for k in range(KT):
                    pe.wait_ge(ld_unit[k], it * 32 + 32)
                    w = ring[:, k, :].rearrange("p (a n) -> p a n", a=2)
                    for t in range(TT):
                        for j in range(4):
                            last = pe.matmul(ps[t][32 * j:32 * j + 32, :], xgT[:, k, 32 * t:32 * t + 32],
                                             w[:, :, 256 * j:256 * j + 256], start=(k == 0), stop=(k == KT - 1))
                    last.then_inc(unit_free, 1)
                if not last_of_round:
                    transpose_x(it + 1)
                for t in range(TT):
                    pe.wait_ge(prod_done, it * TT + (TT + t + 1))
                    if t == 2:
                        pe.wait_ge(y_ev, it * 12 + 12)
                    for c2 in range(2):
                        out = ps[7][:, 256 * t + P * c2:256 * t + P * c2 + P] if t < 2 else \
                            ps[4][:, 256 + P * c2:256 + P * c2 + P]
                        last = pe.transpose(out, act_a[:, t, c2 * P:(c2 + 1) * P], ident[:])
                    last.then_inc(at_ps, 1)
                pe.wait_ge(at_ev, it * 2 + 2)
                pe.wait_ge(y_ev, it * 12 + 12)
                for kk in range(KT):
                    j, c2 = kk // 2, kk % 2
                    if c2 == 0:
                        pe.wait_ge(ld_unit[KT + j], it * 32 + 32)
                    for t in range(TT):
                        for dj in range(4):
                            last = pe.matmul(ps[3 + t // 2][32 * dj:32 * dj + 32, 256 * (t % 2):256 * (t % 2) + 256],
                                             aT[:, t, c2, 32 * j:32 * j + 32],
                                             ring[:, KT + j, c2 * D + 256 * dj:c2 * D + 256 * dj + 256],
                                             start=(kk == 0 and t != 1), stop=(kk == KT - 1),
                                             skip_group_check=True)
                    if c2 == 1:
                        last.then_inc(unit_free, 1)

            pe.wait_ge(dve_cmax, 1)
            transpose_x(0)
            with pe.Fori(0, NE - 1) as e:
                expert(e, False)
            expert(NE - 1, True)
            v = pe.value_load(cmaxi[0:1, 0:1], min_val=0, max_val=T)
            with pe.If(v > CAP):
                with pe.Fori(1, ROUNDS) as r:
                    transpose_x(r * NE)
                    with pe.Fori(0, NE - 1) as e:
                        expert(r * NE + e, False)
                    expert(r * NE + NE - 1, True)
            pe.nop()
            for cond in range(2):
                for b in range(2):
                    last = spread(ps[(5, 0)[cond] + b], 2, 2 + b, cond)
            last.then_inc(pe_g2, 1)

        @block.vector
        def _(dve):
            n = [0]

            def step(ins, wait=True):
                n[0] += 1
                ins.then_inc(dve_done, 1)
                if wait:
                    dve.wait_ge(dve_done, n[0])
            tt, ts, stt, cp = dve.tensor_tensor, dve.tensor_scalar, dve.scalar_tensor_tensor, dve.tensor_copy

            dve.wait_ge(ld_lam, 16 * 5)
            cp(dtexp[0:DG, :].rearrange("p (i s) -> p i s", i=2),
               dtnat[0:DG, :].rearrange("p (i a) -> p i a", a=1).to_broadcast((DG, 2, NS))).then_inc(dve_dt, 1)
            X, N_, R_, Q_ = (tab[:, i, :] for i in (0, 1, 2, 3))
            LR, LI, DT, MAG = (tab[:, i, :] for i in (9, 10, 11, 12))
            intv = tab[:, 4, :].bitcast(I32)
            dve.wait_ge(pe_tr, 2)
            step(cp(LR, ps[7][:, 0:DG]), False)
            step(cp(LI, ps[7][:, DG:2 * DG]), False)
            step(cp(X, ps[7][:, P:P + DG]))

            def exp_of(out):
                step(ts(N_, X, LOG2E, MAGIC, ALU.mult, ALU.add))
                step(ts(N_, N_, -MAGIC, None, ALU.add))
                step(ts(N_, N_, -126.0, 127.0, ALU.max, ALU.min))
                step(stt(R_, N_, -LN2_HI, X, ALU.mult, ALU.add))
                step(stt(R_, N_, -LN2_LO, R_, ALU.mult, ALU.add))
                step(ts(R_, R_, -88.0, 1.0, ALU.max, ALU.min))
                step(ts(Q_, R_, EXP_C[0], None, ALU.mult))
                for coef in EXP_C[1:]:
                    step(stt(Q_, Q_, coef, R_, ALU.add, ALU.mult))
                step(ts(Q_, Q_, 1.0, None, ALU.add))
                step(ts(N_, N_, 127.0, 8388608.0, ALU.add, ALU.mult))
                step(cp(intv, N_))
                step(tt(out, Q_, tab[:, 4, :], ALU.mult))
            exp_of(DT)
            TH = tab[:, 13, :]
            step(tt(TH, LI, DT, ALU.mult))
            step(ts(N_, TH, INV_2PI, MAGIC, ALU.mult, ALU.add))
            step(ts(N_, N_, -MAGIC, None, ALU.add))
            step(stt(TH, N_, -TP1, TH, ALU.mult, ALU.add))
            step(stt(TH, N_, -TP2, TH, ALU.mult, ALU.add))
            step(stt(TH, N_, -TP3, TH, ALU.mult, ALU.add))
            step(ts(tab[:, 5, :], TH, -PI_SAFE, PI_SAFE, ALU.max, ALU.min))
            step(stt(R_, tab[:, 5, :], -1.0, tab[:, 5, :], ALU.mult, ALU.max))
            ts(tab[:, 6, :], R_, -1.0, math.pi / 2, ALU.mult, ALU.add).then_inc(dve_trig, 1)
            dve.wait_ge(dve_trig, 1)
            step(tt(X, LR, DT, ALU.mult))
            exp_of(MAG)
            dve.wait_ge(act_trig, 2)
            WR = tab[:, 14:18, :].rearrange("p n g -> p (n g)").rearrange("p (g k) -> p g k", k=L)
            WI = tab[:, 18:22, :].rearrange("p n g -> p (n g)").rearrange("p (g k) -> p g k", k=L)
            VR = tab[:, 22:27, :].rearrange("p n g -> p (n g)").rearrange("p (g k) -> p g k", k=NP_V)
            VI = tab[:, 27:32, :].rearrange("p n g -> p (n g)").rearrange("p (g k) -> p g k", k=NP_V)
            AR, AI = tab[:, 4, :], tab[:, 5, :]
            step(tt(AR, MAG, tab[:, 8, :], ALU.mult), False)
            step(tt(tab[:, 6, :], MAG, tab[:, 7, :], ALU.mult))
            step(cp(AI, tab[:, 6, :]))
            PR, PI_ = tab[:, 7, :], tab[:, 8, :]
            step(dve.memset(PR, 1.0), False)
            step(dve.memset(PI_, 0.0))
            for k in range(NP_V):
                for d in range(2):
                    g = slice(d * GP, (d + 1) * GP)
                    if k < L:
                        step(cp(WR[:, g, L - 1 - k if d == 0 else k], PR[:, g]), False)
                        step(cp(WI[:, g, L - 1 - k if d == 0 else k], PI_[:, g]), False)
                    step(cp(VR[:, g, k if d == 0 else L - k], PR[:, g]), False)
                    step(cp(VI[:, g, k if d == 0 else L - k], PI_[:, g]), False)
                if k < L:
                    step(tt(X, PR, AR, ALU.mult), False)
                    step(tt(N_, PI_, AI, ALU.mult), False)
                    step(tt(R_, PR, AI, ALU.mult), False)
                    step(tt(Q_, PI_, AR, ALU.mult))
                    step(tt(PR, X, N_, ALU.subtract), False)
                    step(tt(PI_, R_, Q_, ALU.add))
            step(cp(a4r[:], PR), False)
            step(cp(a4i[:, 1, :], PI_), False)
            step(ts(a4i[:, 0, :], PI_, -1.0, None, ALU.mult), False)
            NR, DEN, FR, FI = tab[:, 6, :], tab[:, 13, :], tab[:, 7, :], tab[:, 8, :]
            step(ts(NR, AR, -1.0, None, ALU.add), False)
            step(tt(X, LR, LR, ALU.mult), False)
            step(tt(N_, LI, LI, ALU.mult))
            step(tt(DEN, X, N_, ALU.add))
            step(dve.reciprocal(DEN, DEN))
            step(tt(X, NR, LR, ALU.mult), False)
            step(tt(N_, AI, LI, ALU.mult), False)
            step(tt(R_, AI, LR, ALU.mult), False)
            step(tt(Q_, NR, LI, ALU.mult))
            step(tt(X, X, N_, ALU.add), False)
            step(tt(R_, R_, Q_, ALU.subtract))
            step(tt(FR, X, DEN, ALU.mult), False)
            step(tt(FI, R_, DEN, ALU.mult))
            dve.wait_ge(act_bc, 4)
            braw = t2[:, 0:2 * DG * GS].rearrange("p (r g h) -> p r g h", r=2, h=GS)

            def over_h(a):
                return a.rearrange("p (g a) -> p g a", a=1).to_broadcast((P, DG, GS))
            step(tt(bs3[:, 1], braw[:, 0], over_h(FR), ALU.mult), False)
            step(tt(bs3[:, 0], braw[:, 1], over_h(FI), ALU.mult), False)
            step(tt(bs3[:, 2], braw[:, 1], over_h(FR), ALU.mult))
            step(tt(braw[:, 0], braw[:, 0], over_h(FI), ALU.mult))
            step(tt(bs3[:, 1], bs3[:, 1], bs3[:, 0], ALU.subtract), False)
            step(tt(bs3[:, 2], bs3[:, 2], braw[:, 0], ALU.add))
            step(ts(bs3[:, 0], bs3[:, 2], -1.0, None, ALU.mult))
            dve.wait_ge(act_sq, NT)
            ts(stat[:, 4:4 + NT], stat[:, 0:NT], 1.0 / D, EPS, ALU.mult, ALU.add).then_inc(dve_ms, 1)

            def outer(out, tmp, pr, pi, three, r, g, nk):
                def powers(a):
                    return a[:, g, :].rearrange("p g (k a) -> p g k a", a=1).to_broadcast((P, GP, nk, GS))

                def rep(a):
                    return a[:, g, :].rearrange("p g (a h) -> p g a h", a=1).to_broadcast((P, GP, nk, GS))
                step(tt(out, powers(pr), rep(three[0]), ALU.mult), False)
                step(tt(tmp, powers(pi), rep(three[1]), ALU.mult))
                return tt(out, out, tmp, ALU.add)

            tmp_w = t2[:, 0:GP * L * GS].rearrange("p (g k h) -> p g k h", k=L, h=GS)
            tmp_v = t2.rearrange("p (g k h) -> p g k h", k=NP_V, h=GS)
            for d in range(2):
                for r in range(2):
                    b = 2 * d + r
                    if b >= 2:
                        dve.wait_ge(pe_w, 4 * (b - 1))
                    outer(w_pow[:, b % 2], tmp_w, WR, WI, (bs3[:, 1 + r], bs3[:, r]), r,
                          slice(d * GP, (d + 1) * GP), L).then_inc(dve_w, 1)
                    dve.wait_ge(dve_w, b + 1)
            dve.wait_ge(act_bc, 8)

            def v_part(d, r):
                g = slice(d * GP, (d + 1) * GP)
                outer(V[:, g, r], tmp_v, VR, VI, (cs3[:, r], cs3[:, 1 + r]), r, g, NP_V).then_inc(dve_v, 1)
                dve.wait_ge(dve_v, 2 * d + r + 1)
            dve.wait_ge(act_sq, NT)
            dve.wait_ge(pe_bc, 8)
            v_part(0, 0)

            def ada_rows(b):
                dve.wait_ge(pe_ada, KT * (b + 1))
                step(tt(ada[:, b, :], ps[b][:, :], ada[:, b, :], ALU.add))
                if b == 0:
                    stt(ada[64:P, 0, :], ada[64:P, 0, :], 1.0, gains[64:P, :], ALU.add, ALU.mult).then_inc(dve_ada, 1)
                elif b == 2:
                    stt(ada[0:64, 2, :], ada[0:64, 2, :], 1.0, gains[0:64, :], ALU.add, ALU.mult).then_inc(dve_ada, 1)
                else:
                    dve.sem_inc(dve_ada, 1)
            dve.wait_ge(ld_rows, 16 * 16)
            ada_rows(0)
            dve.wait_ge(act_rt, 1)
            step(dve.reciprocal(stat[:, 4:4 + NT], stat[:, 4:4 + NT]))

            def modulate(t, src, dst, mod, done):
                dve.wait_ge(mod, 1 if t == 0 else 2)
                for b in range(2):
                    c2 = slice(512 * b, 512 * b + 512)
                    step(stt(dst[:, t, c2], src[:, t, c2], stat[:, 4 + t:5 + t], ps[b][:, :], ALU.mult, ALU.mult),
                         b == 1)
                step(tt(dst[:, t, 0:512], dst[:, t, 0:512], ps[2][:, :], ALU.add))
                tt(dst[:, t, 512:D], dst[:, t, 512:D], ps[3][:, :], ALU.add).then_inc(done, 1)
            for t in range(NT):
                modulate(t, x_sb, x_sb, pe_mod, dve_h)
            v_part(0, 1)
            dve.wait_ge(pe_hT, 6)
            v_part(1, 0)
            v_part(1, 1)
            for q in range(4):
                a = slice(32 * q, 32 * q + 32)
                step(cp(i16[a, :], ident[a, 32 * q:32 * q + 16]), q == 3)
            dve.wait_ge(ld_dtab, 16 * 8)
            step(tt(dskip, i16[:, :].rearrange("p (a b h) -> p a b h", a=1, b=1).to_broadcast((P, 2, 8, GS)),
                    dtab[:, :, :].rearrange("p a (q h) -> p a q h", h=1).to_broadcast((P, 2, 8, GS)), ALU.mult))
            for b in (1, 2):
                ada_rows(b)
            dve.wait_ge(pe_ada, 3 * KT)
            step(dve.memset(uT[:, :, CC:CC + 1], 0.0), False)
            n_ut = n[0]
            for m in range(1, 8, 2):
                dve.wait_ge(pe_uT, m + 1)
                src = ps[4 + m % 4][:, 0:4 * C].rearrange("p (g c) -> p g c", c=C)
                step(cp(uT[:, 4 * m:4 * m + 4, 0:CC], src[:, :, 0:CC]), False)
                cp(uT[:, 4 * m:4 * m + 4, CC + 1:CX], src[:, :, CC:C]).then_inc(dve_uT, 2 if m == 1 else 1)
            for m in range(4):
                i, mq = m // 2, m % 2
                dve.wait_ge(pe_k, m + 1)
                step(cp(kpad[:, i, 4 * mq:4 * mq + 4, :], ps[m][:, 0:448].rearrange("p (q w) -> p q w", w=112)))
            tt(kpad[:, :, :, 48:64], kpad[:, :, :, 48:64], dskip, ALU.add).then_inc(dve_k, 1)
            for m in range(32):
                d, g0 = m // 16, 2 * (m % 16)
                dve.wait_ge(pe_p, m + 1)
                if m == 0:
                    dve.wait_ge(ld_tmat, 16 * 32)
                cp(S[64:P, d, 1 - d:1 - d + CX, :, g0:g0 + 2].rearrange("p c r g -> p g r c"),
                   ps[2 * (m % 4) + 1][64:P, 0:4 * CX].rearrange("p (g r c) -> p g r c", g=2, r=2)
                   ).then_inc(dve_p, 1)
            dve.wait_ge(act_p, 32)
            dve.wait_ge(dve_p, 32)
            dve.wait_ge(act_h0, 1)
            hv = h0[:, :].rearrange("p (r d g) -> p r d g", r=2, d=2)
            step(dve.memset(S[:, 0, 0, :, :], 0.0), False)
            step(cp(S[:, 0, CC + 1, :, :], hv[:, :, 0, :]), False)
            step(cp(S[:, 1, CX, :, :], hv[:, :, 1, :]))
            A4R = a4r[:, :].rearrange("p (d a g) -> p d a g", d=2, a=1).to_broadcast((P, 2, 2, GP))
            A4I = a4i[:, :, :].rearrange("p r (d g) -> p d r g", d=2)
            prev = [0, 0]
            for k in range(CL - 1):
                live = [st for st in range(2) if k < (CC, CL - 1)[st]]
                f = [k, CC + 1 + k]
                b = [CC - k, CX - k]
                mark = {}
                for st in live:
                    if prev[st]:
                        dve.wait_ge(dve_done, prev[st])
                    tb = [scan_t[:, st, x, :].rearrange("p (d r g) -> p d r g", d=2, r=2) for x in range(2)]
                    step(tt(tb[0], A4R, chunk_states(0, f[st], b[st] - f[st], False), ALU.mult), False)
                    step(tt(tb[1], A4I, chunk_states(0, f[st], b[st] - f[st], True), ALU.mult), False)
                    mark[st] = n[0]
                for x in range(2):
                    for st in live:
                        tb = scan_t[:, st, x, :].rearrange("p (d r g) -> p d r g", d=2, r=2)
                        to = chunk_states(0, f[st] + 1, b[st] - 1 - f[st] - 1, False)
                        dve.wait_ge(dve_done, mark[st] - (1 - x) if x == 0 else max(prev[st], mark[st]))
                        step(tt(to, to, tb, ALU.add), False)
                        prev[st] = n[0]
            dve.wait_ge(dve_done, n[0])
            dve.sem_inc(dve_scan, 1)

            dve.wait_ge(ld_xagain, 16 * NT)
            for m in range(6):
                t, half = m // 2, m % 2
                c2 = slice(512 * half, 512 * half + 512)
                dve.wait_ge(act_sig, m + 1)
                dve.wait_ge(pe_g1, 1 if t == 0 else 2)
                step(tt(prod, sig, ps[2 * (m % 2)][:, :], ALU.mult))
                step(tt(prod, prod, ps[6 + half][:, :], ALU.mult))
                tt(x1[:, t, c2], x1[:, t, c2], prod, ALU.add).then_inc(dve_x1, 1)
            dve.wait_ge(act_sq, 2 * NT)
            ts(stat[:, 4:4 + NT], stat[:, 0:NT], 1.0 / D, EPS, ALU.mult, ALU.add).then_inc(dve_ms, 1)
            dve.wait_ge(act_rt, 2)
            step(dve.reciprocal(stat[:, 4:4 + NT], stat[:, 4:4 + NT]))
            for t in range(NT):
                modulate(t, x1, h2, pe_mod2, dve_h2)
            dve.wait_ge(act_score, 1)
            dve.wait_ge(pool_late, 13)
            dve.wait_ge(ld_route, 48)
            sc, bi = route[:, 0], route[:, 1]

            def over_e(a):
                return a.to_broadcast((P, NT, NE))
            step(tt(bi, sc, rb.rearrange("p (a e) -> p a e", a=1).to_broadcast((P, NT, NE)), ALU.add))
            b4 = bi.rearrange("p t (g m a) -> p (t g) m a", g=NGRP, a=2)
            s2 = route[:, 2].rearrange("p t (g m) -> p (t g) m", g=NGRP)[:, :, 0:2]
            m2 = route[:, 3].rearrange("p t (g m) -> p (t g) m", g=NGRP)[:, :, 0:2]
            gsc = route[:, 4, :, 0:NGRP]
            g1 = route[:, 5, :, 0:NGRP]
            g2 = route[:, 6, :, 0:NGRP]
            step(tt(s2, b4[:, :, :, 0], b4[:, :, :, 1], ALU.add), False)
            step(tt(m2, b4[:, :, :, 0], b4[:, :, :, 1], ALU.max))

            def per_group(a, i):
                return a.rearrange("p t (g m) -> p t g m", g=NGRP)[:, :, :, i]
            step(tt(g1, per_group(route[:, 2], 0), per_group(route[:, 2], 1), ALU.max), False)
            step(tt(g2, per_group(route[:, 3], 0), per_group(route[:, 3], 1), ALU.add))
            step(tt(gsc, g1, g2, ALU.max))
            gm = route[:, 7, :, 0:1]

            def first_max(val, m1, key, rk, shape, out):
                step(dve.tensor_reduce(m1, val, AX.X, ALU.max))
                step(tt(key, val, m1.to_broadcast(shape), ALU.is_equal))
                step(tt(key, key, rk, ALU.mult))
                step(dve.tensor_reduce(m1, key, AX.X, ALU.max))
                step(tt(out, key, m1.to_broadcast(shape), ALU.is_equal))
            first_max(gsc, gm, g1, grank, (P, NT, NGRP), g2)
            mb = route[:, 8]
            mk = route[:, 9]
            step(cp(mk.rearrange("p t (g m) -> p t g m", g=NGRP),
                    g2.rearrange("p t (g a) -> p t g a", a=1).to_broadcast((P, NT, NGRP, EPG))))
            step(tt(mb, bi, mk, ALU.mult), False)
            step(ts(mk, mk, 1e30, -1e30, ALU.mult, ALU.add))
            step(tt(mb, mb, mk, ALU.add))
            oh = [route[:, 10], route[:, 11]]
            first_max(mb, route[:, 12, :, 0:1], route[:, 13], rank, (P, NT, NE), oh[0])
            step(stt(mb, oh[0], -2e30, mb, ALU.mult, ALU.add))
            first_max(mb, route[:, 14, :, 0:1], route[:, 15], rank, (P, NT, NE), oh[1])
            tt(route[:, 20], oh[0], oh[1], ALU.add).then_inc(dve_mask, 1)
            for k in range(2):
                step(tt(route[:, 16 + k], sc, oh[k], ALU.mult))
                step(dve.tensor_reduce(cmb[:, k, :], route[:, 16 + k], AX.X, ALU.add))
            wsum = route[:, 18, 0, 0:NT]
            step(tt(wsum, cmb[:, 0, :], cmb[:, 1, :], ALU.add))
            step(dve.reciprocal(wsum, wsum))
            for k in range(2):
                step(tt(cmb[:, k, :], cmb[:, k, :], wsum, ALU.mult))
            dve.wait_ge(pe_pos, 1)
            step(dve.tensor_reduce(cmax[:], ps[7][:, NT * NE:(NT + 1) * NE], AX.X, ALU.max))
            cp(cmaxi[:], cmax[:]).then_inc(dve_cmax, 1)
            step(tt(route[:, 21], ps[7][:, 0:NT * NE].rearrange("p (t e) -> p t e", t=NT), e384, ALU.add))
            for k in range(2):
                step(tt(route[:, 22 + k], route[:, 21], oh[k], ALU.mult))
                step(dve.tensor_reduce(route[:, 19, k, 0:NT], route[:, 22 + k], AX.X, ALU.add))
                ins = cp(sloti[:, k, :], route[:, 19, k, 0:NT])
                if k == 0:
                    step(ins)
            ins.then_inc(dve_slot, 1)

            def evict_x(nth):
                dve.wait_ge(xt_ps, nth + 1)
                cp(xgT[:, 0:5, :], ps[5][:, 0:5 * CAP].rearrange("p (k n) -> p k n", k=5)).then_inc(xt_ev, 1)
                cp(xgT[:, 5:8, :], ps[6][:, 0:3 * CAP].rearrange("p (k n) -> p k n", k=3)).then_inc(xt_ev, 1)

            def expert(it, last_of_round):
                for t in range(TT):
                    dve.wait_ge(silu_done, it * TT + (t + 1))
                    tt(act_a[:, t, :], sg[:, t, :], ps[t][:, 256:512], ALU.mult).then_inc(prod_done, 1)
                if not last_of_round:
                    evict_x(it + 1)
                dve.wait_ge(unit_free, it * NU + NU)
                dve.wait_ge(y_free, it + 1)
                for t in range(TT):
                    for j in range(2, 4):
                        src = ps[3 + t // 2][32 * j:32 * j + 32, 256 * (t % 2):256 * (t % 2) + 256]
                        cp(yrow[32 * t:32 * t + 32, 256 * j:256 * j + 256], src).then_inc(y_ev, 1)
            dve.sem_inc(prod_done, TT)
            dve.sem_inc(y_ev, 12)
            evict_x(0)
            with dve.Fori(0, NE - 1) as e:
                expert(e, False)
            expert(NE - 1, True)
            v = dve.value_load(cmaxi[0:1, 0:1], min_val=0, max_val=T)
            with dve.If(v > CAP):
                with dve.Fori(1, ROUNDS) as r:
                    evict_x(r * NE)
                    with dve.Fori(0, NE - 1) as e:
                        expert(r * NE + e, False)
                    expert(r * NE + NE - 1, True)
            dve.nop()
            dve.wait_ge(ld_y2, 32)
            dve.wait_ge(pe_g2, 1)
            for t in range(NT):
                g = 5 if t == 0 else 0
                step(ts(m_out[:, t, :], y2c[:, 0, t, :], cmb[:, 0, t:t + 1], None, ALU.mult))
                step(stt(m_out[:, t, :], y2c[:, 1, t, :], cmb[:, 1, t:t + 1], m_out[:, t, :], ALU.mult, ALU.add))
                for b in range(2):
                    c2 = slice(512 * b, 512 * b + 512)
                    step(tt(m_out[:, t, c2], m_out[:, t, c2], ps[g + b][:, :], ALU.mult), b == 1)
                tt(x1[:, t, :], x1[:, t, :], m_out[:, t, :], ALU.add).then_inc(dve_x2, 1)
                dve.wait_ge(act_sq, 2 * NT + t + 1)
                ts(stat[:, 4 + t:5 + t], stat[:, t:t + 1], 1.0 / D, EPS, ALU.mult, ALU.add).then_inc(dve_ms, 1)
                dve.wait_ge(act_rt, 3 + t)
                step(dve.reciprocal(stat[:, 4 + t:5 + t], stat[:, 4 + t:5 + t]))
                stt(yo[:, t, :], x1[:, t, :], stat[:, 4 + t:5 + t], gfin, ALU.mult, ALU.mult).then_inc(dve_out, 1)


_INS = ["x_prompt", "x_sample", "c", "state_ssm_re", "state_ssm_im", "c_ctx", "norm_mix", "norm_ffn",
        "w_ada", "b_ada", "ssm_w_in", "ssm_lam_re", "ssm_lam_im", "ssm_log_dt", "ssm_b_re", "ssm_b_im",
        "ssm_c_re", "ssm_c_im", "ssm_d", "ssm_w_glu", "router_w", "router_b", "moe_w_gate", "moe_w_up",
        "moe_w_down", "norm_final"]
_OUTS = [("y_prompt", (1, T_CTX, D)), ("y_sample", (1, T_LAT, D)),
         ("new_re", (1, 1, 2, G, NS)), ("new_im", (1, 1, 2, G, NS))]


def kernel(**inputs):
    import numpy as np
    import concourse.bacc as bacc
    from concourse.bass_utils import run_bass_kernel_spmd

    nc = bacc.Bacc("TRN2", target_bir_lowering=False, num_devices=1)
    arrays, args = {}, []
    for name in _INS:
        a = np.ascontiguousarray(inputs[name])
        arrays[f"in_{name}"] = a
        args.append(nc.dram_tensor(f"in_{name}", a.shape, mybir.dt.from_np(a.dtype), kind="ExternalInput").ap())
    for name, shape in _OUTS:
        args.append(nc.dram_tensor(f"out_{name}", shape, F32, kind="ExternalOutput").ap())
    build(nc, *args)
    r = run_bass_kernel_spmd(nc, [arrays], core_ids=[0])
    return tuple(r.results[0][f"out_{name}"] for name, _ in _OUTS)
```

```python
from contextlib import ExitStack
import math

import concourse.bass as bass
from concourse import mybir

F32 = mybir.dt.float32
I32 = mybir.dt.int32
U32 = mybir.dt.uint32
ALU = mybir.AluOpType
ACT = mybir.ActivationFunctionType
AX = mybir.AxisListType

P = 128
D = 1024
KT = D // P
T_CTX, T_LAT = 128, 256
T = T_CTX + T_LAT
NT = T // P
G, GS, NS = 64, 16, 64
GP = G // 2
DG = 2 * GP
L = 4
CC, CL = T_CTX // L, T_LAT // L
C = CC + CL
CX = C + 1
SLOTS = CX + 1
NP_V = L + 1
NE, NGRP, EPG = 16, 4, 4
FE = 1024
CAP = 96
TT = CAP // 32
ROUNDS = T // CAP
EPS = 1e-6
ADA_BANK = (0, 6, 7)
OOB = 1 << 20
UNIT = 2048
NU = 12
MAGIC = 12582912.0
LOG2E = 1.4426950408889634
LN2_HI, LN2_LO = 0.693359375, -2.12194440e-4
INV_2PI = 1.0 / (2.0 * math.pi)
TP1 = 6.28125
TP2 = 0.0019350051879882812
TP3 = 2.0 * math.pi - TP1 - TP2
PI_SAFE = 3.1415925
EXP_C = [1.0 / 5040, 1.0 / 720, 1.0 / 120, 1.0 / 24, 1.0 / 6, 0.5, 1.0]


def build(nc, x_prompt, x_sample, c, state_re, state_im, c_ctx, norm_mix, norm_ffn, w_ada, b_ada,
          w_in, lam_re, lam_im, log_dt, b_re, b_im, c_re, c_im, ssm_d, w_glu, router_w, router_b,
          w_gate, w_up, w_down, norm_final, y_prompt, y_sample, new_re, new_im):
    h2_d = nc.dram_tensor("h2_scratch", [T, D], F32, kind="Internal").ap()
    y2_d = nc.dram_tensor("y2_scratch", [2 * T, D], F32, kind="Internal").ap()
    list_d = nc.dram_tensor("slot_list", [NE * T, 2], I32, kind="Internal").ap()

    ctx = ExitStack()
    with ctx:
        def sb(name, shape, dt=F32):
            return ctx.enter_context(nc.sbuf_tensor(name, shape, dt))

        def sem(name):
            return ctx.enter_context(nc.semaphore(name))

        ring = sb("ring", [P, NU, UNIT])
        sreg = sb("sreg", [P, 2 * SLOTS * DG])
        vreg = sb("vreg", [P, 2 * DG * NP_V * GS])
        tmat = sb("tmat", [P, GP, L * GS])
        ada = sb("ada", [P, 3, 512])
        gains = sb("gains", [P, 512])
        ident = sb("ident", [P, P])
        bsel = sb("bsel", [P, 2, P])
        a4r = sb("a4r", [P, DG])
        a4i = sb("a4i", [P, 2, DG])
        h0 = sb("h0", [P, P])
        silu_c = sb("silu_c", [P, KT, 32])
        stat = sb("stat", [P, 16])
        scan_t = sb("scan_t", [P, 2, 2, P])
        cmb = sb("cmb", [P, 2, NT])
        dtab = sb("dtab", [P, 2, 8])
        i16 = sb("i16", [P, GS])
        sloti = sb("sloti", [P, 2, NT], U32)
        cmax = sb("cmax", [P, 1])
        cmaxi = sb("cmaxi", [P, 1], I32)
        gidx = sb("gidx", [P, 2], U32)
        sidx = sb("sidx", [P, 2], U32)
        pool_tick = sb("pool_tick", [1, 3])

        tab = tmat[:, :, :].rearrange("p g n -> p (g n)").rearrange("p (n g) -> p n g", g=DG)
        dskip = scan_t[:, :, :, :].rearrange("p a b n -> p (a b n)")[:, 0:256].rearrange(
            "p (a q h) -> p a q h", a=2, q=8)
        fins = scan_t[:, :, :, :].rearrange("p a b n -> p (a b n)")[0:2 * GP, 0:2 * P].rearrange(
            "p (d n) -> p d n", d=2)

        ada_w = ring[:, 0:2, :]
        u_c = ring[:, 0:2, :].rearrange("p a b -> p (a b)").rearrange("p (g i h) -> p g i h", i=L, h=GS)
        y_b = ring[:, 0:2, :].rearrange("p a b -> p (a b)")[:, 0:KT * 4 * CX].rearrange(
            "p (n b c) -> p n b c", n=KT, b=4)
        pick = ring[:, 1, UNIT - L * 80:UNIT].rearrange("p (t n) -> p t n", t=L)
        w_pow = ring[:, 2:4, :].rearrange("p a (g k h) -> p a g k h", k=L, h=GS)
        uT = ring[:, 2:4, :].rearrange("p a b -> p (a b)")[:, 0:GP * CX].rearrange("p (g c) -> p g c", c=CX)
        yT = ring[:, 2:4, :].rearrange("p a b -> p (a b)")[:, 0:KT * T].rearrange("p (k t) -> p k t", k=KT)
        kpad = ring[:, 7, 0:16 * 112].rearrange("p (a q w) -> p a q w", a=2, q=8)
        win = ring[:, 4:8, :].rearrange("p a b -> p (a b)").rearrange("p (k n) -> p k n", k=KT)
        pt = ring[:, 8:12, :].rearrange("p a b -> p (a b)").rearrange("p (g r s) -> p g r s", r=2, s=NS)

        S = sreg[:, :].rearrange("p (d c r g) -> p d c r g", d=2, c=SLOTS, r=2)
        off = [0]

        def cut(region, n):
            a = region[:, off[0]:off[0] + n]
            off[0] += n
            return a
        bs3 = cut(sreg, 3 * DG * GS).rearrange("p (r g h) -> p r g h", r=3, g=DG)
        cs3 = cut(sreg, 3 * DG * GS).rearrange("p (r g h) -> p r g h", r=3, g=DG)
        t2 = cut(sreg, GP * NP_V * GS)
        hT = cut(sreg, KT * T).rearrange("p (k t) -> p k t", k=KT)
        off[0] = 0
        bnat = cut(vreg, UNIT)
        cnat = cut(vreg, UNIT)
        lnat = cut(vreg, P)
        hnat = cut(vreg, P)
        dtnat = cut(vreg, 2)
        dtexp = cut(vreg, P)
        rows = cut(vreg, P)
        scr = cut(vreg, D)
        off[0] = 2 * DG * NP_V * GS - NT * D
        x_sb = cut(vreg, NT * D).rearrange("p (t n) -> p t n", t=NT)
        V = vreg[:, :].rearrange("p (g r k h) -> p g r k h", r=2, k=NP_V, h=GS)

        off[0] = 0
        mod2 = cut(sreg, 8 * 512).rearrange("p (a r n) -> p a r n", a=2, r=4)
        x1 = cut(sreg, NT * D).rearrange("p (t n) -> p t n", t=NT)
        h2 = cut(sreg, NT * D).rearrange("p (t n) -> p t n", t=NT)
        rw = cut(sreg, KT * NE).rearrange("p (k e) -> p k e", k=KT)
        rb = cut(sreg, NE)
        route = cut(sreg, 24 * NT * NE).rearrange("p (a t e) -> p a t e", a=24, t=NT)
        e384 = cut(sreg, NT * NE).rearrange("p (t e) -> p t e", t=NT)
        rank = cut(sreg, NT * NE).rearrange("p (t e) -> p t e", t=NT)
        grank = cut(sreg, NT * NGRP).rearrange("p (t e) -> p t e", t=NT)
        tokv = cut(sreg, 4 * NT).bitcast(I32).rearrange("p (k t v) -> p k t v", k=2, t=NT)
        listi = cut(sreg, NE * T * 2 // P).bitcast(I32)
        iotas = cut(sreg, NT * NE).bitcast(I32).rearrange("p (t e) -> p t e", t=NT)
        tri = cut(sreg, 2 * P).rearrange("p (a n) -> p a n", a=2)
        assert off[0] <= 2 * SLOTS * DG
        off[0] = 0
        xg = cut(vreg, D)
        xgT = cut(vreg, KT * CAP).rearrange("p (k t) -> p k t", k=KT)
        sg = cut(vreg, TT * 256).rearrange("p (t n) -> p t n", t=TT)
        act_a = cut(vreg, TT * 256).rearrange("p (t n) -> p t n", t=TT)
        aT = cut(vreg, TT * 2 * P).rearrange("p (t c n) -> p t c n", t=TT, c=2)
        yrow = cut(vreg, D)
        h2T = cut(vreg, KT * T).rearrange("p (k t) -> p k t", k=KT)
        sig = cut(vreg, 512)
        prod = cut(vreg, 512)
        gfin = cut(vreg, D)
        assert off[0] <= 2 * DG * NP_V * GS
        yo = ring[:, 8:10, :].rearrange("p a b -> p (a b)")[:, 0:NT * D].rearrange("p (t n) -> p t n", t=NT)
        y2c = ring[:, 4:7, :].rearrange("p a b -> p (a b)").rearrange("p (k t n) -> p k t n", k=2, t=NT)
        m_out = h2

        ps = [ctx.enter_context(nc.psum_tensor(f"ps{i}", [P, 512], F32)) for i in range(8)]

        ld_cond, ld_x, ld_lam, ld_bc, ld_rows, ld_dtab = (sem(n) for n in (
            "ld_cond", "ld_x", "ld_lam", "ld_bc", "ld_rows", "ld_dtab"))
        ld_ada = [sem(f"ld_ada{i}") for i in range(2)]
        ld_late = [sem(f"ld_late{i}") for i in range(4)]
        ld_win, ld_tmat, ld_glu, ld_xagain, ld_route, ld_y2 = (sem(n) for n in (
            "ld_win", "ld_tmat", "ld_glu", "ld_xagain", "ld_route", "ld_y2"))
        ld_unit = [sem(f"ld_unit{u}") for u in range(NU)]
        pool_zero, pool_const, pool_late, pool_pick = (sem(n) for n in (
            "pool_zero", "pool_const", "pool_late", "pool_pick"))
        pe_tr, pe_ada, pe_bc, pe_w, pe_mod, pe_hT, pe_u, pe_uT, pe_k, pe_p, pe_y, pe_fin, pe_yT = (
            sem(n) for n in ("pe_tr", "pe_ada", "pe_bc", "pe_w", "pe_mod", "pe_hT", "pe_u", "pe_uT",
                             "pe_k", "pe_p", "pe_y", "pe_fin", "pe_yT"))
        pe_glu, pe_g1, pe_h2T, pe_logit, pe_pos, pe_g2 = (sem(n) for n in (
            "pe_glu", "pe_g1", "pe_h2T", "pe_logit", "pe_pos", "pe_g2"))
        act_silu, act_sq, act_rt, act_trig, act_bc, act_pt, act_hT, act_u, act_uT, act_p, act_gelu = (
            sem(n) for n in ("act_silu", "act_sq", "act_rt", "act_trig", "act_bc", "act_pt", "act_hT",
                             "act_u", "act_uT", "act_p", "act_gelu"))
        act_yT, act_sig, act_h2T, act_score, act_fin, act_h0 = (sem(n) for n in (
            "act_yT", "act_sig", "act_h2T", "act_score", "act_fin", "act_h0"))
        dve_done, pe_rows2, dve_rows2 = (sem(n) for n in ("dve_done", "pe_rows2", "dve_rows2"))
        dve_dt, dve_trig, dve_bbar, dve_cs, dve_w, dve_v, dve_ms, dve_ada, dve_h, dve_k, dve_uT, dve_p = (
            sem(n) for n in ("dve_dt", "dve_trig", "dve_bbar", "dve_cs", "dve_w", "dve_v", "dve_ms",
                             "dve_ada", "dve_h", "dve_k", "dve_uT", "dve_p"))
        dve_h0, dve_scan, dve_x1, dve_h2, dve_mask, dve_slot, dve_cmax, dve_x2, dve_out = (sem(n) for n in (
            "dve_h0", "dve_scan", "dve_x1", "dve_h2", "dve_mask", "dve_slot", "dve_cmax", "dve_x2", "dve_out"))
        st_list, st_h2, st_out, st_scatter = (sem(n) for n in ("st_list", "st_h2", "st_out", "st_scatter"))
        unit_free, ld_idx, ld_xg, xt_ps, xt_ev, silu_done, prod_done, at_ps, at_ev, y_ev, ld_sidx, y_sent = (
            sem(n) for n in ("unit_free", "ld_idx", "ld_xg", "xt_ps", "xt_ev", "silu_done", "prod_done",
                             "at_ps", "at_ev", "y_ev", "ld_sidx", "y_sent"))

        y_free = sem("y_free")
        ticks = [sem("gather_tick"), sem("send_tick"), y_free]

        flat_s = sreg[:, :]
        FS = 2 * SLOTS * DG

        def chunk_states(d0, slot0, dslot, swap):
            first = slot0 * DG + (GP if swap else 0)
            return bass.AP(flat_s.tensor, flat_s.offset + first,
                           [[FS, P], [(SLOTS + dslot) * DG, 2], [-GP if swap else GP, 2], [1, GP]])

        def lam_rows(a):
            return a.rearrange("a d (g i) s -> (a d g) (i s)", i=2)

        block = ctx.enter_context(nc.Block())

        @block.sync
        def _(sp):
            def ada_piece(n):
                b, k = divmod(n, KT)
                if n >= 2:
                    sp.wait_ge(pe_ada, n - 1)
                sp.dma_start(ada_w[:, n % 2, :],
                             w_ada[0, k * P:(k + 1) * P, b * UNIT:(b + 1) * UNIT]).then_inc(ld_ada[n % 2], 16)
            for t in range(NT):
                src = x_prompt[0] if t == 0 else x_sample[0, (t - 1) * P:t * P, :]
                sp.dma_start(x_sb[:, t, :], src).then_inc(ld_x, 16)
            for n in range(KT):
                ada_piece(n)
            for k in range(KT):
                sp.dma_start(win[:, k, :], w_in[0, k * P:(k + 1) * P, :]).then_inc(ld_win, 16)
            sp.wait_ge(pe_u, 8)
            for k in range(3):
                sp.dma_start(ring[:, 4 + k, :], w_glu[0, k * P:(k + 1) * P, :]).then_inc(ld_glu, 16)
            sp.wait_ge(dve_k, 1)
            for i in range(2):
                for j in range(L):
                    for q in range(4):
                        dst = tmat[64 * i + 16 * j:64 * i + 16 * j + 16, q:GP:4, :]
                        sp.dma_start(dst, kpad[32 * q:32 * q + 16, i, :, (3 - j) * GS:(7 - j) * GS]
                                     ).then_inc(ld_tmat, 16)
            sp.wait_ge(pe_p, 32)
            for n in range(KT, 3 * KT):
                b, k = divmod(n, KT)
                if n >= KT + 4:
                    sp.wait_ge(pe_ada, n - 3)
                sp.dma_start(ring[:, 8 + n % 4, :],
                             w_ada[0, k * P:(k + 1) * P, b * UNIT:(b + 1) * UNIT]).then_inc(ld_late[n % 4], 16)
            sp.wait_ge(ld_tmat, 16 * 32)
            for k in range(3, KT):
                if k >= 4:
                    sp.wait_ge(pe_ada, 3 * KT - KT + k + 1)
                sp.dma_start(ring[:, 4 + k, :], w_glu[0, k * P:(k + 1) * P, :]).then_inc(ld_glu, 16)
            sp.wait_ge(pe_y, 4)
            sp.wait_ge(pe_fin, 2)
            for t in range(NT):
                src = x_prompt[0] if t == 0 else x_sample[0, (t - 1) * P:t * P, :]
                sp.dma_start(x1[:, t, :], src).then_inc(ld_xagain, 16)
            sp.dma_start(rw, router_w.rearrange("(k p) e -> p k e", p=P)).then_inc(ld_route, 16)
            sp.dma_start(rb, router_b.rearrange("(a e) -> a e", a=1).broadcast_to((P, NE))).then_inc(ld_route, 16)
            sp.dma_start(gfin, norm_final.rearrange("(a e) -> a e", a=1).broadcast_to((P, D))).then_inc(ld_route, 16)
            for r, dst in ((0, new_re), (1, new_im)):
                for d in range(2):
                    if r == 0:
                        sp.wait_ge(act_fin, d + 1)
                    sp.dma_start(dst[0, 0, d].rearrange("(g i) s -> g (i s)", i=2),
                                 fins[r * GP:(r + 1) * GP, d, :]).then_inc(st_out, 16)

            def load_unit(u, e):
                if u < KT:
                    for h, w in enumerate((w_gate, w_up)):
                        sp.dma_start(ring[:, u, h * D:(h + 1) * D],
                                     w[0, bass.ds(e, 1), u * P:(u + 1) * P, :].rearrange("a p n -> (a p) n")
                                     ).then_inc(ld_unit[u], 16)
                else:
                    for h in range(2):
                        k = 2 * (u - KT) + h
                        sp.dma_start(ring[:, u, h * D:(h + 1) * D],
                                     w_down[0, bass.ds(e, 1), k * P:(k + 1) * P, :].rearrange("a p n -> (a p) n")
                                     ).then_inc(ld_unit[u], 16)

            sp.wait_ge(pe_yT, 8)
            for u in range(2):
                load_unit(u, 0)
            sp.wait_ge(pe_glu, 12)
            for u in range(2, NU):
                load_unit(u, 0)
            with sp.Fori(1, NE) as e:
                for u in range(NU):
                    sp.wait_ge(unit_free, e * NU + (u + 1 - NU))
                    load_unit(u, e)
            sp.wait_ge(y_sent, 16 * NE)
            v = sp.value_load(cmaxi[0:1, 0:1], min_val=0, max_val=T)
            with sp.If(v > CAP):
                with sp.Fori(1, ROUNDS) as r:
                    with sp.Fori(0, NE) as e:
                        for u in range(NU):
                            sp.wait_ge(unit_free, r * (NE * NU) + e * NU + (u + 1 - NU))
                            load_unit(u, e)
                sp.wait_ge(y_sent, 16 * NE * ROUNDS)
            sp.nop()
            for k in range(2):
                sp.dma_start(y2c[:, k, :, :], y2_d[k * T:(k + 1) * T, :].rearrange("(t p) n -> p t n", p=P)
                             ).then_inc(ld_y2, 16)
            for t in range(NT):
                sp.wait_ge(dve_out, t + 1)
                dst = y_prompt[0] if t == 0 else y_sample[0, (t - 1) * P:t * P, :]
                sp.dma_start(dst, yo[:, t, :]).then_inc(st_out, 16)
            sp.wait_ge(st_out, 16 * (4 + NT))
            sp.wait_ge(st_h2, 16 * NT)
            sp.wait_ge(st_list, 16)
            sp.wait_ge(st_scatter, 16 * 2 * NT)

        @block.gpsimd
        def _(pool):
            n = [0]

            def after(ins):
                n[0] += 1
                ins.then_inc(pool_const, 1)
                pool.wait_ge(pool_const, n[0])
            pool.memset(ada[:], 0.0).then_inc(pool_zero, 1)
            pool.memset(gains[:], 0.0).then_inc(pool_zero, 1)
            pool.memset(dtab[:], 0.0).then_inc(pool_zero, 1)
            pool.memset(silu_c[:], 0.0).then_inc(pool_zero, 1)
            after(pool.memset(ident[:], 0.0))
            after(pool.affine_select(out=ident[:], in_=ident[:], compare_op=ALU.not_equal, fill=1.0, base=0,
                                     pattern=[[-1, P]], channel_multiplier=1))
            after(pool.memset(bsel[:], 0.0))
            for cond in range(2):
                for j in range(4):
                    after(pool.affine_select(out=bsel[:, cond, :], in_=bsel[:, cond, :], compare_op=ALU.not_equal,
                                             fill=1.0, base=-(32 * j + cond), pattern=[[0, P]],
                                             channel_multiplier=1))
            assert n[0] == 11
            pool.wait_ge(pe_uT, 8)
            after(pool.memset(pick, 0.0))
            for c2 in range(2):
                pool.tensor_copy(pick[:, :, 16 + 32 * c2:32 + 32 * c2],
                                 ident[:, 64 * c2:64 * c2 + 64].rearrange("p (t h) -> p t h", h=GS)
                                 ).then_inc(pool_pick, 1)
            pool.wait_ge(pe_y, 4)
            pool.wait_ge(pe_fin, 2)
            n[0] = 0

            def late(ins):
                n[0] += 1
                ins.then_inc(pool_late, 1)
                pool.wait_ge(pool_late, n[0])
            late(pool.memset(tri, 1.0))
            late(pool.affine_select(out=tri[:, 0, :], in_=tri[:, 0, :], compare_op=ALU.is_gt, fill=0.0, base=0,
                                    pattern=[[1, P]], channel_multiplier=-1))
            late(pool.iota(iotas, pattern=[[0, NT], [T, NE]], base=0, channel_multiplier=0))
            late(pool.tensor_copy(e384, iotas))
            late(pool.iota(iotas, pattern=[[0, NT], [-1, NE]], base=NE, channel_multiplier=0))
            late(pool.tensor_copy(rank, iotas))
            late(pool.iota(iotas[:, :, 0:NGRP], pattern=[[0, NT], [-1, NGRP]], base=NGRP, channel_multiplier=0))
            late(pool.tensor_copy(grank, iotas[:, :, 0:NGRP]))
            for k in range(2):
                late(pool.iota(tokv[:, k, :, 0], pattern=[[P, NT]], base=0, channel_multiplier=1))
                late(pool.iota(tokv[:, k, :, 1], pattern=[[P, NT]], base=k * T, channel_multiplier=1))
            late(pool.memset(listi, OOB))
            assert n[0] == 13
            pool.dma_start(list_d.rearrange("(p a) v -> p (a v)", p=P), listi).then_inc(st_list, 16)
            pool.wait_ge(dve_scan, 1)
            pool.wait_ge(pe_y, 4)
            pool.memset(xg, 0.0).then_inc(pool_late, 1)
            pool.wait_ge(pool_late, 14)
            pool.wait_ge(st_list, 16)
            pool.wait_ge(dve_slot, 1)
            for k in range(2):
                for t in range(NT):
                    pool.indirect_dma_start(out=list_d, out_offset=bass.IndirectOffsetOnAxis(
                        ap=sloti[:, k, t:t + 1], axis=0), in_=tokv[:, k, t, :], in_offset=None,
                        bounds_check=NE * T - 1, oob_is_err=False).then_inc(st_scatter, 16)
            pool.wait_ge(st_scatter, 16 * 2 * NT)
            pool.wait_ge(st_h2, 16 * NT)
            pool.wait_ge(dve_cmax, 1)
            last_token = pool.to_reg(T - 1)
            last_row = pool.to_reg(2 * T - 1)

            def carry_waits(which, before):
                pool.wait_ge(ticks[which], before + 1)
                pool.tensor_tensor(pool_tick[:, which:which + 1], ident[0:1, 0:1], ident[0:1, 0:1], ALU.mult
                                   ).then_inc(ticks[which], 1)

            def gather(base, nth, used):
                if used is not None:
                    pool.wait_ge(ld_xg, nth * 16)
                pool.dma_start(gidx[0:CAP, :], list_d[bass.ds(base, CAP), :].bitcast(U32)).then_inc(ld_idx, 16)
                pool.wait_ge(ld_idx, nth * 16 + 16)
                if used is not None:
                    pool.wait_ge(xt_ps, used)
                carry_waits(0, nth)
                pool.indirect_dma_start(out=xg[0:CAP, :], out_offset=None, in_=h2_d,
                                        in_offset=bass.IndirectOffsetOnAxis(ap=gidx[0:CAP, 0:1], axis=0),
                                        bounds_check=last_token, oob_is_err=False).then_inc(ld_xg, 16)

            def send(base, it):
                pool.dma_start(sidx[0:CAP, :], list_d[bass.ds(base, CAP), :].bitcast(U32)).then_inc(ld_sidx, 16)
                pool.wait_ge(ld_sidx, it * 16 + 16)
                pool.wait_ge(y_ev, it * 12 + 24)
                carry_waits(1, it)
                pool.indirect_dma_start(out=y2_d, out_offset=bass.IndirectOffsetOnAxis(
                    ap=sidx[0:CAP, 1:2], axis=0), in_=yrow[0:CAP, :], in_offset=None,
                    bounds_check=last_row, oob_is_err=False).then_inc(y_sent, 16)
                pool.wait_ge(y_sent, it * 16 + 16)
                carry_waits(2, it)

            for which in range(3):
                pool.sem_inc(ticks[which], 1)
            gather(0, 0, None)
            with pool.Fori(0, NE - 1) as e:
                gather(e * T + T, e + 1, e + 1)
                send(e * T, e)
            send((NE - 1) * T, NE - 1)
            v = pool.value_load(cmaxi[0:1, 0:1], min_val=0, max_val=T)
            with pool.If(v > CAP):
                with pool.Fori(1, ROUNDS) as r:
                    gather(r * CAP, r * NE, r * NE)
                    with pool.Fori(0, NE - 1) as e:
                        gather(e * T + T + r * CAP, r * NE + e + 1, r * NE + e + 1)
                        send(e * T + r * CAP, r * NE + e)
                    send((NE - 1) * T + r * CAP, r * NE + NE - 1)
            pool.nop()

        @block.scalar
        def _(act):
            act.dma_start(rows[0:8, :], c_ctx.rearrange("(k p) -> k p", p=P)).then_inc(ld_cond, 16)
            act.dma_start(rows[8:16, :], c[0].rearrange("(k p) -> k p", p=P)).then_inc(ld_cond, 16)
            act.dma_start(lnat[0:DG, :], lam_rows(lam_re)).then_inc(ld_lam, 16)
            act.dma_start(lnat[DG:P, :], lam_rows(lam_im)).then_inc(ld_lam, 16)
            act.dma_start(dtnat[0:DG, :], log_dt.rearrange("a d (g i) -> (a d g) i", i=2)).then_inc(ld_lam, 16)
            act.dma_start(hnat[0:DG, :], state_re[0].rearrange("a d (g i) s -> (a d g) (i s)", i=2)).then_inc(ld_lam, 16)
            act.dma_start(hnat[DG:P, :], state_im[0].rearrange("a d (g i) s -> (a d g) (i s)", i=2)).then_inc(ld_lam, 16)
            for r, (b, cc) in enumerate(((b_re, c_re), (b_im, c_im))):
                act.dma_start(bnat[r * DG:(r + 1) * DG, :], b.rearrange("a d (g i) s h -> (a d g) (i s h)", i=2)
                              ).then_inc(ld_bc, 16)
                for i in range(2):
                    act.dma_start(cnat[r * DG:(r + 1) * DG, :].rearrange("p (h i s) -> p i h s", h=GS, i=2)[:, i],
                                  cc.rearrange("a d (g i) h s -> i (a d g) h s", i=2)[i]).then_inc(ld_bc, 16)
            act.wait_ge(pool_zero, 4)
            rows_b = b_ada.rearrange("o (b j n) -> o b j n", b=3, n=512)
            for j in range(4):
                for cond in range(2):
                    r = 32 * j + cond
                    act.dma_start(ada[r:r + 1, :, :], rows_b[:, :, j, :]).then_inc(ld_rows, 16)
                    gain = (norm_ffn if j < 2 else norm_mix)[0:1, (j % 2) * 512:(j % 2 + 1) * 512]
                    act.dma_start(gains[r:r + 1, :], gain).then_inc(ld_rows, 16)
            for q in range(4):
                for i in range(2):
                    act.dma_start(dtab[32 * q:32 * q + 16, i, :], ssm_d[0].rearrange(
                        "(m q i h) -> q i h m", m=8, q=4, i=2)[q, i], allow_slow_non_contiguous=True
                        ).then_inc(ld_dtab, 16)

            act.wait_ge(pe_tr, 1)
            act.activation(silu_c[:, :, 0:2].rearrange("p k c -> p c k"),
                           ps[3][:, 0:16].rearrange("p (c k) -> p c k", c=2), ACT.Silu).then_inc(act_silu, 1)
            act.wait_ge(pe_tr, 2)
            act.activation(h0[:], ps[4][:, 0:P], ACT.Copy).then_inc(act_h0, 1)
            braw = t2[:, 0:2 * DG * GS].rearrange("p (r g h) -> p r g h", r=2, h=GS)
            for m in range(4):
                act.wait_ge(pe_bc, m + 1)
                act.activation(braw[:, :, :, 4 * m:4 * m + 4],
                               ps[5 + m % 2][:, :].rearrange("p (h r g) -> p r g h", h=4, r=2), ACT.Copy
                               ).then_inc(act_bc, 1)
            act.wait_ge(dve_trig, 1)
            act.activation(tab[:, 7, :], tab[:, 5, :], ACT.Sin).then_inc(act_trig, 1)
            act.activation(tab[:, 8, :], tab[:, 6, :], ACT.Sin).then_inc(act_trig, 1)
            for m in range(4):
                act.wait_ge(pe_bc, 5 + m)
                src = ps[5 + m % 2][:, :].rearrange("p (h r g) -> p r g h", h=4, r=2)
                act.activation(cs3[:, 0, :, 4 * m:4 * m + 4], src[:, 0], ACT.Copy)
                act.activation(cs3[:, 1, :, 4 * m:4 * m + 4], src[:, 1], ACT.Copy, scale=-1.0)
                act.activation(cs3[:, 2, :, 4 * m:4 * m + 4], src[:, 0], ACT.Copy, scale=-1.0).then_inc(act_bc, 1)
            act.wait_ge(ld_x, 16 * NT)
            for t in range(NT):
                if t:
                    act.wait_ge(act_sq, t)
                act.activation(scr, x_sb[:, t, :], ACT.Square, accum_out=stat[:, t:t + 1]).then_inc(act_sq, 1)
            act.wait_ge(dve_ms, 1)
            act.activation(stat[:, 4:4 + NT], stat[:, 4:4 + NT], ACT.Sqrt).then_inc(act_rt, 1)
            for m in range(2 * NT):
                t, k0 = m // 2, 4 * (m % 2)
                act.wait_ge(pe_hT, m + 1)
                act.activation(hT[:, k0:k0 + 4, t * P:(t + 1) * P],
                               ps[m % 2][:, :].rearrange("p (k n) -> p k n", k=4), ACT.Copy).then_inc(act_hT, 1)
            for m in range(8):
                i, half = m // 2, m % 2
                act.wait_ge(pe_u, m + 1)
                act.activation(u_c[0:C, 32 * half:32 * half + 32, i, :],
                               ps[4 + m % 2][0:C, :].rearrange("p (g h) -> p g h", h=GS), ACT.Copy
                               ).then_inc(act_u, 1)
                for w in range(4 * m, min(4 * m + 4, 16)):
                    act.wait_ge(pe_w, w + 1)
                    r = (w // 4) % 2
                    g0 = (w // 8) * GP + (w % 4) * 8
                    for i in range(2):
                        bank = ps[2 * (w % 2) + i]
                        act.activation(pt[64 * i:64 * i + 64, g0:g0 + 8, r, :],
                                       bank[64 * i:64 * i + 64, :].rearrange("p (g s) -> p g s", s=NS), ACT.Copy
                                       ).then_inc(act_pt, 1)
            for m in range(0, 8, 2):
                act.wait_ge(pe_uT, m + 1)
                src = ps[4 + m % 4][:, 0:4 * C].rearrange("p (g c) -> p g c", c=C)
                act.activation(uT[:, 4 * m:4 * m + 4, 0:CC], src[:, :, 0:CC], ACT.Copy)
                act.activation(uT[:, 4 * m:4 * m + 4, CC + 1:CX], src[:, :, CC:C], ACT.Copy).then_inc(act_uT, 1)
            for m in range(32):
                d, g0 = m // 16, 2 * (m % 16)
                act.wait_ge(pe_p, m + 1)
                act.activation(S[0:64, d, 1 - d:1 - d + CX, :, g0:g0 + 2].rearrange("p c r g -> p g r c"),
                               ps[2 * (m % 4)][0:64, 0:4 * CX].rearrange("p (g r c) -> p g r c", g=2, r=2),
                               ACT.Copy).then_inc(act_p, 1)
            def store_yT(k):
                act.wait_ge(pe_yT, k + 1)
                src = ps[k][:, 0:L * CX].rearrange("p (i c) -> p c i", i=L)
                dst = yT[:, k, :].rearrange("p (c i) -> p c i", i=L)
                act.activation(dst[:, 0:CC, :], src[:, 0:CC, :], ACT.Copy)
                act.activation(dst[:, CC:C, :], src[:, CC + 1:CX, :], ACT.Copy).then_inc(act_yT, 1)
            for k in range(KT):
                act.wait_ge(pe_y, k // 2 + 1)
                act.activation(y_b[:, k, :, :], ps[k][:, 0:4 * CX].rearrange("p (b c) -> p b c", b=4),
                               ACT.Gelu_apprx_tanh).then_inc(act_gelu, 1)
                if k == KT - 1:
                    for m in range(KT):
                        store_yT(m)
            for d in range(2):
                act.wait_ge(pe_fin, d + 1)
                act.activation(fins[:, d, :], ps[4 + d][0:2 * GP, 0:P], ACT.Copy).then_inc(act_fin, 1)

            def store_h2T(t):
                for m in (2 * t, 2 * t + 1):
                    k0 = 4 * (m % 2)
                    act.wait_ge(pe_h2T, m + 1)
                    act.activation(h2T[:, k0:k0 + 4, t * P:(t + 1) * P],
                                   ps[4 + m % 2][:, :].rearrange("p (k n) -> p k n", k=4), ACT.Copy
                                   ).then_inc(act_h2T, 1)
            for t in range(NT):
                for m in (2 * t, 2 * t + 1):
                    act.wait_ge(pe_glu, 2 * m + 2)
                    if m:
                        act.wait_ge(dve_x1, m)
                    act.activation(sig, ps[2 * (m % 2) + 1][:, :], ACT.Sigmoid).then_inc(act_sig, 1)
                act.wait_ge(dve_x1, 2 * t + 2)
                if t:
                    act.wait_ge(act_sq, NT + t)
                act.activation(yrow, x1[:, t, :], ACT.Square, accum_out=stat[:, t:t + 1]).then_inc(act_sq, 1)
                act.wait_ge(dve_ms, 2 + t)
                act.activation(stat[:, 4 + t:5 + t], stat[:, 4 + t:5 + t], ACT.Sqrt).then_inc(act_rt, 1)
                if t == 1:
                    store_h2T(0)
            for t in range(NT):
                act.wait_ge(dve_h2, t + 1)
                act.dma_start(h2_d[t * P:(t + 1) * P, :], h2[:, t, :]).then_inc(st_h2, 16)
                if t:
                    store_h2T(t)
            act.wait_ge(pe_logit, NT)
            act.activation(route[:, 0], ps[6][:, 0:NT * NE].rearrange("p (t e) -> p t e", t=NT), ACT.Sigmoid
                           ).then_inc(act_score, 1)

            def expert(it):
                for t in range(TT):
                    act.wait_ge(unit_free, it * NU + KT)
                    act.activation(sg[:, t, :], ps[t][:, 0:256], ACT.Silu).then_inc(silu_done, 1)
                act.wait_ge(at_ps, it * TT + 2)
                act.activation(aT[:, 0:2, :, :], ps[7][:, :].rearrange("p (t c n) -> p t c n", t=2, c=2), ACT.Copy
                               ).then_inc(at_ev, 1)
                act.wait_ge(at_ps, it * TT + 3)
                act.activation(aT[:, 2, :, :], ps[4][:, 256:512].rearrange("p (c n) -> p c n", c=2), ACT.Copy
                               ).then_inc(at_ev, 1)
                act.wait_ge(unit_free, it * NU + NU)
                act.wait_ge(y_free, it + 1)
                for t in range(TT):
                    for j in range(2):
                        src = ps[3 + t // 2][32 * j:32 * j + 32, 256 * (t % 2):256 * (t % 2) + 256]
                        act.activation(yrow[32 * t:32 * t + 32, 256 * j:256 * j + 256], src, ACT.Copy
                                       ).then_inc(y_ev, 1)
            act.wait_ge(dve_cmax, 1)
            with act.Fori(0, NE) as e:
                expert(e)
            v = act.value_load(cmaxi[0:1, 0:1], min_val=0, max_val=T)
            with act.If(v > CAP):
                with act.Fori(1, ROUNDS) as r:
                    with act.Fori(0, NE) as e:
                        expert(r * NE + e)
            act.nop()
            for t in range(NT):
                act.wait_ge(dve_x2, t + 1)
                act.activation(h2[:, t, :], x1[:, t, :], ACT.Square, accum_out=stat[:, t:t + 1]).then_inc(act_sq, 1)
                act.wait_ge(dve_ms, 2 + NT + t)
                act.activation(stat[:, 4 + t:5 + t], stat[:, 4 + t:5 + t], ACT.Sqrt).then_inc(act_rt, 1)

        @block.tensor
        def _(pe):
            def ada_piece(n):
                b, k = divmod(n, KT)
                if b == 0:
                    pe.wait_ge(ld_ada[n % 2], 16 * (n // 2 + 1))
                else:
                    pe.wait_ge(ld_late[n % 4], 16 * (n // 4 - 1))
                src = ada_w[:, n % 2, :] if b == 0 else ring[:, 8 + n % 4, :]
                for j in range(4):
                    last = pe.matmul(ps[ADA_BANK[b]][32 * j:32 * j + 32, :], silu_c[:, k, :],
                                     src[:, j * 512:(j + 1) * 512], start=(k == 0), stop=(k == KT - 1))
                last.then_inc(pe_ada, 1)

            def spread(bank, b, j, cond):
                return pe.matmul(bank[:, :], bsel[32 * j:32 * j + 32, cond, :], ada[32 * j:32 * j + 32, b, :],
                                 start=True, stop=True)

            pe.wait_ge(pool_const, 11)
            pe.wait_ge(ld_cond, 32)
            pe.transpose(ps[3][:, 0:16], rows[0:16, :], ident[0:16, 0:16]).then_inc(pe_tr, 1)
            pe.wait_ge(ld_lam, 16 * 5)
            pe.wait_ge(dve_dt, 1)
            pe.transpose(ps[4][:, 0:P], hnat, ident[:])
            pe.transpose(ps[7][:, 0:P], lnat, ident[:])
            pe.transpose(ps[7][:, P:P + DG], dtexp[0:DG, :], ident[0:DG, 0:DG]).then_inc(pe_tr, 1)
            pe.wait_ge(ld_bc, 16 * 6)
            for m in range(8):
                nat = bnat if m < 4 else cnat
                if m >= 2:
                    pe.wait_ge(act_bc, m - 1)
                for h in range(4 * (m % 4), 4 * (m % 4) + 4):
                    if m < 4:
                        src = nat.rearrange("p (n h) -> p n h", h=GS)[:, :, h]
                    else:
                        src = nat[:, h * P:(h + 1) * P]
                    last = pe.transpose(ps[5 + m % 2][:, (h % 4) * P:(h % 4 + 1) * P], src, ident[:])
                last.then_inc(pe_bc, 1)
            pe.wait_ge(act_silu, 1)
            for n in range(KT):
                ada_piece(n)
            pe.wait_ge(dve_ada, 1)
            pe.wait_ge(act_bc, 8)
            for cond in range(2):
                for b in range(2):
                    spread(ps[4 * cond + b], 0, 2 + b, cond)
                    last = spread(ps[4 * cond + 2 + b], 0, b, cond)
                last.then_inc(pe_mod, 1)
            for m in range(2 * NT):
                t, k0 = m // 2, 4 * (m % 2)
                pe.wait_ge(dve_h, t + 1)
                if m >= 2:
                    pe.wait_ge(act_hT, m - 1)
                for k in range(k0, k0 + 4):
                    last = pe.transpose(ps[m % 2][:, (k % 4) * P:(k % 4 + 1) * P],
                                        x_sb[:, t, k * P:(k + 1) * P], ident[:])
                last.then_inc(pe_hT, 1)
            pe.wait_ge(act_hT, 6)
            pe.wait_ge(ld_win, 16 * KT)
            for m in range(8):
                i, half = m // 2, m % 2
                if m >= 2:
                    pe.wait_ge(act_u, m - 1)
                for k in range(KT):
                    last = pe.matmul(ps[4 + m % 2][0:C, :], hT[:, k, i:T:L], win[:, k, half * 512:(half + 1) * 512],
                                     start=(k == 0), stop=(k == KT - 1))
                last.then_inc(pe_u, 1)
                for w in range(4 * m, min(4 * m + 4, 16)):
                    if w % 4 == 0:
                        pe.wait_ge(dve_w, m + 1)
                    if w >= 2:
                        pe.wait_ge(act_pt, 2 * (w - 1))
                    for g in range(8 * (w % 4), 8 * (w % 4) + 8):
                        for i in range(2):
                            a = slice(64 * i, 64 * i + 64)
                            last = pe.matmul(ps[2 * (w % 2) + i][a, (g % 8) * NS:(g % 8 + 1) * NS],
                                             w_pow[a, m % 2, g, :, :].rearrange("p k h -> p (k h)"),
                                             ident[a, a], start=True, stop=True)
                    last.then_inc(pe_w, 1)
            pe.wait_ge(act_u, 8)
            for m in range(8):
                if m >= 4:
                    pe.wait_ge(act_uT if m % 2 == 0 else dve_uT, (m - 4) // 2 + (1 if m % 2 == 0 else 2))
                for g in range(4 * m, 4 * m + 4):
                    src = u_c[0:C, 2 * g:2 * g + 2, :, :].rearrange("p i j h -> p (i j h)")
                    last = pe.transpose(ps[4 + m % 4][:, (g % 4) * C:(g % 4 + 1) * C], src, ident[0:C, 0:C])
                last.then_inc(pe_uT, 1)
            pe.wait_ge(dve_v, 4)
            pe.wait_ge(act_pt, 32)
            for i in range(2):
                for mq in range(2):
                    bank = ps[2 * i + mq]
                    for m4 in range(4):
                        for q in range(4):
                            g = 4 * (4 * mq + m4) + q
                            out = bank[32 * q:32 * q + 32, 112 * m4:112 * m4 + 112]
                            for d in range(2):
                                for r in range(2):
                                    o = ((1 + r) * DG + d * GP + g) * GS
                                    lhs = flat_s[64 * i:64 * i + 64, o:o + 32]
                                    rhs = V[64 * i:64 * i + 64, d * GP + g, r, d:d + 4, :].rearrange("p k h -> p (k h)")
                                    last = pe.matmul(out[:, 48:112] if d == 0 else out[:, 0:64], lhs, rhs,
                                                     start=(m4 == 0 and d == 0 and r == 0), stop=True,
                                                     skip_group_check=True)
                    last.then_inc(pe_k, 1)
            pe.wait_ge(act_uT, 4)
            pe.wait_ge(dve_uT, 5)
            pe.wait_ge(dve_k, 1)
            for m in range(32):
                d, g0 = m // 16, 2 * (m % 16)
                if m >= 4:
                    pe.wait_ge(act_p, m - 3)
                    pe.wait_ge(dve_p, m - 3)
                for gi in range(2):
                    for r in range(2):
                        for i in range(2):
                            a = slice(64 * i, 64 * i + 64)
                            o = (2 * gi + r) * CX
                            last = pe.matmul(ps[2 * (m % 4) + i][a, o:o + CX], pt[a, d * GP + g0 + gi, r, :],
                                             uT[a, g0 + gi, :], start=True, stop=True)
                last.then_inc(pe_p, 1)
            def y_parts(kk):
                for b in range(4):
                    for c2 in range(2):
                        yield (8 * kk + 2 * b + c2, [ps[2 * kk + i][64 * c2:64 * c2 + 64, b * CX:(b + 1) * CX]
                                                     for i in range(2)], b == 0)

            def y_inside(kk):
                for g, out, first in y_parts(kk):
                    for i in range(2):
                        a = slice(64 * i, 64 * i + 64)
                        pe.matmul(out[i], tmat[a, g, :], uT[a, g, :], start=first, stop=False,
                                  skip_group_check=True)

            def y_state(kk):
                parts = list(y_parts(kk))
                for b in range(4):
                    for d in range(2):
                        for r in range(2):
                            for g, out, _ in parts[2 * b:2 * b + 2]:
                                for i in range(2):
                                    a = slice(64 * i, 64 * i + 64)
                                    last = pe.matmul(
                                        out[i], V[a, d * GP + g, r, 1 - d:5 - d, :].rearrange("p k h -> p (k h)"),
                                        S[a, d, d:d + CX, r, g], start=False, stop=(d == 1 and r == 1),
                                        skip_group_check=True)
                last.then_inc(pe_y, 1)

            def y_channels(k):
                pe.wait_ge(act_gelu, 2 * (k // 2) + 2)
                for t in range(L):
                    for i in range(2):
                        for q in range(2):
                            last = pe.matmul(ps[k][64 * q:64 * q + 64, t * CX:(t + 1) * CX],
                                             pick[:, t, 16 - 16 * i:80 - 16 * i],
                                             y_b[:, 2 * (k // 2) + i, 2 * (k % 2) + q, :],
                                             start=(i == 0), stop=(i == 1))
                last.then_inc(pe_yT, 1)
            pe.wait_ge(act_p, 32)
            pe.wait_ge(dve_p, 32)
            pe.wait_ge(ld_tmat, 16 * 32)
            for kk in range(3):
                y_inside(kk)
            for n in range(KT, 3 * KT):
                ada_piece(n)
            pe.wait_ge(dve_scan, 1)
            for kk in range(3):
                y_state(kk)
            pe.wait_ge(dve_ada, 3)
            y_inside(3)
            y_state(3)
            pe.wait_ge(pool_pick, 2)
            for k in range(KT):
                y_channels(k)
            pe.wait_ge(act_yT, 6)
            for d in range(2):
                slot = CC if d == 0 else 0
                pe.transpose(ps[4 + d][0:2 * GP, 0:P], S[:, d, slot, :, :].rearrange("p r g -> p (r g)"),
                             ident[:]).then_inc(pe_fin, 1)
            pe.wait_ge(act_yT, 8)
            pe.wait_ge(act_fin, 2)
            pe.wait_ge(ld_glu, 16 * KT)

            def rows2(pair):
                for n in (2 * pair, 2 * pair + 1):
                    cond, row = n // 4, n % 4
                    if n >= 2:
                        pe.wait_ge(dve_rows2, n - 1)
                    b, j = (2, row) if row < 2 else (1, row)
                    spread(ps[4 + n % 2], b, j, cond).then_inc(pe_rows2, 1)

            def transpose_h2(t):
                pe.wait_ge(dve_h2, t + 1)
                for m in (2 * t, 2 * t + 1):
                    k0 = 4 * (m % 2)
                    if m >= 2:
                        pe.wait_ge(act_h2T, m - 1)
                    for k in range(k0, k0 + 4):
                        last = pe.transpose(ps[4 + m % 2][:, (k % 4) * P:(k % 4 + 1) * P],
                                            h2[:, t, k * P:(k + 1) * P], ident[:])
                    last.then_inc(pe_h2T, 1)
            rows2(0)
            for m in range(6):
                t, half = m // 2, m % 2
                if m in (0, 2):
                    if m:
                        pe.wait_ge(dve_x1, 2)
                    spread(ps[6], 1, 0, m // 2)
                    spread(ps[7], 1, 1, m // 2).then_inc(pe_g1, 1)
                if m >= 2:
                    pe.wait_ge(dve_x1, m - 1)
                for part in range(2):
                    col = part * D + half * 512
                    for k in range(KT):
                        last = pe.matmul(ps[2 * (m % 2) + part][:, :], yT[:, k, t * P:(t + 1) * P],
                                         ring[:, 4 + k, col:col + 512], start=(k == 0), stop=(k == KT - 1))
                    last.then_inc(pe_glu, 1)
                    if 2 * m + part < 3:
                        rows2(2 * m + part + 1)
                if m == 3:
                    pe.wait_ge(dve_rows2, 8)
                    transpose_h2(0)
            transpose_h2(1)
            transpose_h2(2)
            pe.wait_ge(act_h2T, 6)
            pe.wait_ge(ld_route, 48)
            for t in range(NT):
                for k in range(KT):
                    last = pe.matmul(ps[6][:, t * NE:(t + 1) * NE], h2T[:, k, t * P:(t + 1) * P], rw[:, k, :],
                                     start=(k == 0), stop=(k == KT - 1))
                last.then_inc(pe_logit, 1)
            pe.wait_ge(dve_mask, 1)
            pe.wait_ge(pool_late, 13)
            for t in range(NT + 1):
                out = ps[7][:, t * NE:(t + 1) * NE]
                for u in range(min(t + 1, NT)):
                    last = pe.matmul(out, tri[:, 0 if u == t else 1, :], route[:, 20, u, :],
                                     start=(u == 0), stop=(u == min(t, NT - 1)))
            last.then_inc(pe_pos, 1)

            def transpose_x(nth):
                pe.wait_ge(ld_xg, nth * 16 + 16)
                for k in range(KT):
                    bank, col = (ps[5], k) if k < 5 else (ps[6], k - 5)
                    last = pe.transpose(bank[:, col * CAP:(col + 1) * CAP], xg[0:CAP, k * P:(k + 1) * P],
                                        ident[0:CAP, 0:CAP])
                last.then_inc(xt_ps, 1)

            def expert(it, last_of_round):
                pe.wait_ge(xt_ev, it * 2 + 2)
                pe.wait_ge(prod_done, it * TT + TT)
                for k in range(KT):
                    pe.wait_ge(ld_unit[k], it * 32 + 32)
                    w = ring[:, k, :].rearrange("p (a n) -> p a n", a=2)
                    for t in range(TT):
                        for j in range(4):
                            last = pe.matmul(ps[t][32 * j:32 * j + 32, :], xgT[:, k, 32 * t:32 * t + 32],
                                             w[:, :, 256 * j:256 * j + 256], start=(k == 0), stop=(k == KT - 1))
                    last.then_inc(unit_free, 1)
                if not last_of_round:
                    transpose_x(it + 1)
                for t in range(TT):
                    pe.wait_ge(prod_done, it * TT + (TT + t + 1))
                    if t == 2:
                        pe.wait_ge(y_ev, it * 12 + 12)
                    for c2 in range(2):
                        out = ps[7][:, 256 * t + P * c2:256 * t + P * c2 + P] if t < 2 else \
                            ps[4][:, 256 + P * c2:256 + P * c2 + P]
                        last = pe.transpose(out, act_a[:, t, c2 * P:(c2 + 1) * P], ident[:])
                    last.then_inc(at_ps, 1)
                pe.wait_ge(at_ev, it * 2 + 2)
                pe.wait_ge(y_ev, it * 12 + 12)
                for kk in range(KT):
                    j, c2 = kk // 2, kk % 2
                    if c2 == 0:
                        pe.wait_ge(ld_unit[KT + j], it * 32 + 32)
                    for t in range(TT):
                        for dj in range(4):
                            last = pe.matmul(ps[3 + t // 2][32 * dj:32 * dj + 32, 256 * (t % 2):256 * (t % 2) + 256],
                                             aT[:, t, c2, 32 * j:32 * j + 32],
                                             ring[:, KT + j, c2 * D + 256 * dj:c2 * D + 256 * dj + 256],
                                             start=(kk == 0 and t != 1), stop=(kk == KT - 1),
                                             skip_group_check=True)
                    if c2 == 1:
                        last.then_inc(unit_free, 1)

            pe.wait_ge(dve_cmax, 1)
            transpose_x(0)
            with pe.Fori(0, NE - 1) as e:
                expert(e, False)
            expert(NE - 1, True)
            v = pe.value_load(cmaxi[0:1, 0:1], min_val=0, max_val=T)
            with pe.If(v > CAP):
                with pe.Fori(1, ROUNDS) as r:
                    transpose_x(r * NE)
                    with pe.Fori(0, NE - 1) as e:
                        expert(r * NE + e, False)
                    expert(r * NE + NE - 1, True)
            pe.nop()
            for cond in range(2):
                for b in range(2):
                    last = spread(ps[(5, 0)[cond] + b], 2, 2 + b, cond)
            last.then_inc(pe_g2, 1)

        @block.vector
        def _(dve):
            n = [0]

            def step(ins, wait=True):
                n[0] += 1
                ins.then_inc(dve_done, 1)
                if wait:
                    dve.wait_ge(dve_done, n[0])
            tt, ts, stt, cp = dve.tensor_tensor, dve.tensor_scalar, dve.scalar_tensor_tensor, dve.tensor_copy

            dve.wait_ge(ld_lam, 16 * 5)
            cp(dtexp[0:DG, :].rearrange("p (i s) -> p i s", i=2),
               dtnat[0:DG, :].rearrange("p (i a) -> p i a", a=1).to_broadcast((DG, 2, NS))).then_inc(dve_dt, 1)
            X, N_, R_, Q_ = (tab[:, i, :] for i in (0, 1, 2, 3))
            LR, LI, DT, MAG = (tab[:, i, :] for i in (9, 10, 11, 12))
            intv = tab[:, 4, :].bitcast(I32)
            dve.wait_ge(pe_tr, 2)
            step(cp(LR, ps[7][:, 0:DG]), False)
            step(cp(LI, ps[7][:, DG:2 * DG]), False)
            step(cp(X, ps[7][:, P:P + DG]))

            def exp_of(out):
                step(ts(N_, X, LOG2E, MAGIC, ALU.mult, ALU.add))
                step(ts(N_, N_, -MAGIC, None, ALU.add))
                step(ts(N_, N_, -126.0, 127.0, ALU.max, ALU.min))
                step(stt(R_, N_, -LN2_HI, X, ALU.mult, ALU.add))
                step(stt(R_, N_, -LN2_LO, R_, ALU.mult, ALU.add))
                step(ts(R_, R_, -88.0, 1.0, ALU.max, ALU.min))
                step(ts(Q_, R_, EXP_C[0], None, ALU.mult))
                for coef in EXP_C[1:]:
                    step(stt(Q_, Q_, coef, R_, ALU.add, ALU.mult))
                step(ts(Q_, Q_, 1.0, None, ALU.add))
                step(ts(N_, N_, 127.0, 8388608.0, ALU.add, ALU.mult))
                step(cp(intv, N_))
                step(tt(out, Q_, tab[:, 4, :], ALU.mult))
            exp_of(DT)
            TH = tab[:, 13, :]
            step(tt(TH, LI, DT, ALU.mult))
            step(ts(N_, TH, INV_2PI, MAGIC, ALU.mult, ALU.add))
            step(ts(N_, N_, -MAGIC, None, ALU.add))
            step(stt(TH, N_, -TP1, TH, ALU.mult, ALU.add))
            step(stt(TH, N_, -TP2, TH, ALU.mult, ALU.add))
            step(stt(TH, N_, -TP3, TH, ALU.mult, ALU.add))
            step(ts(tab[:, 5, :], TH, -PI_SAFE, PI_SAFE, ALU.max, ALU.min))
            step(stt(R_, tab[:, 5, :], -1.0, tab[:, 5, :], ALU.mult, ALU.max))
            ts(tab[:, 6, :], R_, -1.0, math.pi / 2, ALU.mult, ALU.add).then_inc(dve_trig, 1)
            dve.wait_ge(dve_trig, 1)
            step(tt(X, LR, DT, ALU.mult))
            exp_of(MAG)
            dve.wait_ge(act_trig, 2)
            WR = tab[:, 14:18, :].rearrange("p n g -> p (n g)").rearrange("p (g k) -> p g k", k=L)
            WI = tab[:, 18:22, :].rearrange("p n g -> p (n g)").rearrange("p (g k) -> p g k", k=L)
            VR = tab[:, 22:27, :].rearrange("p n g -> p (n g)").rearrange("p (g k) -> p g k", k=NP_V)
            VI = tab[:, 27:32, :].rearrange("p n g -> p (n g)").rearrange("p (g k) -> p g k", k=NP_V)
            AR, AI = tab[:, 4, :], tab[:, 5, :]
            step(tt(AR, MAG, tab[:, 8, :], ALU.mult), False)
            step(tt(tab[:, 6, :], MAG, tab[:, 7, :], ALU.mult))
            step(cp(AI, tab[:, 6, :]))
            PR, PI_ = tab[:, 7, :], tab[:, 8, :]
            step(dve.memset(PR, 1.0), False)
            step(dve.memset(PI_, 0.0))
            for k in range(NP_V):
                for d in range(2):
                    g = slice(d * GP, (d + 1) * GP)
                    if k < L:
                        step(cp(WR[:, g, L - 1 - k if d == 0 else k], PR[:, g]), False)
                        step(cp(WI[:, g, L - 1 - k if d == 0 else k], PI_[:, g]), False)
                    step(cp(VR[:, g, k if d == 0 else L - k], PR[:, g]), False)
                    step(cp(VI[:, g, k if d == 0 else L - k], PI_[:, g]), False)
                if k < L:
                    step(tt(X, PR, AR, ALU.mult), False)
                    step(tt(N_, PI_, AI, ALU.mult), False)
                    step(tt(R_, PR, AI, ALU.mult), False)
                    step(tt(Q_, PI_, AR, ALU.mult))
                    step(tt(PR, X, N_, ALU.subtract), False)
                    step(tt(PI_, R_, Q_, ALU.add))
            step(cp(a4r[:], PR), False)
            step(cp(a4i[:, 1, :], PI_), False)
            step(ts(a4i[:, 0, :], PI_, -1.0, None, ALU.mult), False)
            NR, DEN, FR, FI = tab[:, 6, :], tab[:, 13, :], tab[:, 7, :], tab[:, 8, :]
            step(ts(NR, AR, -1.0, None, ALU.add), False)
            step(tt(X, LR, LR, ALU.mult), False)
            step(tt(N_, LI, LI, ALU.mult))
            step(tt(DEN, X, N_, ALU.add))
            step(dve.reciprocal(DEN, DEN))
            step(tt(X, NR, LR, ALU.mult), False)
            step(tt(N_, AI, LI, ALU.mult), False)
            step(tt(R_, AI, LR, ALU.mult), False)
            step(tt(Q_, NR, LI, ALU.mult))
            step(tt(X, X, N_, ALU.add), False)
            step(tt(R_, R_, Q_, ALU.subtract))
            step(tt(FR, X, DEN, ALU.mult), False)
            step(tt(FI, R_, DEN, ALU.mult))
            dve.wait_ge(act_bc, 4)
            braw = t2[:, 0:2 * DG * GS].rearrange("p (r g h) -> p r g h", r=2, h=GS)

            def over_h(a):
                return a.rearrange("p (g a) -> p g a", a=1).to_broadcast((P, DG, GS))
            step(tt(bs3[:, 1], braw[:, 0], over_h(FR), ALU.mult), False)
            step(tt(bs3[:, 0], braw[:, 1], over_h(FI), ALU.mult), False)
            step(tt(bs3[:, 2], braw[:, 1], over_h(FR), ALU.mult))
            step(tt(braw[:, 0], braw[:, 0], over_h(FI), ALU.mult))
            step(tt(bs3[:, 1], bs3[:, 1], bs3[:, 0], ALU.subtract), False)
            step(tt(bs3[:, 2], bs3[:, 2], braw[:, 0], ALU.add))
            step(ts(bs3[:, 0], bs3[:, 2], -1.0, None, ALU.mult))
            dve.wait_ge(act_sq, NT)
            ts(stat[:, 4:4 + NT], stat[:, 0:NT], 1.0 / D, EPS, ALU.mult, ALU.add).then_inc(dve_ms, 1)

            def outer(out, tmp, pr, pi, three, r, g, nk):
                def powers(a):
                    return a[:, g, :].rearrange("p g (k a) -> p g k a", a=1).to_broadcast((P, GP, nk, GS))

                def rep(a):
                    return a[:, g, :].rearrange("p g (a h) -> p g a h", a=1).to_broadcast((P, GP, nk, GS))
                step(tt(out, powers(pr), rep(three[0]), ALU.mult), False)
                step(tt(tmp, powers(pi), rep(three[1]), ALU.mult))
                return tt(out, out, tmp, ALU.add)

            tmp_w = t2[:, 0:GP * L * GS].rearrange("p (g k h) -> p g k h", k=L, h=GS)
            tmp_v = t2.rearrange("p (g k h) -> p g k h", k=NP_V, h=GS)
            def w_part(b):
                d, r = divmod(b, 2)
                if b >= 2:
                    dve.wait_ge(pe_w, 4 * (b - 1))
                outer(w_pow[:, b % 2], tmp_w, WR, WI, (bs3[:, 1 + r], bs3[:, r]), r,
                      slice(d * GP, (d + 1) * GP), L).then_inc(dve_w, 1)
                dve.wait_ge(dve_w, b + 1)

            def v_part(d, r):
                g = slice(d * GP, (d + 1) * GP)
                outer(V[:, g, r], tmp_v, VR, VI, (cs3[:, r], cs3[:, 1 + r]), r, g, NP_V).then_inc(dve_v, 1)
                dve.wait_ge(dve_v, 2 * d + r + 1)

            def ada_rows(b):
                dve.wait_ge(pe_ada, KT * (b + 1))
                step(tt(ada[:, b, :], ps[ADA_BANK[b]][:, :], ada[:, b, :], ALU.add))
                if b == 0:
                    stt(ada[64:P, 0, :], ada[64:P, 0, :], 1.0, gains[64:P, :], ALU.add, ALU.mult).then_inc(dve_ada, 1)
                elif b == 2:
                    stt(ada[0:64, 2, :], ada[0:64, 2, :], 1.0, gains[0:64, :], ALU.add, ALU.mult).then_inc(dve_ada, 1)
                else:
                    dve.sem_inc(dve_ada, 1)
            dve.wait_ge(ld_rows, 16 * 16)
            w_part(0)
            ada_rows(0)
            dve.wait_ge(act_rt, 1)
            step(dve.reciprocal(stat[:, 4:4 + NT], stat[:, 4:4 + NT]))

            def modulate(t, src, dst, rows4, done):
                for b in range(2):
                    c2 = slice(512 * b, 512 * b + 512)
                    step(stt(dst[:, t, c2], src[:, t, c2], stat[:, 4 + t:5 + t], rows4[b], ALU.mult, ALU.mult),
                         b == 1)
                step(tt(dst[:, t, 0:512], dst[:, t, 0:512], rows4[2], ALU.add), False)
                tt(dst[:, t, 512:D], dst[:, t, 512:D], rows4[3], ALU.add).then_inc(done, 1)
                dve.wait_ge(dve_done, n[0])
            for t in range(NT):
                dve.wait_ge(pe_mod, 1 if t == 0 else 2)
                modulate(t, x_sb, x_sb, [ps[b + (4 if t else 0)][:, :] for b in range(4)], dve_h)
            w_part(1)
            dve.wait_ge(act_bc, 8)
            dve.wait_ge(act_sq, NT)
            dve.wait_ge(pe_bc, 8)
            v_part(0, 0)
            w_part(2)
            dve.wait_ge(pe_hT, 6)
            v_part(0, 1)
            w_part(3)
            v_part(1, 0)
            v_part(1, 1)
            for q in range(4):
                a = slice(32 * q, 32 * q + 32)
                step(cp(i16[a, :], ident[a, 32 * q:32 * q + 16]), q == 3)
            dve.wait_ge(ld_dtab, 16 * 8)
            step(tt(dskip, i16[:, :].rearrange("p (a b h) -> p a b h", a=1, b=1).to_broadcast((P, 2, 8, GS)),
                    dtab[:, :, :].rearrange("p a (q h) -> p a q h", h=1).to_broadcast((P, 2, 8, GS)), ALU.mult))
            dve.wait_ge(pe_w, 16)
            step(dve.memset(uT[:, :, CC:CC + 1], 0.0), False)
            n_ut = n[0]
            for m in range(1, 8, 2):
                dve.wait_ge(pe_uT, m + 1)
                src = ps[4 + m % 4][:, 0:4 * C].rearrange("p (g c) -> p g c", c=C)
                step(cp(uT[:, 4 * m:4 * m + 4, 0:CC], src[:, :, 0:CC]), False)
                cp(uT[:, 4 * m:4 * m + 4, CC + 1:CX], src[:, :, CC:C]).then_inc(dve_uT, 2 if m == 1 else 1)
            for m in range(4):
                i, mq = m // 2, m % 2
                dve.wait_ge(pe_k, m + 1)
                step(cp(kpad[:, i, 4 * mq:4 * mq + 4, :], ps[m][:, 0:448].rearrange("p (q w) -> p q w", w=112)))
            tt(kpad[:, :, :, 48:64], kpad[:, :, :, 48:64], dskip, ALU.add).then_inc(dve_k, 1)
            for m in range(32):
                d, g0 = m // 16, 2 * (m % 16)
                dve.wait_ge(pe_p, m + 1)
                cp(S[64:P, d, 1 - d:1 - d + CX, :, g0:g0 + 2].rearrange("p c r g -> p g r c"),
                   ps[2 * (m % 4) + 1][64:P, 0:4 * CX].rearrange("p (g r c) -> p g r c", g=2, r=2)
                   ).then_inc(dve_p, 1)
            dve.wait_ge(act_p, 32)
            dve.wait_ge(dve_p, 32)
            dve.wait_ge(act_h0, 1)
            hv = h0[:, :].rearrange("p (r d g) -> p r d g", r=2, d=2)
            step(dve.memset(S[:, 0, 0, :, :], 0.0), False)
            step(cp(S[:, 0, CC + 1, :, :], hv[:, :, 0, :]), False)
            step(cp(S[:, 1, CX, :, :], hv[:, :, 1, :]))
            A4R = a4r[:, :].rearrange("p (d a g) -> p d a g", d=2, a=1).to_broadcast((P, 2, 2, GP))
            A4I = a4i[:, :, :].rearrange("p r (d g) -> p d r g", d=2)
            prev = [0, 0]
            for k in range(CL - 1):
                live = [st for st in range(2) if k < (CC, CL - 1)[st]]
                f = [k, CC + 1 + k]
                b = [CC - k, CX - k]
                mark = {}
                for st in live:
                    if prev[st]:
                        dve.wait_ge(dve_done, prev[st])
                    tb = [scan_t[:, st, x, :].rearrange("p (d r g) -> p d r g", d=2, r=2) for x in range(2)]
                    step(tt(tb[0], A4R, chunk_states(0, f[st], b[st] - f[st], False), ALU.mult), False)
                    step(tt(tb[1], A4I, chunk_states(0, f[st], b[st] - f[st], True), ALU.mult), False)
                    mark[st] = n[0]
                for x in range(2):
                    for st in live:
                        tb = scan_t[:, st, x, :].rearrange("p (d r g) -> p d r g", d=2, r=2)
                        to = chunk_states(0, f[st] + 1, b[st] - 1 - f[st] - 1, False)
                        dve.wait_ge(dve_done, mark[st] - (1 - x) if x == 0 else max(prev[st], mark[st]))
                        step(tt(to, to, tb, ALU.add), False)
                        prev[st] = n[0]
            dve.wait_ge(dve_done, n[0])
            dve.sem_inc(dve_scan, 1)

            for b in (1, 2):
                ada_rows(b)

            def rows2(n):
                dve.wait_ge(pe_rows2, n + 1)
                cp(mod2[:, n // 4, n % 4, :], ps[4 + n % 2][:, :]).then_inc(dve_rows2, 1)
            dve.wait_ge(pe_fin, 2)
            for k in range(6):
                rows2(k)
            dve.wait_ge(ld_xagain, 16 * NT)
            for t in range(NT):
                for half in range(2):
                    m = 2 * t + half
                    c2 = slice(512 * half, 512 * half + 512)
                    dve.wait_ge(act_sig, m + 1)
                    dve.wait_ge(pe_g1, 1 if t == 0 else 2)
                    step(tt(prod, sig, ps[2 * (m % 2)][:, :], ALU.mult))
                    step(tt(prod, prod, ps[6 + half][:, :], ALU.mult))
                    tt(x1[:, t, c2], x1[:, t, c2], prod, ALU.add).then_inc(dve_x1, 1)
                    dve.wait_ge(dve_x1, m + 1)
                    if m == 0:
                        rows2(6)
                        rows2(7)
                dve.wait_ge(act_sq, NT + t + 1)
                ts(stat[:, 4 + t:5 + t], stat[:, t:t + 1], 1.0 / D, EPS, ALU.mult, ALU.add).then_inc(dve_ms, 1)
                dve.wait_ge(act_rt, 2 + t)
                step(dve.reciprocal(stat[:, 4 + t:5 + t], stat[:, 4 + t:5 + t]))
                dve.wait_ge(dve_rows2, 8)
                modulate(t, x1, h2, [mod2[:, 1 if t else 0, b, :] for b in range(4)], dve_h2)
            dve.wait_ge(act_score, 1)
            dve.wait_ge(pool_late, 13)
            dve.wait_ge(ld_route, 48)
            sc, bi = route[:, 0], route[:, 1]

            def over_e(a):
                return a.to_broadcast((P, NT, NE))
            step(tt(bi, sc, rb.rearrange("p (a e) -> p a e", a=1).to_broadcast((P, NT, NE)), ALU.add))
            b4 = bi.rearrange("p t (g m a) -> p (t g) m a", g=NGRP, a=2)
            s2 = route[:, 2].rearrange("p t (g m) -> p (t g) m", g=NGRP)[:, :, 0:2]
            m2 = route[:, 3].rearrange("p t (g m) -> p (t g) m", g=NGRP)[:, :, 0:2]
            gsc = route[:, 4, :, 0:NGRP]
            g1 = route[:, 5, :, 0:NGRP]
            g2 = route[:, 6, :, 0:NGRP]
            step(tt(s2, b4[:, :, :, 0], b4[:, :, :, 1], ALU.add), False)
            step(tt(m2, b4[:, :, :, 0], b4[:, :, :, 1], ALU.max))

            def per_group(a, i):
                return a.rearrange("p t (g m) -> p t g m", g=NGRP)[:, :, :, i]
            step(tt(g1, per_group(route[:, 2], 0), per_group(route[:, 2], 1), ALU.max), False)
            step(tt(g2, per_group(route[:, 3], 0), per_group(route[:, 3], 1), ALU.add))
            step(tt(gsc, g1, g2, ALU.max))
            gm = route[:, 7, :, 0:1]

            def first_max(val, m1, key, rk, shape, out):
                step(dve.tensor_reduce(m1, val, AX.X, ALU.max))
                step(tt(key, val, m1.to_broadcast(shape), ALU.is_equal))
                step(tt(key, key, rk, ALU.mult))
                step(dve.tensor_reduce(m1, key, AX.X, ALU.max))
                step(tt(out, key, m1.to_broadcast(shape), ALU.is_equal))
            first_max(gsc, gm, g1, grank, (P, NT, NGRP), g2)
            mb = route[:, 8]
            mk = route[:, 9]
            step(cp(mk.rearrange("p t (g m) -> p t g m", g=NGRP),
                    g2.rearrange("p t (g a) -> p t g a", a=1).to_broadcast((P, NT, NGRP, EPG))))
            step(tt(mb, bi, mk, ALU.mult), False)
            step(ts(mk, mk, 1e30, -1e30, ALU.mult, ALU.add))
            step(tt(mb, mb, mk, ALU.add))
            oh = [route[:, 10], route[:, 11]]
            first_max(mb, route[:, 12, :, 0:1], route[:, 13], rank, (P, NT, NE), oh[0])
            step(stt(mb, oh[0], -2e30, mb, ALU.mult, ALU.add))
            first_max(mb, route[:, 14, :, 0:1], route[:, 15], rank, (P, NT, NE), oh[1])
            tt(route[:, 20], oh[0], oh[1], ALU.add).then_inc(dve_mask, 1)
            for k in range(2):
                step(tt(route[:, 16 + k], sc, oh[k], ALU.mult))
                step(dve.tensor_reduce(cmb[:, k, :], route[:, 16 + k], AX.X, ALU.add))
            wsum = route[:, 18, 0, 0:NT]
            step(tt(wsum, cmb[:, 0, :], cmb[:, 1, :], ALU.add))
            step(dve.reciprocal(wsum, wsum))
            for k in range(2):
                step(tt(cmb[:, k, :], cmb[:, k, :], wsum, ALU.mult))
            dve.wait_ge(pe_pos, 1)
            step(dve.tensor_reduce(cmax[:], ps[7][:, NT * NE:(NT + 1) * NE], AX.X, ALU.max))
            cp(cmaxi[:], cmax[:]).then_inc(dve_cmax, 1)
            step(tt(route[:, 21], ps[7][:, 0:NT * NE].rearrange("p (t e) -> p t e", t=NT), e384, ALU.add))
            for k in range(2):
                step(tt(route[:, 22 + k], route[:, 21], oh[k], ALU.mult))
                step(dve.tensor_reduce(route[:, 19, k, 0:NT], route[:, 22 + k], AX.X, ALU.add))
                ins = cp(sloti[:, k, :], route[:, 19, k, 0:NT])
                if k == 0:
                    step(ins)
            ins.then_inc(dve_slot, 1)

            def evict_x(nth):
                dve.wait_ge(xt_ps, nth + 1)
                cp(xgT[:, 0:5, :], ps[5][:, 0:5 * CAP].rearrange("p (k n) -> p k n", k=5)).then_inc(xt_ev, 1)
                cp(xgT[:, 5:8, :], ps[6][:, 0:3 * CAP].rearrange("p (k n) -> p k n", k=3)).then_inc(xt_ev, 1)

            def expert(it, last_of_round):
                for t in range(TT):
                    dve.wait_ge(silu_done, it * TT + (t + 1))
                    tt(act_a[:, t, :], sg[:, t, :], ps[t][:, 256:512], ALU.mult).then_inc(prod_done, 1)
                if not last_of_round:
                    evict_x(it + 1)
                dve.wait_ge(unit_free, it * NU + NU)
                dve.wait_ge(y_free, it + 1)
                for t in range(TT):
                    for j in range(2, 4):
                        src = ps[3 + t // 2][32 * j:32 * j + 32, 256 * (t % 2):256 * (t % 2) + 256]
                        cp(yrow[32 * t:32 * t + 32, 256 * j:256 * j + 256], src).then_inc(y_ev, 1)
            dve.sem_inc(prod_done, TT)
            dve.sem_inc(y_ev, 12)
            evict_x(0)
            with dve.Fori(0, NE - 1) as e:
                expert(e, False)
            expert(NE - 1, True)
            v = dve.value_load(cmaxi[0:1, 0:1], min_val=0, max_val=T)
            with dve.If(v > CAP):
                with dve.Fori(1, ROUNDS) as r:
                    evict_x(r * NE)
                    with dve.Fori(0, NE - 1) as e:
                        expert(r * NE + e, False)
                    expert(r * NE + NE - 1, True)
            dve.nop()
            dve.wait_ge(ld_y2, 32)
            dve.wait_ge(pe_g2, 1)
            for t in range(NT):
                g = 5 if t == 0 else 0
                step(ts(m_out[:, t, :], y2c[:, 0, t, :], cmb[:, 0, t:t + 1], None, ALU.mult))
                step(stt(m_out[:, t, :], y2c[:, 1, t, :], cmb[:, 1, t:t + 1], m_out[:, t, :], ALU.mult, ALU.add))
                for b in range(2):
                    c2 = slice(512 * b, 512 * b + 512)
                    step(tt(m_out[:, t, c2], m_out[:, t, c2], ps[g + b][:, :], ALU.mult), b == 1)
                tt(x1[:, t, :], x1[:, t, :], m_out[:, t, :], ALU.add).then_inc(dve_x2, 1)
                dve.wait_ge(act_sq, 2 * NT + t + 1)
                ts(stat[:, 4 + t:5 + t], stat[:, t:t + 1], 1.0 / D, EPS, ALU.mult, ALU.add).then_inc(dve_ms, 1)
                dve.wait_ge(act_rt, 2 + NT + t)
                step(dve.reciprocal(stat[:, 4 + t:5 + t], stat[:, 4 + t:5 + t]))
                stt(yo[:, t, :], x1[:, t, :], stat[:, 4 + t:5 + t], gfin, ALU.mult, ALU.mult).then_inc(dve_out, 1)


_INS = ["x_prompt", "x_sample", "c", "state_ssm_re", "state_ssm_im", "c_ctx", "norm_mix", "norm_ffn",
        "w_ada", "b_ada", "ssm_w_in", "ssm_lam_re", "ssm_lam_im", "ssm_log_dt", "ssm_b_re", "ssm_b_im",
        "ssm_c_re", "ssm_c_im", "ssm_d", "ssm_w_glu", "router_w", "router_b", "moe_w_gate", "moe_w_up",
        "moe_w_down", "norm_final"]
_OUTS = [("y_prompt", (1, T_CTX, D)), ("y_sample", (1, T_LAT, D)),
         ("new_re", (1, 1, 2, G, NS)), ("new_im", (1, 1, 2, G, NS))]


def kernel(**inputs):
    import numpy as np
    import concourse.bacc as bacc
    from concourse.bass_utils import run_bass_kernel_spmd

    nc = bacc.Bacc("TRN2", target_bir_lowering=False, num_devices=1)
    arrays, args = {}, []
    for name in _INS:
        a = np.ascontiguousarray(inputs[name])
        arrays[f"in_{name}"] = a
        args.append(nc.dram_tensor(f"in_{name}", a.shape, mybir.dt.from_np(a.dtype), kind="ExternalInput").ap())
    for name, shape in _OUTS:
        args.append(nc.dram_tensor(f"out_{name}", shape, F32, kind="ExternalOutput").ap())
    build(nc, *args)
    r = run_bass_kernel_spmd(nc, [arrays], core_ids=[0])
    return tuple(r.results[0][f"out_{name}"] for name, _ in _OUTS)
```

```python
from contextlib import ExitStack
import math

import concourse.bass as bass
from concourse import mybir

F32 = mybir.dt.float32
I32 = mybir.dt.int32
U32 = mybir.dt.uint32
ALU = mybir.AluOpType
ACT = mybir.ActivationFunctionType
AX = mybir.AxisListType

P = 128
D = 1024
KT = D // P
T_CTX, T_LAT = 128, 256
T = T_CTX + T_LAT
NT = T // P
G, GS, NS = 64, 16, 64
GP = G // 2
DG = 2 * GP
L = 4
CC, CL = T_CTX // L, T_LAT // L
C = CC + CL
CX = C + 1
SLOTS = CX + 1
NP_V = L + 1
NE, NGRP, EPG = 16, 4, 4
FE = 1024
CAP = 96
TT = CAP // 32
ROUNDS = T // CAP
EPS = 1e-6
ADA_BANK = (0, 6, 7)
ADA_SLOTS = (0, 1, 2, 3, 8, 9, 10)
OOB = 1 << 20
UNIT = 2048
NU = 12
MAGIC = 12582912.0
LOG2E = 1.4426950408889634
LN2_HI, LN2_LO = 0.693359375, -2.12194440e-4
INV_2PI = 1.0 / (2.0 * math.pi)
TP1 = 6.28125
TP2 = 0.0019350051879882812
TP3 = 2.0 * math.pi - TP1 - TP2
PI_SAFE = 3.1415925
EXP_C = [1.0 / 5040, 1.0 / 720, 1.0 / 120, 1.0 / 24, 1.0 / 6, 0.5, 1.0]


def build(nc, x_prompt, x_sample, c, state_re, state_im, c_ctx, norm_mix, norm_ffn, w_ada, b_ada,
          w_in, lam_re, lam_im, log_dt, b_re, b_im, c_re, c_im, ssm_d, w_glu, router_w, router_b,
          w_gate, w_up, w_down, norm_final, y_prompt, y_sample, new_re, new_im):
    y2_d = nc.dram_tensor("y2_scratch", [2 * T, D], F32, kind="Internal").ap()
    rows_d = nc.dram_tensor("ada_rows", [2, 2, 4, 512], F32, kind="Internal").ap()
    list_d = nc.dram_tensor("slot_list", [NE * T, 1], I32, kind="Internal").ap()

    ctx = ExitStack()
    with ctx:
        def sb(name, shape, dt=F32):
            return ctx.enter_context(nc.sbuf_tensor(name, shape, dt))

        def sem(name):
            return ctx.enter_context(nc.semaphore(name))

        ring = sb("ring", [P, NU, UNIT])
        sreg = sb("sreg", [P, 2 * SLOTS * DG])
        vreg = sb("vreg", [P, 2 * DG * NP_V * GS])
        tmat = sb("tmat", [P, GP, L * GS])
        ada = sb("ada", [P, 3, 512])
        gains = sb("gains", [P, 512])
        ident = sb("ident", [P, P])
        a4r = sb("a4r", [P, DG])
        a4i = sb("a4i", [P, 2, DG])
        h0 = sb("h0", [P, P])
        silu_c = sb("silu_c", [P, KT, 32])
        stat = sb("stat", [P, 16])
        scan_t = sb("scan_t", [P, 2, 2, P])
        cmb = sb("cmb", [P, 2, NT])
        dtab = sb("dtab", [P, 2, 8])
        i16 = sb("i16", [P, GS])
        dskip = sb("dskip", [P, 2, 8, GS])
        sloti = sb("sloti", [P, 2, NT], U32)
        cmax = sb("cmax", [P, 1])
        cmaxi = sb("cmaxi", [P, 1], I32)
        counts = sb("counts", [P, NE], I32)
        slots = sb("slots", [P, NE, ROUNDS], U32)
        sidx = sb("sidx", [P, 1], U32)
        pool_tick = sb("pool_tick", [1, 2])

        tab = tmat[:, :, :].rearrange("p g n -> p (g n)").rearrange("p (n g) -> p n g", g=DG)
        gate_rows = tmat[:, :, :].rearrange("p g n -> p (g n)").rearrange("p (a n) -> p a n", a=2)
        b_keep = tmat[:, :, :].rearrange("p g n -> p (g n)").rearrange("p (r g h) -> p r g h", r=2, h=GS)
        fins = scan_t[:, :, :, :].rearrange("p a b n -> p (a b n)")[0:2 * GP, 0:2 * P].rearrange(
            "p (d n) -> p d n", d=2)

        row_pick = ring[:, 11, 0:8 * P].rearrange("p (j c n) -> p j c n", j=4, c=2)
        u_c = ring[:, 0:2, :].rearrange("p a b -> p (a b)").rearrange("p (g i h) -> p g i h", i=L, h=GS)
        y_b = ring[:, 0:2, :].rearrange("p a b -> p (a b)")[:, 0:KT * 4 * CX].rearrange(
            "p (k b c) -> p k b c", k=KT, b=4)
        pick = ring[:, 1, UNIT - L * 32:UNIT].rearrange("p (t n) -> p t n", t=L)
        w_pow = ring[:, 2:4, :].rearrange("p a (g k h) -> p a g k h", k=L, h=GS)
        uT = ring[:, 2:4, :].rearrange("p a b -> p (a b)")[:, 0:GP * CX].rearrange("p (g c) -> p g c", c=CX)
        yT = ring[:, 2:4, :].rearrange("p a b -> p (a b)")[:, 0:KT * T].rearrange("p (k t) -> p k t", k=KT)
        kpad = ring[:, 7, 0:16 * 112].rearrange("p (a q w) -> p a q w", a=2, q=8)
        win = ring[:, 4:8, :].rearrange("p a b -> p (a b)").rearrange("p (k n) -> p k n", k=KT)
        pads = ring[:, 4:12, :].rearrange("p a b -> p (a b)").rearrange("p (n j) -> p n j", j=P)
        pt = [pads[:, (1 - d) * 2 * GP:(2 - d) * 2 * GP, :].rearrange("p (g r) j -> p g r j", r=2) for d in range(2)]
        v_pad = pads.rearrange("p (g d r) j -> p g d r j", d=2, r=2)

        S = sreg[:, :].rearrange("p (d c r g) -> p d c r g", d=2, c=SLOTS, r=2)
        off = [0]

        def cut(region, n):
            a = region[:, off[0]:off[0] + n]
            off[0] += n
            return a
        bs3 = cut(sreg, 3 * DG * GS).rearrange("p (r g h) -> p r g h", r=3, g=DG)
        cs3 = cut(sreg, 3 * DG * GS).rearrange("p (r g h) -> p r g h", r=3, g=DG)
        t2 = cut(sreg, GP * NP_V * GS)
        hT = cut(sreg, KT * T).rearrange("p (k t) -> p k t", k=KT)
        off[0] = 0
        bnat = cut(vreg, UNIT)
        cnat = cut(vreg, UNIT)
        lnat = cut(vreg, P)
        hnat = cut(vreg, P)
        dtnat = cut(vreg, 2)
        dtexp = cut(vreg, P)
        rows = cut(vreg, P)
        scr = cut(vreg, D)
        off[0] = 2 * DG * NP_V * GS - NT * D
        x_sb = cut(vreg, NT * D).rearrange("p (t n) -> p t n", t=NT)
        V = vreg[:, :].rearrange("p (g r k h) -> p g r k h", r=2, k=NP_V, h=GS)

        off[0] = 0
        mod2 = cut(sreg, 4 * D).rearrange("p (a r n) -> p a r n", a=2, r=2)
        x1 = cut(sreg, NT * D).rearrange("p (t n) -> p t n", t=NT)
        h2 = cut(sreg, NT * D).rearrange("p (t n) -> p t n", t=NT)
        rw = cut(sreg, KT * NE).rearrange("p (k e) -> p k e", k=KT)
        rb = cut(sreg, NE)
        route = cut(sreg, 24 * NT * NE).rearrange("p (a t e) -> p a t e", a=24, t=NT)
        earlier = cut(sreg, (NT + 1) * NE)
        e_slot = cut(sreg, NT * NE).rearrange("p (t e) -> p t e", t=NT)
        rank = cut(sreg, NT * NE).rearrange("p (t e) -> p t e", t=NT)
        grank = cut(sreg, NT * NGRP).rearrange("p (t e) -> p t e", t=NT)
        tokv = cut(sreg, 2 * NT).bitcast(I32).rearrange("p (k t) -> p k t", k=2)
        listi = cut(sreg, NE * T // P).bitcast(I32)
        iotas = cut(sreg, NT * NE).bitcast(I32).rearrange("p (t e) -> p t e", t=NT)
        tri = cut(sreg, 2 * P).rearrange("p (a n) -> p a n", a=2)
        assert off[0] <= 2 * SLOTS * DG
        off[0] = 0
        onehot = cut(vreg, NT * CAP).rearrange("p (t n) -> p t n", t=NT)
        slot_no = cut(vreg, CAP)
        slot_noi = cut(vreg, CAP).bitcast(I32)
        posm = cut(vreg, NT * NE).rearrange("p (t e) -> p t e", t=NT)
        xgT = cut(vreg, KT * CAP).rearrange("p (k t) -> p k t", k=KT)
        sg = cut(vreg, TT * 256).rearrange("p (t n) -> p t n", t=TT)
        act_a = cut(vreg, TT * 256).rearrange("p (t n) -> p t n", t=TT)
        aT = cut(vreg, TT * 2 * P).rearrange("p (t c n) -> p t c n", t=TT, c=2)
        yrow = cut(vreg, D)
        h2T = cut(vreg, KT * T).rearrange("p (k t) -> p k t", k=KT)
        sig = cut(vreg, 512)
        prod = cut(vreg, 512)
        gfin = cut(vreg, D)
        assert off[0] <= 2 * DG * NP_V * GS
        yo = ring[:, 8:10, :].rearrange("p a b -> p (a b)")[:, 0:NT * D].rearrange("p (t n) -> p t n", t=NT)
        y2c = ring[:, 4:7, :].rearrange("p a b -> p (a b)").rearrange("p (k t n) -> p k t n", k=2, t=NT)
        m_out = h2

        ps = [ctx.enter_context(nc.psum_tensor(f"ps{i}", [P, 512], F32)) for i in range(8)]

        ld_cond, ld_x, ld_lam, ld_bc, ld_rows, ld_dtab = (sem(n) for n in (
            "ld_cond", "ld_x", "ld_lam", "ld_bc", "ld_rows", "ld_dtab"))
        ld_ada = [sem(f"ld_ada{i}") for i in range(len(ADA_SLOTS))]
        ld_late = [sem(f"ld_late{i}") for i in range(4)]
        ld_win, ld_tmat, ld_glu, ld_xagain, ld_route = (sem(n) for n in (
            "ld_win", "ld_tmat", "ld_glu", "ld_xagain", "ld_route"))
        ld_unit = [sem(f"ld_unit{u}") for u in range(NU)]
        pool_zero, pool_const, pool_late, pool_pick, pool_pad, act_vpad, act_k, pool_k, dve_keep = (sem(n) for n in (
            "pool_zero", "pool_const", "pool_late", "pool_pick", "pool_pad", "act_vpad",
            "act_k", "pool_k", "dve_keep"))
        pe_tr, pe_ada, pe_bc, pe_w, pe_mod, pe_hT, pe_u, pe_uT, pe_k, pe_p, pe_y, pe_fin, pe_yT = (
            sem(n) for n in ("pe_tr", "pe_ada", "pe_bc", "pe_w", "pe_mod", "pe_hT", "pe_u", "pe_uT",
                             "pe_k", "pe_p", "pe_y", "pe_fin", "pe_yT"))
        pe_glu, pe_h2T, pe_logit, pe_pos = (sem(n) for n in (
            "pe_glu", "pe_h2T", "pe_logit", "pe_pos"))
        act_silu, act_sq, act_rt, act_trig, act_bc, act_pt, act_hT, act_u, act_uT, act_p, act_gelu = (
            sem(n) for n in ("act_silu", "act_sq", "act_rt", "act_trig", "act_bc", "act_pt", "act_hT",
                             "act_u", "act_uT", "act_p", "act_gelu"))
        act_yT, act_sig, act_h2T, act_score, act_fin, act_h0 = (sem(n) for n in (
            "act_yT", "act_sig", "act_h2T", "act_score", "act_fin", "act_h0"))
        dve_done, act_mo = sem("dve_done"), sem("act_mo")
        st_rows, ld_g1, ld_g2, ld_mod2 = (sem(n) for n in ("st_rows", "ld_g1", "ld_g2", "ld_mod2"))
        ld_y2 = [sem(f"ld_y2_{t}") for t in range(NT)]
        dve_dt, dve_trig, dve_w, dve_v, dve_ms, dve_ada, dve_h, dve_uT, dve_p = (
            sem(n) for n in ("dve_dt", "dve_trig", "dve_w", "dve_v", "dve_ms",
                             "dve_ada", "dve_h", "dve_uT", "dve_p"))
        dve_scan, dve_x1, dve_h2, dve_mask, dve_slot, dve_cmax, dve_x2, dve_out = (sem(n) for n in (
            "dve_scan", "dve_x1", "dve_h2", "dve_mask", "dve_slot", "dve_cmax", "dve_x2", "dve_out"))
        st_list, st_out, st_scatter = (sem(n) for n in ("st_list", "st_out", "st_scatter"))
        unit_free, ld_idx, oh_ready, xt_ps, xt_ev, silu_done, prod_done, at_ps, at_ev, y_ev, y_sent = (
            sem(n) for n in ("unit_free", "ld_idx", "oh_ready", "xt_ps", "xt_ev", "silu_done", "prod_done",
                             "at_ps", "at_ev", "y_ev", "y_sent"))

        y_free, sidx_ready, dve_round = sem("y_free"), sem("sidx_ready"), sem("dve_round")
        ticks = [sem("send_tick"), y_free]

        flat_s = sreg[:, :]
        FS = 2 * SLOTS * DG

        def chunk_states(slot0, dslot, swap):
            first = slot0 * DG + (GP if swap else 0)
            return bass.AP(flat_s.tensor, flat_s.offset + first,
                           [[FS, P], [(SLOTS + dslot) * DG, 2], [-GP if swap else GP, 2], [1, GP]])

        def lam_rows(a):
            return a.rearrange("a d (g i) s -> (a d g) (i s)", i=2)

        block = ctx.enter_context(nc.Block())

        @block.sync
        def _(sp):
            def ada_piece(n):
                slot = n % len(ADA_SLOTS)
                if n >= len(ADA_SLOTS):
                    sp.wait_ge(pe_ada, n + 1 - len(ADA_SLOTS))
                sp.dma_start(ring[:, ADA_SLOTS[slot], :],
                             w_ada[0, n * P:(n + 1) * P, 0:UNIT]).then_inc(ld_ada[slot], 16)
            sp.dma_start(lnat[0:DG, :], lam_rows(lam_re)).then_inc(ld_lam, 16)
            sp.dma_start(lnat[DG:P, :], lam_rows(lam_im)).then_inc(ld_lam, 16)
            sp.dma_start(hnat[0:DG, :], state_re[0].rearrange("a d (g i) s -> (a d g) (i s)", i=2)).then_inc(ld_lam, 16)
            sp.dma_start(hnat[DG:P, :], state_im[0].rearrange("a d (g i) s -> (a d g) (i s)", i=2)).then_inc(ld_lam, 16)
            for n in range(len(ADA_SLOTS)):
                ada_piece(n)
            for t in range(NT):
                src = x_prompt[0] if t == 0 else x_sample[0, (t - 1) * P:t * P, :]
                sp.dma_start(x_sb[:, t, :], src).then_inc(ld_x, 16)
            for n in range(len(ADA_SLOTS), KT):
                ada_piece(n)
            sp.wait_ge(ld_ada[6], 16)
            for k in range(KT):
                sp.dma_start(win[:, k, :], w_in[0, k * P:(k + 1) * P, :]).then_inc(ld_win, 16)
            def load_T():
                sp.wait_ge(pool_k, 1)
                for i in range(2):
                    for j in range(L):
                        for q in range(4):
                            dst = tmat[64 * i + 16 * j:64 * i + 16 * j + 16, q:GP:4, :]
                            sp.dma_start(dst, kpad[32 * q:32 * q + 16, i, :, (3 - j) * GS:(7 - j) * GS]
                                         ).then_inc(ld_tmat, 16)

            sp.wait_ge(pe_p, 16)
            for n in range(KT, 3 * KT):
                b, k = divmod(n, KT)
                if n == KT + 8:
                    load_T()
                if n >= KT + 4:
                    sp.wait_ge(pe_ada, n - 3)
                sp.dma_start(ring[:, 8 + n % 4, :],
                             w_ada[0, k * P:(k + 1) * P, b * UNIT:(b + 1) * UNIT]).then_inc(ld_late[n % 4], 16)
            def load_rows(dst, cond, b, j, done):
                sp.dma_start(dst, rows_d[cond:cond + 1, b - 1, j:j + 2, :].rearrange("a j n -> a (j n)"
                                                                                    ).broadcast_to((P, D))
                             ).then_inc(done, 16)
            sp.wait_ge(dve_ada, 3)
            for cond in range(2):
                sp.dma_start(rows_d[cond].rearrange("b j n -> j b n"), ada[cond:P:32, 1:3, :]
                             ).then_inc(st_rows, 16)
            sp.wait_ge(st_rows, 32)
            for k in range(KT):
                sp.wait_ge(pe_y, k + 1)
                sp.dma_start(ring[:, 4 + k, :], w_glu[0, k * P:(k + 1) * P, :]).then_inc(ld_glu, 16)
            for cond in range(2):
                load_rows(gate_rows[:, cond, :], cond, 1, 0, ld_g1)
            sp.wait_ge(pe_fin, 2)
            for t in range(NT):
                src = x_prompt[0] if t == 0 else x_sample[0, (t - 1) * P:t * P, :]
                sp.dma_start(x1[:, t, :], src).then_inc(ld_xagain, 16)
            for cond in range(2):
                load_rows(mod2[:, cond, 0, :], cond, 2, 0, ld_mod2)
                load_rows(mod2[:, cond, 1, :], cond, 1, 2, ld_mod2)
            sp.dma_start(rw, router_w.rearrange("(k p) e -> p k e", p=P)).then_inc(ld_route, 16)
            sp.dma_start(rb, router_b.rearrange("(a e) -> a e", a=1).broadcast_to((P, NE))).then_inc(ld_route, 16)
            sp.dma_start(gfin, norm_final.rearrange("(a e) -> a e", a=1).broadcast_to((P, D))).then_inc(ld_route, 16)
            for r, dst in ((0, new_re), (1, new_im)):
                for d in range(2):
                    if r == 0:
                        sp.wait_ge(act_fin, d + 1)
                    sp.dma_start(dst[0, 0, d].rearrange("(g i) s -> g (i s)", i=2),
                                 fins[r * GP:(r + 1) * GP, d, :]).then_inc(st_out, 16)

            def load_unit(u, e):
                if u < KT:
                    for h, w in enumerate((w_gate, w_up)):
                        sp.dma_start(ring[:, u, h * D:(h + 1) * D],
                                     w[0, bass.ds(e, 1), u * P:(u + 1) * P, :].rearrange("a p n -> (a p) n")
                                     ).then_inc(ld_unit[u], 16)
                else:
                    for h in range(2):
                        k = 2 * (u - KT) + h
                        sp.dma_start(ring[:, u, h * D:(h + 1) * D],
                                     w_down[0, bass.ds(e, 1), k * P:(k + 1) * P, :].rearrange("a p n -> (a p) n")
                                     ).then_inc(ld_unit[u], 16)

            sp.wait_ge(pe_yT, 8)
            for u in range(2):
                load_unit(u, 0)
            sp.wait_ge(pe_glu, 12)
            for u in range(2, NU):
                load_unit(u, 0)
            sp.wait_ge(dve_x1, 6)
            for cond in range(2):
                load_rows(gate_rows[:, cond, :], cond, 2, 2, ld_g2)
            with sp.Fori(1, NE) as e:
                for u in range(NU):
                    sp.wait_ge(unit_free, e * NU + (u + 1 - NU))
                    load_unit(u, e)
            sp.wait_ge(y_sent, 16 * NE)
            v = sp.value_load(cmaxi[0:1, 0:1], min_val=0, max_val=T)
            with sp.If(v > CAP):
                with sp.Fori(1, ROUNDS) as r:
                    with sp.Fori(0, NE) as e:
                        for u in range(NU):
                            sp.wait_ge(unit_free, r * (NE * NU) + e * NU + (u + 1 - NU))
                            load_unit(u, e)
                sp.wait_ge(y_sent, 16 * NE * ROUNDS)
            sp.nop()
            for t in range(NT):
                for k in range(2):
                    sp.dma_start(y2c[:, k, t, :], y2_d[k * T + t * P:k * T + (t + 1) * P, :]).then_inc(ld_y2[t], 16)
            for t in range(NT):
                sp.wait_ge(dve_out, t + 1)
                dst = y_prompt[0] if t == 0 else y_sample[0, (t - 1) * P:t * P, :]
                sp.dma_start(dst, yo[:, t, :]).then_inc(st_out, 16)
            sp.wait_ge(st_out, 16 * (4 + NT))
            sp.wait_ge(st_list, 16)
            sp.wait_ge(st_scatter, 16 * 2 * NT)

        @block.gpsimd
        def _(pool):
            n = [0]

            def after(ins):
                n[0] += 1
                ins.then_inc(pool_const, 1)
                pool.wait_ge(pool_const, n[0])
            pool.memset(ada[:], 0.0).then_inc(pool_zero, 1)
            pool.memset(gains[:], 0.0).then_inc(pool_zero, 1)
            pool.memset(dtab[:], 0.0).then_inc(pool_zero, 1)
            pool.memset(silu_c[:], 0.0).then_inc(pool_zero, 1)
            after(pool.memset(ident[:], 0.0))
            after(pool.affine_select(out=ident[:], in_=ident[:], compare_op=ALU.not_equal, fill=1.0, base=0,
                                     pattern=[[-1, P]], channel_multiplier=1))
            after(pool.memset(row_pick, 0.0))
            after(pool.affine_select(out=row_pick, in_=row_pick, compare_op=ALU.not_equal, fill=1.0, base=0,
                                     pattern=[[-32, 4], [-1, 2], [0, P]], channel_multiplier=1))
            assert n[0] == 4

            def zero_blocks(n0, n1, before):
                for i in range(2):
                    pool.memset(pads[64 * i:64 * i + 64, n0:n1, 64 * (1 - i):64 * (2 - i)], 0.0).then_inc(pool_pad, 1)
                    pool.wait_ge(pool_pad, before + i + 1)
            pool.wait_ge(pe_ada, KT)
            pool.wait_ge(pe_mod, 2)
            zero_blocks(2 * GP, 4 * GP, 0)
            pool.wait_ge(pe_u, 8)
            zero_blocks(0, 2 * GP, 2)
            pool.wait_ge(pe_uT, 8)
            for i in range(2):
                pool.tensor_copy(pick[:, :, 16 * i:16 * i + 16],
                                 ident[:, 64 * i:64 * i + 64].rearrange("p (t h) -> p t h", h=GS)
                                 ).then_inc(pool_pick, 1)
                pool.wait_ge(pool_pick, i + 1)
            pool.wait_ge(act_k, 4)
            pool.wait_ge(dve_keep, 1)
            pool.tensor_tensor(kpad[:, :, :, 48:64], kpad[:, :, :, 48:64], dskip[:, :, :, :], ALU.add
                               ).then_inc(pool_k, 1)
            pool.wait_ge(pool_k, 1)
            pool.wait_ge(ld_tmat, 16 * 32)
            zero_blocks(3 * UNIT // P, 4 * UNIT // P, 4)
            pool.wait_ge(pe_ada, 3 * KT)
            zero_blocks(2 * GP, 4 * GP, 6)
            pool.wait_ge(pe_y, 8)
            pool.wait_ge(pe_fin, 2)
            n[0] = 0

            def late(ins):
                n[0] += 1
                ins.then_inc(pool_late, 1)
                pool.wait_ge(pool_late, n[0])
            late(pool.memset(tri, 1.0))
            late(pool.affine_select(out=tri[:, 0, :], in_=tri[:, 0, :], compare_op=ALU.is_gt, fill=0.0, base=0,
                                    pattern=[[1, P]], channel_multiplier=-1))
            late(pool.iota(iotas, pattern=[[0, NT], [ROUNDS, NE]], base=0, channel_multiplier=0))
            late(pool.tensor_copy(e_slot, iotas))
            late(pool.iota(iotas, pattern=[[0, NT], [-1, NE]], base=NE, channel_multiplier=0))
            late(pool.tensor_copy(rank, iotas))
            late(pool.iota(iotas[:, :, 0:NGRP], pattern=[[0, NT], [-1, NGRP]], base=NGRP, channel_multiplier=0))
            late(pool.tensor_copy(grank, iotas[:, :, 0:NGRP]))
            for k in range(2):
                late(pool.iota(tokv[:, k, :], pattern=[[P, NT]], base=k * T, channel_multiplier=1))
            late(pool.iota(slot_noi, pattern=[[1, CAP]], base=0, channel_multiplier=0))
            late(pool.tensor_copy(slot_no, slot_noi))
            late(pool.memset(listi, OOB))
            assert n[0] == 13
            pool.dma_start(list_d.rearrange("(p a) v -> p (a v)", p=P), listi).then_inc(st_list, 16)
            pool.wait_ge(st_list, 16)
            pool.wait_ge(dve_slot, 1)
            for k in range(2):
                for t in range(NT):
                    pool.indirect_dma_start(out=list_d, out_offset=bass.IndirectOffsetOnAxis(
                        ap=sloti[:, k, t:t + 1], axis=0), in_=tokv[:, k, t:t + 1], in_offset=None,
                        bounds_check=NE * T - 1, oob_is_err=False).then_inc(st_scatter, 16)
            pool.wait_ge(st_scatter, 16 * 2 * NT)
            pool.dma_start(slots[0:CAP, :, :].rearrange("p e r -> p (e r)"),
                           list_d.rearrange("(p n) v -> p (n v)", p=CAP).bitcast(U32)).then_inc(ld_idx, 16)
            pool.wait_ge(ld_idx, 16)
            pool.wait_ge(dve_cmax, 1)
            last_row = pool.to_reg(2 * T - 1)

            def carry_waits(which, before):
                pool.wait_ge(ticks[which], before + 1)
                pool.tensor_tensor(pool_tick[:, which:which + 1], ident[0:1, 0:1], ident[0:1, 0:1], ALU.mult
                                   ).then_inc(ticks[which], 1)

            def send(e, rnd, it, count=None):
                pool.tensor_copy(sidx[0:CAP, :], slots[0:CAP, bass.ds(e, 1), bass.ds(rnd, 1)].rearrange(
                    "p a b -> p (a b)")).then_inc(sidx_ready, 1)
                pool.wait_ge(sidx_ready, it + 1)
                pool.wait_ge(y_ev, it * 12 + 24)
                carry_waits(0, it)

                def rows_out(n):
                    pool.indirect_dma_start(out=y2_d, out_offset=bass.IndirectOffsetOnAxis(
                        ap=sidx[0:n, 0:1], axis=0), in_=yrow[0:n, :], in_offset=None,
                        bounds_check=last_row, oob_is_err=False).then_inc(y_sent, 16)
                if count is None:
                    rows_out(CAP)
                else:
                    with pool.If(count > 64):
                        rows_out(CAP)
                    with pool.If(count <= 64):
                        rows_out(64)
                pool.wait_ge(y_sent, it * 16 + 16)
                carry_waits(1, it)

            for which in range(2):
                pool.sem_inc(ticks[which], 1)
            with pool.Fori(0, NE) as e:
                send(e, 0, e, pool.value_load(counts[0:1, bass.ds(e, 1)], min_val=0, max_val=T))
            v = pool.value_load(cmaxi[0:1, 0:1], min_val=0, max_val=T)
            with pool.If(v > CAP):
                with pool.Fori(1, ROUNDS) as r:
                    with pool.Fori(0, NE) as e:
                        send(e, r, r * NE + e)
            pool.nop()

        @block.scalar
        def _(act):
            act.dma_start(dtnat[0:DG, :], log_dt.rearrange("a d (g i) -> (a d g) i", i=2)).then_inc(ld_lam, 16)
            act.dma_start(rows[0:8, :], c_ctx.rearrange("(k p) -> k p", p=P)).then_inc(ld_cond, 16)
            act.dma_start(rows[8:16, :], c[0].rearrange("(k p) -> k p", p=P)).then_inc(ld_cond, 16)
            act.wait_ge(pool_zero, 4)
            for cond in range(2):
                act.dma_start(ada[cond:P:32, :, :], b_ada.rearrange("o (b j n) -> j (o b) n", b=3, n=512)
                              ).then_inc(ld_rows, 16)
                for j, norm in ((0, norm_ffn), (2, norm_mix)):
                    act.dma_start(gains[32 * j + cond:32 * j + 64:32, :], norm.rearrange("o (j n) -> (o j) n", j=2)
                                  ).then_inc(ld_rows, 16)
            act.wait_ge(pe_tr, 1)
            act.activation(silu_c[:, :, 0:2].rearrange("p k c -> p c k"),
                           ps[3][:, 0:16].rearrange("p (c k) -> p c k", c=2), ACT.Silu).then_inc(act_silu, 1)
            act.wait_ge(pe_tr, 2)
            act.activation(h0[:], ps[4][:, 0:P], ACT.Copy).then_inc(act_h0, 1)
            act.wait_ge(dve_trig, 1)
            act.activation(tab[:, 7, :], tab[:, 5, :], ACT.Sin).then_inc(act_trig, 1)
            act.activation(tab[:, 8, :], tab[:, 6, :], ACT.Sin).then_inc(act_trig, 1)
            act.wait_ge(ld_ada[3], 16)
            for r, (b, cc) in enumerate(((b_re, c_re), (b_im, c_im))):
                act.dma_start(bnat[r * DG:(r + 1) * DG, :], b.rearrange("a d (g i) s h -> (a d g) (i s h)", i=2)
                              ).then_inc(ld_bc, 16)
                for i in range(2):
                    act.dma_start(cnat[r * DG:(r + 1) * DG, :].rearrange("p (h i s) -> p i h s", h=GS, i=2)[:, i],
                                  cc.rearrange("a d (g i) h s -> i (a d g) h s", i=2)[i]).then_inc(ld_bc, 16)
            for q in range(4):
                for i in range(2):
                    act.dma_start(dtab[32 * q:32 * q + 16, i, :], ssm_d[0].rearrange(
                        "(m q i h) -> q i h m", m=8, q=4, i=2)[q, i], allow_slow_non_contiguous=True
                        ).then_inc(ld_dtab, 16)

            act.wait_ge(ld_x, 16 * NT)
            for t in range(NT):
                if t:
                    act.wait_ge(act_sq, t)
                act.activation(scr, x_sb[:, t, :], ACT.Square, accum_out=stat[:, t:t + 1]).then_inc(act_sq, 1)
            act.wait_ge(dve_ms, 1)
            act.activation(stat[:, 4:4 + NT], stat[:, 4:4 + NT], ACT.Sqrt).then_inc(act_rt, 1)
            braw = t2[:, 0:2 * DG * GS].rearrange("p (r g h) -> p r g h", r=2, h=GS)
            for m in range(4):
                act.wait_ge(pe_bc, m + 1)
                act.activation(braw[:, :, :, 4 * m:4 * m + 4],
                               ps[2 + m % 2][:, :].rearrange("p (h r g) -> p r g h", h=4, r=2), ACT.Copy
                               ).then_inc(act_bc, 1)

            for m in range(2 * NT):
                t, k0 = m // 2, 4 * (m % 2)
                act.wait_ge(pe_hT, m + 1)
                act.activation(hT[:, k0:k0 + 4, t * P:(t + 1) * P],
                               ps[m % 2][:, :].rearrange("p (k n) -> p k n", k=4), ACT.Copy).then_inc(act_hT, 1)

            def store_W(batch):
                d, r = divmod(batch, 2)
                act.wait_ge(pool_pad, 2)
                for w in range(4 * batch, 4 * batch + 4):
                    act.wait_ge(pe_w, w + 1)
                    g0 = (w % 4) * 8
                    for i in range(2):
                        a = slice(64 * i, 64 * i + 64)
                        act.activation(pt[d][a, g0:g0 + 8, r, a],
                                       ps[2 * (w % 2) + i][a, :].rearrange("p (g s) -> p g s", s=NS), ACT.Copy
                                       ).then_inc(act_pt, 1)
            for m in range(8):
                i, half = m // 2, m % 2
                act.wait_ge(pe_u, m + 1)
                act.activation(u_c[0:C, 32 * half:32 * half + 32, i, :],
                               ps[4 + m % 2][0:C, :].rearrange("p (g h) -> p g h", h=GS), ACT.Copy
                               ).then_inc(act_u, 1)
                if m == 0:
                    for n in range(4):
                        act.wait_ge(pe_bc, 5 + n)
                        h = slice(4 * n, 4 * n + 4)
                        src = ps[2 + n % 2][:, :].rearrange("p (h r g) -> p r g h", h=4, r=2)
                        act.activation(cs3[:, 0, :, h], src[:, 0], ACT.Copy)
                        act.activation(cs3[:, 1, :, h], src[:, 1], ACT.Copy, scale=-1.0)
                        act.activation(cs3[:, 2, :, h], src[:, 0], ACT.Copy, scale=-1.0).then_inc(act_bc, 1)
                if m in (1, 2):
                    store_W(m - 1)
            store_W(2)
            store_W(3)
            for m in range(0, 8, 2):
                act.wait_ge(pe_uT, m + 1)
                src = ps[4 + m % 4][:, 0:4 * C].rearrange("p (g c) -> p g c", c=C)
                act.activation(uT[:, 4 * m:4 * m + 4, 0:CC], src[:, :, 0:CC], ACT.Copy)
                act.activation(uT[:, 4 * m:4 * m + 4, CC + 1:CX], src[:, :, CC:C], ACT.Copy).then_inc(act_uT, 1)
            for m in range(0, 32, 2):
                d, g0 = m // 16, 2 * (m % 16)
                act.wait_ge(pe_p, m + 1)
                act.activation(S[:, d, 1 - d:1 - d + CX, :, g0:g0 + 2].rearrange("p c r g -> p g r c"),
                               ps[m % 8][:, 0:4 * CX].rearrange("p (g r c) -> p g r c", g=2, r=2),
                               ACT.Copy).then_inc(act_p, 1)
            for m in range(4):
                i, mq = m // 2, m % 2
                act.wait_ge(pe_k, m + 1)
                act.activation(kpad[:, i, 4 * mq:4 * mq + 4, :], ps[m][:, 0:448].rearrange("p (q w) -> p q w", w=112),
                               ACT.Copy).then_inc(act_k, 1)
            for half in range(2):
                if half == 0:
                    act.wait_ge(ld_tmat, 16 * 32)
                else:
                    act.wait_ge(pe_ada, 3 * KT)
                for i in range(2):
                    a = slice(64 * i, 64 * i + 64)
                    for d in range(2):
                        g = slice(16 * half, 16 * half + 16)
                        act.activation(v_pad[a, g, d, :, a],
                                       V[a, d * GP + 16 * half:d * GP + 16 * half + 16, :, 1 - d:5 - d, :].rearrange(
                                           "p g r k h -> p g r (k h)"), ACT.Copy).then_inc(act_vpad, 1)
            def store_yT(k):
                act.wait_ge(pe_yT, k + 1)
                src = ps[k][:, 0:L * CX].rearrange("p (i c) -> p c i", i=L)
                dst = yT[:, k, :].rearrange("p (c i) -> p c i", i=L)
                act.activation(dst[:, 0:CC, :], src[:, 0:CC, :], ACT.Copy)
                act.activation(dst[:, CC:C, :], src[:, CC + 1:CX, :], ACT.Copy).then_inc(act_yT, 1)
            for k in range(KT):
                act.wait_ge(pe_y, k + 1)
                act.activation(y_b[:, k, :, :], ps[k][:, 0:4 * CX].rearrange("p (b c) -> p b c", b=4),
                               ACT.Gelu_apprx_tanh).then_inc(act_gelu, 1)
                if k == KT - 1:
                    for m in range(KT):
                        store_yT(m)
            for d in range(2):
                act.wait_ge(pe_fin, d + 1)
                act.activation(fins[:, d, :], ps[4 + d][0:2 * GP, 0:P], ACT.Copy).then_inc(act_fin, 1)

            def store_h2T(t):
                for m in (2 * t, 2 * t + 1):
                    k0 = 4 * (m % 2)
                    act.wait_ge(pe_h2T, m + 1)
                    act.activation(h2T[:, k0:k0 + 4, t * P:(t + 1) * P],
                                   ps[4 + m % 2][:, :].rearrange("p (k n) -> p k n", k=4), ACT.Copy
                                   ).then_inc(act_h2T, 1)
            for t in range(NT):
                for m in (2 * t, 2 * t + 1):
                    act.wait_ge(pe_glu, 2 * m + 2)
                    if m:
                        act.wait_ge(dve_x1, m)
                    act.activation(sig, ps[2 * (m % 2) + 1][:, :], ACT.Sigmoid).then_inc(act_sig, 1)
                    if m == 4:
                        store_h2T(1)
                act.wait_ge(dve_x1, 2 * t + 2)
                if t:
                    act.wait_ge(act_sq, NT + t)
                act.activation(yrow, x1[:, t, :], ACT.Square, accum_out=stat[:, t:t + 1]).then_inc(act_sq, 1)
                act.wait_ge(dve_ms, 2 + t)
                act.activation(stat[:, 4 + t:5 + t], stat[:, 4 + t:5 + t], ACT.Sqrt).then_inc(act_rt, 1)
                if t == 1:
                    store_h2T(0)
            store_h2T(2)
            act.wait_ge(pe_logit, NT)
            act.activation(route[:, 0], ps[6][:, 0:NT * NE].rearrange("p (t e) -> p t e", t=NT), ACT.Sigmoid
                           ).then_inc(act_score, 1)

            def expert(it):
                for t in range(TT):
                    act.wait_ge(unit_free, it * NU + KT)
                    act.activation(sg[:, t, :], ps[t][:, 0:256], ACT.Silu).then_inc(silu_done, 1)
                act.wait_ge(at_ps, it * TT + 2)
                act.activation(aT[:, 0:2, :, :], ps[7][:, :].rearrange("p (t c n) -> p t c n", t=2, c=2), ACT.Copy
                               ).then_inc(at_ev, 1)
                act.wait_ge(at_ps, it * TT + 3)
                act.activation(aT[:, 2, :, :], ps[4][:, 256:512].rearrange("p (c n) -> p c n", c=2), ACT.Copy
                               ).then_inc(at_ev, 1)
                act.wait_ge(unit_free, it * NU + NU)
                act.wait_ge(y_free, it + 1)
                for t in range(TT):
                    for j in range(2):
                        src = ps[3 + t // 2][32 * j:32 * j + 32, 256 * (t % 2):256 * (t % 2) + 256]
                        act.activation(yrow[32 * t:32 * t + 32, 256 * j:256 * j + 256], src, ACT.Copy
                                       ).then_inc(y_ev, 1)
            act.wait_ge(dve_cmax, 1)
            with act.Fori(0, NE) as e:
                expert(e)
            v = act.value_load(cmaxi[0:1, 0:1], min_val=0, max_val=T)
            with act.If(v > CAP):
                with act.Fori(1, ROUNDS) as r:
                    with act.Fori(0, NE) as e:
                        expert(r * NE + e)
            act.nop()

            def first_expert(t):
                act.wait_ge(ld_y2[t], 32)
                act.activation(m_out[:, t, :], y2c[:, 0, t, :], ACT.Copy, scale=cmb[:, 0, t:t + 1]).then_inc(act_mo, 1)
            first_expert(0)
            first_expert(1)
            for t in range(NT):
                act.wait_ge(dve_x2, t + 1)
                act.activation(m_out[:, t, :], x1[:, t, :], ACT.Square, accum_out=stat[:, t:t + 1]).then_inc(act_sq, 1)
                act.wait_ge(dve_ms, 2 + NT + t)
                act.activation(stat[:, 4 + t:5 + t], stat[:, 4 + t:5 + t], ACT.Sqrt).then_inc(act_rt, 1)
                if t == 0:
                    first_expert(2)

        @block.tensor
        def _(pe):
            def ada_piece(n):
                b, k = divmod(n, KT)
                slot = n % len(ADA_SLOTS)
                if b == 0:
                    pe.wait_ge(ld_ada[slot], 16 * (n // len(ADA_SLOTS) + 1))
                else:
                    pe.wait_ge(ld_late[n % 4], 16 * (n // 4 - 1))
                src = ring[:, ADA_SLOTS[slot] if b == 0 else 8 + n % 4, :]
                for j in range(4):
                    last = pe.matmul(ps[ADA_BANK[b]][32 * j:32 * j + 32, :], silu_c[:, k, :],
                                     src[:, j * 512:(j + 1) * 512], start=(k == 0), stop=(k == KT - 1))
                last.then_inc(pe_ada, 1)

            def spread(bank, b, j, cond):
                return pe.matmul(bank[:, :], row_pick[:, j, cond, :], ada[:, b, :], start=True, stop=True)

            pe.wait_ge(pool_const, 4)
            pe.wait_ge(ld_cond, 32)
            pe.transpose(ps[3][:, 0:16], rows[0:16, :], ident[0:16, 0:16]).then_inc(pe_tr, 1)
            pe.wait_ge(ld_lam, 16 * 5)
            pe.wait_ge(dve_dt, 1)
            pe.transpose(ps[4][:, 0:P], hnat, ident[:])
            pe.transpose(ps[7][:, 0:P], lnat, ident[:])
            pe.transpose(ps[7][:, P:P + DG], dtexp[0:DG, :], ident[0:DG, 0:DG]).then_inc(pe_tr, 1)
            pe.wait_ge(act_silu, 1)
            for n in range(KT):
                ada_piece(n)
            pe.wait_ge(dve_ada, 1)
            pe.wait_ge(act_h0, 1)
            for cond in range(2):
                for b in range(2):
                    spread(ps[4 * cond + b], 0, 2 + b, cond)
                    last = spread(ps[4 * cond + 2 + b], 0, b, cond)
                last.then_inc(pe_mod, 1)

            def transpose_bc(m):
                nat = bnat if m < 4 else cnat
                if m >= 2:
                    pe.wait_ge(act_bc, m - 1)
                for h in range(4 * (m % 4), 4 * (m % 4) + 4):
                    if m < 4:
                        src = nat.rearrange("p (n h) -> p n h", h=GS)[:, :, h]
                    else:
                        src = nat[:, h * P:(h + 1) * P]
                    last = pe.transpose(ps[2 + m % 2][:, (h % 4) * P:(h % 4 + 1) * P], src, ident[:])
                last.then_inc(pe_bc, 1)
            pe.wait_ge(ld_bc, 16 * 6)
            pe.wait_ge(dve_h, 1)
            for m in range(4):
                transpose_bc(m)
            for m in range(2 * NT):
                t, k0 = m // 2, 4 * (m % 2)
                pe.wait_ge(dve_h, t + 1)
                if m >= 2:
                    pe.wait_ge(act_hT, m - 1)
                for k in range(k0, k0 + 4):
                    last = pe.transpose(ps[m % 2][:, (k % 4) * P:(k % 4 + 1) * P],
                                        x_sb[:, t, k * P:(k + 1) * P], ident[:])
                last.then_inc(pe_hT, 1)
            pe.wait_ge(act_hT, 6)
            pe.wait_ge(ld_win, 16 * KT)

            def transpose_W(batch):
                pe.wait_ge(dve_w, batch + 1)
                for w in range(4 * batch, 4 * batch + 4):
                    if w >= 2:
                        pe.wait_ge(act_pt, 2 * (w - 1))
                    for g in range(8 * (w % 4), 8 * (w % 4) + 8):
                        for i in range(2):
                            a = slice(64 * i, 64 * i + 64)
                            last = pe.matmul(ps[2 * (w % 2) + i][a, (g % 8) * NS:(g % 8 + 1) * NS],
                                             w_pow[:, batch % 2, g, :, :].rearrange("p k h -> p (k h)"),
                                             ident[:, a], start=True, stop=True)
                    last.then_inc(pe_w, 1)
            for m in range(8):
                i, half = m // 2, m % 2
                if m >= 2:
                    pe.wait_ge(act_u, m - 1)
                for k in range(KT):
                    last = pe.matmul(ps[4 + m % 2][0:C, :], hT[:, k, i:T:L], win[:, k, half * 512:(half + 1) * 512],
                                     start=(k == 0), stop=(k == KT - 1))
                last.then_inc(pe_u, 1)
                if m == 0:
                    for n in range(4, 8):
                        transpose_bc(n)
                    pe.wait_ge(act_bc, 8)
                if m in (1, 2):
                    transpose_W(m - 1)
            transpose_W(2)
            transpose_W(3)
            pe.wait_ge(act_u, 8)
            for m in range(8):
                if m >= 4:
                    pe.wait_ge(act_uT if m % 2 == 0 else dve_uT, (m - 4) // 2 + (1 if m % 2 == 0 else 2))
                for g in range(4 * m, 4 * m + 4):
                    src = u_c[0:C, 2 * g:2 * g + 2, :, :].rearrange("p i j h -> p (i j h)")
                    last = pe.transpose(ps[4 + m % 4][:, (g % 4) * C:(g % 4 + 1) * C], src, ident[0:C, 0:C])
                last.then_inc(pe_uT, 1)
            pe.wait_ge(act_uT, 4)
            pe.wait_ge(dve_uT, 5)
            pe.wait_ge(act_pt, 32)
            pe.wait_ge(dve_keep, 1)
            for m in range(32):
                d, g0 = m // 16, 2 * (m % 16)
                if m == 16:
                    pe.wait_ge(pool_pad, 4)
                if m >= 8:
                    pe.wait_ge(dve_p if m % 2 else act_p, (m - 8) // 2 + 1)
                for gi in range(2):
                    for r in range(2):
                        o = (2 * gi + r) * CX
                        last = pe.matmul(ps[m % 8][:, o:o + CX], pt[d][:, g0 + gi, r, :], uT[:, g0 + gi, :],
                                         start=True, stop=True)
                last.then_inc(pe_p, 1)
            pe.wait_ge(act_p, 16)
            pe.wait_ge(dve_p, 16)
            for i in range(2):
                for mq in range(2):
                    bank = ps[2 * i + mq]
                    for m4 in range(4):
                        for q in range(4):
                            g = 4 * (4 * mq + m4) + q
                            out = bank[32 * q:32 * q + 16, 112 * m4:112 * m4 + 112]
                            for d in range(2):
                                for r in range(2):
                                    lhs = b_keep[64 * i:64 * i + 64, r, d * GP + g, :]
                                    rhs = V[64 * i:64 * i + 64, d * GP + g, r, d:d + 4, :].rearrange("p k h -> p (k h)")
                                    last = pe.matmul(out[:, 48:112] if d == 0 else out[:, 0:64], lhs, rhs,
                                                     start=(m4 == 0 and d == 0 and r == 0), stop=True,
                                                     skip_group_check=True)
                    last.then_inc(pe_k, 1)
            def y_inside(k):
                for q in range(4):
                    for i in range(2):
                        a = slice(64 * i, 64 * i + 64)
                        pe.matmul(ps[k][a, q * CX:(q + 1) * CX], tmat[a, 4 * k + q, :], uT[a, 4 * k + q, :],
                                  start=(q == 0), stop=False, skip_group_check=True)

            def y_state(k):
                for q in range(4):
                    for d in range(2):
                        for r in range(2):
                            last = pe.matmul(ps[k][:, q * CX:(q + 1) * CX], v_pad[:, 4 * k + q, d, r, :],
                                             S[:, d, d:d + CX, r, 4 * k + q], start=False,
                                             stop=(d == 1 and r == 1), skip_group_check=True)
                last.then_inc(pe_y, 1)

            def y_channels(k):
                pe.wait_ge(act_gelu, k + 1)
                for t in range(L):
                    for q in range(4):
                        last = pe.matmul(ps[k][32 * q:32 * q + 32, t * CX:(t + 1) * CX], pick[:, t, :],
                                         y_b[:, k, q, :], start=True, stop=True)
                last.then_inc(pe_yT, 1)
            for n in range(KT, 3 * KT):
                ada_piece(n)
            pe.wait_ge(ld_tmat, 16 * 32)
            pe.wait_ge(act_k, 4)
            for k in range(6):
                y_inside(k)
            pe.wait_ge(dve_scan, 1)
            pe.wait_ge(act_vpad, 8)
            pe.wait_ge(pool_pad, 8)
            for k in range(6):
                y_state(k)
            pe.wait_ge(dve_ada, 3)
            for k in (6, 7):
                y_inside(k)
                y_state(k)
            pe.wait_ge(pool_pick, 2)
            for k in range(KT):
                y_channels(k)
            pe.wait_ge(act_yT, 6)
            for d in range(2):
                slot = CC if d == 0 else 0
                pe.transpose(ps[4 + d][0:2 * GP, 0:P], S[:, d, slot, :, :].rearrange("p r g -> p (r g)"),
                             ident[:]).then_inc(pe_fin, 1)
            pe.wait_ge(act_yT, 8)
            pe.wait_ge(act_fin, 2)
            pe.wait_ge(ld_glu, 16 * KT)

            def transpose_h2(t):
                pe.wait_ge(dve_h2, t + 1)
                for m in (2 * t, 2 * t + 1):
                    k0 = 4 * (m % 2)
                    if m >= 2:
                        pe.wait_ge(act_h2T, m - 1)
                    for k in range(k0, k0 + 4):
                        last = pe.transpose(ps[4 + m % 2][:, (k % 4) * P:(k % 4 + 1) * P],
                                            h2[:, t, k * P:(k + 1) * P], ident[:])
                    last.then_inc(pe_h2T, 1)

            def logits(t):
                if t == 0:
                    pe.wait_ge(ld_route, 48)
                pe.wait_ge(act_h2T, 2 * t + 2)
                for k in range(KT):
                    last = pe.matmul(ps[6][:, t * NE:(t + 1) * NE], h2T[:, k, t * P:(t + 1) * P], rw[:, k, :],
                                     start=(k == 0), stop=(k == KT - 1))
                last.then_inc(pe_logit, 1)
            for m in range(6):
                t, half = m // 2, m % 2
                if m >= 2:
                    pe.wait_ge(dve_x1, m - 1)
                for part in range(2):
                    col = part * D + half * 512
                    for k in range(KT):
                        last = pe.matmul(ps[2 * (m % 2) + part][:, :], yT[:, k, t * P:(t + 1) * P],
                                         ring[:, 4 + k, col:col + 512], start=(k == 0), stop=(k == KT - 1))
                    last.then_inc(pe_glu, 1)
                if m == 3:
                    transpose_h2(0)
                elif m == 4:
                    transpose_h2(1)
                    logits(0)
            logits(1)
            transpose_h2(2)
            logits(2)
            pe.wait_ge(dve_mask, 1)
            pe.wait_ge(pool_late, 13)
            pe.matmul(ps[7][:, 0:(NT + 1) * NE], tri[:, 1, :], earlier, start=True, stop=False, skip_group_check=True)
            last = pe.matmul(ps[7][:, 0:NT * NE], tri[:, 0, :], route[:, 20].rearrange("p t e -> p (t e)"),
                             start=False, stop=True, skip_group_check=True)
            last.then_inc(pe_pos, 1)

            def gather_x(nth):
                pe.wait_ge(oh_ready, nth + 1)
                for k in range(KT):
                    bank, col = (ps[5], k) if k < 5 else (ps[6], k - 5)
                    for t in range(NT):
                        last = pe.matmul(bank[:, col * CAP:(col + 1) * CAP], h2[:, t, k * P:(k + 1) * P],
                                         onehot[:, t, :], start=(t == 0), stop=(t == NT - 1))
                last.then_inc(xt_ps, 1)

            def expert(it, last_of_round, tiles):
                pe.wait_ge(xt_ev, it * 2 + 2)
                pe.wait_ge(prod_done, it * TT + TT)
                for k in range(KT):
                    pe.wait_ge(ld_unit[k], it * 32 + 32)
                    w = ring[:, k, :].rearrange("p (a n) -> p a n", a=2)
                    for t in range(tiles):
                        for j in range(4):
                            last = pe.matmul(ps[t][32 * j:32 * j + 32, :], xgT[:, k, 32 * t:32 * t + 32],
                                             w[:, :, 256 * j:256 * j + 256], start=(k == 0), stop=(k == KT - 1))
                    last.then_inc(unit_free, 1)
                if not last_of_round:
                    gather_x(it + 1)
                for t in range(tiles):
                    pe.wait_ge(prod_done, it * TT + (TT + t + 1))
                    if t == 2:
                        pe.wait_ge(y_ev, it * 12 + 12)
                    for c2 in range(2):
                        out = ps[7][:, 256 * t + P * c2:256 * t + P * c2 + P] if t < 2 else \
                            ps[4][:, 256 + P * c2:256 + P * c2 + P]
                        last = pe.transpose(out, act_a[:, t, c2 * P:(c2 + 1) * P], ident[:])
                    last.then_inc(at_ps, 1 if t < tiles - 1 else 1 + TT - tiles)
                pe.wait_ge(at_ev, it * 2 + 2)
                pe.wait_ge(y_ev, it * 12 + 12)
                for kk in range(KT):
                    j, c2 = kk // 2, kk % 2
                    if c2 == 0:
                        pe.wait_ge(ld_unit[KT + j], it * 32 + 32)
                    for t in range(tiles):
                        for dj in range(4):
                            last = pe.matmul(ps[3 + t // 2][32 * dj:32 * dj + 32, 256 * (t % 2):256 * (t % 2) + 256],
                                             aT[:, t, c2, 32 * j:32 * j + 32],
                                             ring[:, KT + j, c2 * D + 256 * dj:c2 * D + 256 * dj + 256],
                                             start=(kk == 0 and t != 1), stop=(kk == KT - 1),
                                             skip_group_check=True)
                    if c2 == 1:
                        last.then_inc(unit_free, 1)

            def expert_by_count(e, last_of_round):
                n = pe.value_load(counts[0:1, bass.ds(e, 1)], min_val=0, max_val=T)
                with pe.If(n > 64):
                    expert(e, last_of_round, TT)
                with pe.If(n <= 64):
                    expert(e, last_of_round, 2)

            gather_x(0)
            pe.wait_ge(dve_cmax, 1)
            with pe.Fori(0, NE - 1) as e:
                expert_by_count(e, False)
            expert_by_count(NE - 1, True)
            v = pe.value_load(cmaxi[0:1, 0:1], min_val=0, max_val=T)
            with pe.If(v > CAP):
                with pe.Fori(1, ROUNDS) as r:
                    gather_x(r * NE)
                    with pe.Fori(0, NE - 1) as e:
                        expert(r * NE + e, False, TT)
                    expert(r * NE + NE - 1, True, TT)
            pe.nop()

        @block.vector
        def _(dve):
            n = [0]

            def step(ins, wait=True):
                n[0] += 1
                ins.then_inc(dve_done, 1)
                if wait:
                    dve.wait_ge(dve_done, n[0])
            tt, ts, stt, cp = dve.tensor_tensor, dve.tensor_scalar, dve.scalar_tensor_tensor, dve.tensor_copy

            dve.wait_ge(ld_lam, 16 * 5)
            cp(dtexp[0:DG, :].rearrange("p (i s) -> p i s", i=2),
               dtnat[0:DG, :].rearrange("p (i a) -> p i a", a=1).to_broadcast((DG, 2, NS))).then_inc(dve_dt, 1)
            X, N_, R_, Q_ = (tab[:, i, :] for i in (0, 1, 2, 3))
            LR, LI, DT, MAG = (tab[:, i, :] for i in (9, 10, 11, 12))
            intv = tab[:, 4, :].bitcast(I32)
            dve.wait_ge(pe_tr, 2)
            step(cp(LR, ps[7][:, 0:DG]), False)
            step(cp(LI, ps[7][:, DG:2 * DG]), False)
            step(cp(X, ps[7][:, P:P + DG]))

            def exp_of(out):
                step(ts(N_, X, LOG2E, MAGIC, ALU.mult, ALU.add))
                step(ts(N_, N_, -MAGIC, None, ALU.add))
                step(ts(N_, N_, -126.0, 127.0, ALU.max, ALU.min))
                step(stt(R_, N_, -LN2_HI, X, ALU.mult, ALU.add))
                step(stt(R_, N_, -LN2_LO, R_, ALU.mult, ALU.add))
                step(ts(R_, R_, -88.0, 1.0, ALU.max, ALU.min))
                step(ts(Q_, R_, EXP_C[0], None, ALU.mult))
                for coef in EXP_C[1:]:
                    step(stt(Q_, Q_, coef, R_, ALU.add, ALU.mult))
                step(ts(Q_, Q_, 1.0, None, ALU.add))
                step(ts(N_, N_, 127.0, 8388608.0, ALU.add, ALU.mult))
                step(cp(intv, N_))
                step(tt(out, Q_, tab[:, 4, :], ALU.mult))
            exp_of(DT)
            TH = tab[:, 13, :]
            step(tt(TH, LI, DT, ALU.mult))
            step(ts(N_, TH, INV_2PI, MAGIC, ALU.mult, ALU.add))
            step(ts(N_, N_, -MAGIC, None, ALU.add))
            step(stt(TH, N_, -TP1, TH, ALU.mult, ALU.add))
            step(stt(TH, N_, -TP2, TH, ALU.mult, ALU.add))
            step(stt(TH, N_, -TP3, TH, ALU.mult, ALU.add))
            step(ts(tab[:, 5, :], TH, -PI_SAFE, PI_SAFE, ALU.max, ALU.min))
            step(stt(R_, tab[:, 5, :], -1.0, tab[:, 5, :], ALU.mult, ALU.max))
            ts(tab[:, 6, :], R_, -1.0, math.pi / 2, ALU.mult, ALU.add).then_inc(dve_trig, 1)
            dve.wait_ge(dve_trig, 1)
            step(tt(X, LR, DT, ALU.mult))
            exp_of(MAG)
            dve.wait_ge(act_trig, 2)
            WR = tab[:, 14:18, :].rearrange("p n g -> p (n g)").rearrange("p (g k) -> p g k", k=L)
            WI = tab[:, 18:22, :].rearrange("p n g -> p (n g)").rearrange("p (g k) -> p g k", k=L)
            VR = tab[:, 22:27, :].rearrange("p n g -> p (n g)").rearrange("p (g k) -> p g k", k=NP_V)
            VI = tab[:, 27:32, :].rearrange("p n g -> p (n g)").rearrange("p (g k) -> p g k", k=NP_V)
            AR, AI = tab[:, 4, :], tab[:, 5, :]
            step(tt(AR, MAG, tab[:, 8, :], ALU.mult), False)
            step(tt(tab[:, 6, :], MAG, tab[:, 7, :], ALU.mult))
            step(cp(AI, tab[:, 6, :]))
            PR, PI_ = tab[:, 7, :], tab[:, 8, :]
            step(dve.memset(PR, 1.0), False)
            step(dve.memset(PI_, 0.0))
            for k in range(NP_V):
                for d in range(2):
                    g = slice(d * GP, (d + 1) * GP)
                    if k < L:
                        step(cp(WR[:, g, L - 1 - k if d == 0 else k], PR[:, g]), False)
                        step(cp(WI[:, g, L - 1 - k if d == 0 else k], PI_[:, g]), False)
                    step(cp(VR[:, g, k if d == 0 else L - k], PR[:, g]), False)
                    step(cp(VI[:, g, k if d == 0 else L - k], PI_[:, g]), False)
                if k < L:
                    step(tt(X, PR, AR, ALU.mult), False)
                    step(tt(N_, PI_, AI, ALU.mult), False)
                    step(tt(R_, PR, AI, ALU.mult), False)
                    step(tt(Q_, PI_, AR, ALU.mult))
                    step(tt(PR, X, N_, ALU.subtract), False)
                    step(tt(PI_, R_, Q_, ALU.add))
            step(cp(a4r[:], PR), False)
            step(cp(a4i[:, 1, :], PI_), False)
            step(ts(a4i[:, 0, :], PI_, -1.0, None, ALU.mult), False)
            NR, DEN, FR, FI = tab[:, 6, :], tab[:, 13, :], tab[:, 7, :], tab[:, 8, :]
            step(ts(NR, AR, -1.0, None, ALU.add), False)
            step(tt(X, LR, LR, ALU.mult), False)
            step(tt(N_, LI, LI, ALU.mult))
            step(tt(DEN, X, N_, ALU.add))
            step(dve.reciprocal(DEN, DEN))
            step(tt(X, NR, LR, ALU.mult), False)
            step(tt(N_, AI, LI, ALU.mult), False)
            step(tt(R_, AI, LR, ALU.mult), False)
            step(tt(Q_, NR, LI, ALU.mult))
            step(tt(X, X, N_, ALU.add), False)
            step(tt(R_, R_, Q_, ALU.subtract))
            step(tt(FR, X, DEN, ALU.mult), False)
            step(tt(FI, R_, DEN, ALU.mult))
            dve.wait_ge(act_sq, NT)
            ts(stat[:, 4:4 + NT], stat[:, 0:NT], 1.0 / D, EPS, ALU.mult, ALU.add).then_inc(dve_ms, 1)

            def ada_rows(b):
                dve.wait_ge(pe_ada, KT * (b + 1))
                step(tt(ada[:, b, :], ps[ADA_BANK[b]][:, :], ada[:, b, :], ALU.add))
                if b == 0:
                    stt(ada[64:P, 0, :], ada[64:P, 0, :], 1.0, gains[64:P, :], ALU.add, ALU.mult).then_inc(dve_ada, 1)
                elif b == 2:
                    stt(ada[0:64, 2, :], ada[0:64, 2, :], 1.0, gains[0:64, :], ALU.add, ALU.mult).then_inc(dve_ada, 1)
                else:
                    dve.sem_inc(dve_ada, 1)
            dve.wait_ge(ld_rows, 16 * 6)
            ada_rows(0)

            def outer(out, tmp, pr, pi, three, r, g, nk):
                def powers(a):
                    return a[:, g, :].rearrange("p g (k a) -> p g k a", a=1).to_broadcast((P, GP, nk, GS))

                def rep(a):
                    return a[:, g, :].rearrange("p g (a h) -> p g a h", a=1).to_broadcast((P, GP, nk, GS))
                step(tt(out, powers(pr), rep(three[0]), ALU.mult), False)
                step(tt(tmp, powers(pi), rep(three[1]), ALU.mult))
                return tt(out, out, tmp, ALU.add)

            tmp_w = t2[:, 0:GP * L * GS].rearrange("p (g k h) -> p g k h", k=L, h=GS)
            tmp_v = t2.rearrange("p (g k h) -> p g k h", k=NP_V, h=GS)
            def w_part(b):
                d, r = divmod(b, 2)
                if b >= 2:
                    dve.wait_ge(pe_w, 4 * (b - 1))
                outer(w_pow[:, b % 2], tmp_w, WR, WI, (bs3[:, 1 + r], bs3[:, r]), r,
                      slice(d * GP, (d + 1) * GP), L).then_inc(dve_w, 1)
                dve.wait_ge(dve_w, b + 1)

            def v_part(d, r):
                g = slice(d * GP, (d + 1) * GP)
                outer(V[:, g, r], tmp_v, VR, VI, (cs3[:, r], cs3[:, 1 + r]), r, g, NP_V).then_inc(dve_v, 1)
                dve.wait_ge(dve_v, 2 * d + r + 1)

            dve.wait_ge(act_rt, 1)
            step(dve.reciprocal(stat[:, 4:4 + NT], stat[:, 4:4 + NT]))

            def modulate(t, src, dst, rows4, done):
                for b in range(2):
                    c2 = slice(512 * b, 512 * b + 512)
                    step(stt(dst[:, t, c2], src[:, t, c2], stat[:, 4 + t:5 + t], rows4[b], ALU.mult, ALU.mult),
                         b == 1)
                step(tt(dst[:, t, 0:512], dst[:, t, 0:512], rows4[2], ALU.add), False)
                tt(dst[:, t, 512:D], dst[:, t, 512:D], rows4[3], ALU.add).then_inc(done, 1)
                dve.wait_ge(dve_done, n[0])
            for t in range(NT):
                dve.wait_ge(pe_mod, 1 if t == 0 else 2)
                modulate(t, x_sb, x_sb, [ps[b + (4 if t else 0)][:, :] for b in range(4)], dve_h)
            dve.wait_ge(act_bc, 4)
            braw = t2[:, 0:2 * DG * GS].rearrange("p (r g h) -> p r g h", r=2, h=GS)

            def over_h(a):
                return a.rearrange("p (g a) -> p g a", a=1).to_broadcast((P, DG, GS))
            step(tt(bs3[:, 1], braw[:, 0], over_h(FR), ALU.mult), False)
            step(tt(bs3[:, 0], braw[:, 1], over_h(FI), ALU.mult), False)
            step(tt(bs3[:, 2], braw[:, 1], over_h(FR), ALU.mult))
            step(tt(braw[:, 0], braw[:, 0], over_h(FI), ALU.mult))
            step(tt(bs3[:, 1], bs3[:, 1], bs3[:, 0], ALU.subtract), False)
            step(tt(bs3[:, 2], bs3[:, 2], braw[:, 0], ALU.add))
            step(ts(bs3[:, 0], bs3[:, 2], -1.0, None, ALU.mult))
            w_part(0)
            w_part(1)
            dve.wait_ge(act_bc, 8)
            dve.wait_ge(act_sq, NT)
            dve.wait_ge(pe_bc, 8)
            v_part(0, 0)
            w_part(2)
            dve.wait_ge(pe_hT, 6)
            v_part(0, 1)
            w_part(3)
            v_part(1, 0)
            v_part(1, 1)
            for q in range(4):
                a = slice(32 * q, 32 * q + 32)
                step(cp(i16[a, :], ident[a, 32 * q:32 * q + 16]), q == 3)
            dve.wait_ge(ld_dtab, 16 * 8)
            step(tt(dskip[:, :, :, :],
                    i16[:, :].rearrange("p (a b h) -> p a b h", a=1, b=1).to_broadcast((P, 2, 8, GS)),
                    dtab[:, :, :].rearrange("p a (q h) -> p a q h", h=1).to_broadcast((P, 2, 8, GS)), ALU.mult))
            cp(b_keep, bs3[:, 1:3]).then_inc(dve_keep, 1)
            dve.wait_ge(pe_w, 16)
            step(dve.memset(uT[:, :, CC:CC + 1], 0.0), False)
            n_ut = n[0]
            for m in range(1, 8, 2):
                dve.wait_ge(pe_uT, m + 1)
                src = ps[4 + m % 4][:, 0:4 * C].rearrange("p (g c) -> p g c", c=C)
                step(cp(uT[:, 4 * m:4 * m + 4, 0:CC], src[:, :, 0:CC]), False)
                cp(uT[:, 4 * m:4 * m + 4, CC + 1:CX], src[:, :, CC:C]).then_inc(dve_uT, 2 if m == 1 else 1)
            for m in range(1, 32, 2):
                d, g0 = m // 16, 2 * (m % 16)
                dve.wait_ge(pe_p, m + 1)
                cp(S[:, d, 1 - d:1 - d + CX, :, g0:g0 + 2].rearrange("p c r g -> p g r c"),
                   ps[m % 8][:, 0:4 * CX].rearrange("p (g r c) -> p g r c", g=2, r=2)).then_inc(dve_p, 1)
            dve.wait_ge(act_p, 16)
            dve.wait_ge(dve_p, 16)
            dve.wait_ge(act_h0, 1)
            hv = h0[:, :].rearrange("p (r d g) -> p r d g", r=2, d=2)
            step(dve.memset(S[:, 0, 0, :, :], 0.0), False)
            step(cp(S[:, 0, CC + 1, :, :], hv[:, :, 0, :]), False)
            step(cp(S[:, 1, CX, :, :], hv[:, :, 1, :]))
            A4R = a4r[:, :].rearrange("p (d a g) -> p d a g", d=2, a=1).to_broadcast((P, 2, 2, GP))
            A4I = a4i[:, :, :].rearrange("p r (d g) -> p d r g", d=2)
            prev = [0, 0]
            for k in range(CL - 1):
                live = [st for st in range(2) if k < (CC, CL - 1)[st]]
                f = [k, CC + 1 + k]
                b = [CC - k, CX - k]
                mark = {}
                for st in live:
                    if prev[st]:
                        dve.wait_ge(dve_done, prev[st])
                    tb = [scan_t[:, st, x, :].rearrange("p (d r g) -> p d r g", d=2, r=2) for x in range(2)]
                    step(tt(tb[0], A4R, chunk_states(f[st], b[st] - f[st], False), ALU.mult), False)
                    step(tt(tb[1], A4I, chunk_states(f[st], b[st] - f[st], True), ALU.mult), False)
                    mark[st] = n[0]
                for x in range(2):
                    for st in live:
                        tb = scan_t[:, st, x, :].rearrange("p (d r g) -> p d r g", d=2, r=2)
                        to = chunk_states(f[st] + 1, b[st] - 1 - f[st] - 1, False)
                        dve.wait_ge(dve_done, mark[st] - (1 - x) if x == 0 else max(prev[st], mark[st]))
                        step(tt(to, to, tb, ALU.add), False)
                        prev[st] = n[0]
            dve.wait_ge(dve_done, n[0])
            dve.sem_inc(dve_scan, 1)

            for b in (1, 2):
                ada_rows(b)

            dve.wait_ge(ld_g1, 32)
            dve.wait_ge(ld_xagain, 16 * NT)
            for t in range(NT):
                for half in range(2):
                    m = 2 * t + half
                    c2 = slice(512 * half, 512 * half + 512)
                    dve.wait_ge(act_sig, m + 1)
                    step(tt(prod, sig, ps[2 * (m % 2)][:, :], ALU.mult))
                    step(tt(prod, prod, gate_rows[:, 1 if t else 0, c2], ALU.mult))
                    tt(x1[:, t, c2], x1[:, t, c2], prod, ALU.add).then_inc(dve_x1, 1)
                    dve.wait_ge(dve_x1, m + 1)
                dve.wait_ge(act_sq, NT + t + 1)
                ts(stat[:, 4 + t:5 + t], stat[:, t:t + 1], 1.0 / D, EPS, ALU.mult, ALU.add).then_inc(dve_ms, 1)
                dve.wait_ge(act_rt, 2 + t)
                step(dve.reciprocal(stat[:, 4 + t:5 + t], stat[:, 4 + t:5 + t]))
                dve.wait_ge(ld_mod2, 64)
                modulate(t, x1, h2, [mod2[:, 1 if t else 0, b // 2, 512 * (b % 2):512 * (b % 2) + 512]
                                     for b in range(4)], dve_h2)
            dve.wait_ge(act_score, 1)
            dve.wait_ge(pool_late, 13)
            dve.wait_ge(ld_route, 48)
            sc, bi = route[:, 0], route[:, 1]
            step(dve.memset(earlier[:, 0:NE], 0.0), False)

            def over_e(a):
                return a.to_broadcast((P, NT, NE))
            step(tt(bi, sc, rb.rearrange("p (a e) -> p a e", a=1).to_broadcast((P, NT, NE)), ALU.add))
            b4 = bi.rearrange("p t (g m a) -> p (t g) m a", g=NGRP, a=2)
            s2 = route[:, 2].rearrange("p t (g m) -> p (t g) m", g=NGRP)[:, :, 0:2]
            m2 = route[:, 3].rearrange("p t (g m) -> p (t g) m", g=NGRP)[:, :, 0:2]
            gsc = route[:, 4, :, 0:NGRP]
            g1 = route[:, 5, :, 0:NGRP]
            g2 = route[:, 6, :, 0:NGRP]
            step(tt(s2, b4[:, :, :, 0], b4[:, :, :, 1], ALU.add), False)
            step(tt(m2, b4[:, :, :, 0], b4[:, :, :, 1], ALU.max))

            def per_group(a, i):
                return a.rearrange("p t (g m) -> p t g m", g=NGRP)[:, :, :, i]
            step(tt(g1, per_group(route[:, 2], 0), per_group(route[:, 2], 1), ALU.max), False)
            step(tt(g2, per_group(route[:, 3], 0), per_group(route[:, 3], 1), ALU.add))
            step(tt(gsc, g1, g2, ALU.max))
            gm = route[:, 7, :, 0:1]

            def first_max(val, m1, key, rk, shape, out):
                step(dve.tensor_reduce(m1, val, AX.X, ALU.max))
                step(tt(key, val, m1.to_broadcast(shape), ALU.is_equal))
                step(tt(key, key, rk, ALU.mult))
                step(dve.tensor_reduce(m1, key, AX.X, ALU.max))
                step(tt(out, key, m1.to_broadcast(shape), ALU.is_equal))
            first_max(gsc, gm, g1, grank, (P, NT, NGRP), g2)
            mb = route[:, 8]
            mk = route[:, 9]
            step(cp(mk.rearrange("p t (g m) -> p t g m", g=NGRP),
                    g2.rearrange("p t (g a) -> p t g a", a=1).to_broadcast((P, NT, NGRP, EPG))))
            step(tt(mb, bi, mk, ALU.mult), False)
            step(ts(mk, mk, 1e30, -1e30, ALU.mult, ALU.add))
            step(tt(mb, mb, mk, ALU.add))
            oh = [route[:, 10], route[:, 11]]
            first_max(mb, route[:, 12, :, 0:1], route[:, 13], rank, (P, NT, NE), oh[0])
            step(stt(mb, oh[0], -2e30, mb, ALU.mult, ALU.add))
            first_max(mb, route[:, 14, :, 0:1], route[:, 15], rank, (P, NT, NE), oh[1])
            mask = route[:, 20]
            step(tt(mask, oh[0], oh[1], ALU.add))
            step(cp(earlier[:, NE:2 * NE], mask[:, 0, :]), False)
            step(tt(earlier[:, 2 * NE:3 * NE], mask[:, 0, :], mask[:, 1, :], ALU.add))
            tt(earlier[:, 3 * NE:4 * NE], earlier[:, 2 * NE:3 * NE], mask[:, 2, :], ALU.add).then_inc(dve_mask, 1)
            for k in range(2):
                step(tt(route[:, 16 + k], sc, oh[k], ALU.mult))
                step(dve.tensor_reduce(cmb[:, k, :], route[:, 16 + k], AX.X, ALU.add))
            wsum = route[:, 18, 0, 0:NT]
            step(tt(wsum, cmb[:, 0, :], cmb[:, 1, :], ALU.add))
            step(dve.reciprocal(wsum, wsum))
            for k in range(2):
                step(tt(cmb[:, k, :], cmb[:, k, :], wsum, ALU.mult))
            dve.wait_ge(pe_pos, 1)
            place = ps[7][:, 0:NT * NE].rearrange("p (t e) -> p t e", t=NT)
            step(stt(posm, place, 1.0, route[:, 20], ALU.add, ALU.mult))
            step(ts(posm, posm, -1.0, None, ALU.add))

            def find_tokens(e):
                tt(onehot, posm[:, :, bass.ds(e, 1)].to_broadcast((P, NT, CAP)),
                   slot_no.rearrange("p (a n) -> p a n", a=1).to_broadcast((P, NT, CAP)), ALU.is_equal
                   ).then_inc(oh_ready, 1)
            find_tokens(0)
            step(cp(counts[:], ps[7][:, NT * NE:(NT + 1) * NE]))
            step(dve.tensor_reduce(cmax[:], ps[7][:, NT * NE:(NT + 1) * NE], AX.X, ALU.max))
            cp(cmaxi[:], cmax[:]).then_inc(dve_cmax, 1)
            rnd = route[:, 18]
            step(ts(rnd, place, float(CAP), None, ALU.is_ge))
            for k in range(2, ROUNDS):
                step(stt(rnd, place, float(k * CAP), rnd, ALU.is_ge, ALU.add))
            step(stt(route[:, 21], place, float(NE * ROUNDS), e_slot, ALU.mult, ALU.add))
            step(stt(route[:, 21], rnd, float(1 - CAP * NE * ROUNDS), route[:, 21], ALU.mult, ALU.add))
            for k in range(2):
                step(tt(route[:, 22 + k], route[:, 21], oh[k], ALU.mult))
                step(dve.tensor_reduce(route[:, 19, k, 0:NT], route[:, 22 + k], AX.X, ALU.add))
                ins = cp(sloti[:, k, :], route[:, 19, k, 0:NT])
                if k == 0:
                    step(ins)
            ins.then_inc(dve_slot, 1)

            def evict_x(nth):
                dve.wait_ge(xt_ps, nth + 1)
                cp(xgT[:, 0:5, :], ps[5][:, 0:5 * CAP].rearrange("p (k n) -> p k n", k=5)).then_inc(xt_ev, 1)
                cp(xgT[:, 5:8, :], ps[6][:, 0:3 * CAP].rearrange("p (k n) -> p k n", k=3)).then_inc(xt_ev, 1)

            def expert(it, last_of_round, next_but_one):
                for t in range(TT):
                    dve.wait_ge(silu_done, it * TT + (t + 1))
                    tt(act_a[:, t, :], sg[:, t, :], ps[t][:, 256:512], ALU.mult).then_inc(prod_done, 1)
                if not last_of_round:
                    evict_x(it + 1)
                if next_but_one is not None:
                    find_tokens(next_but_one)
                dve.wait_ge(unit_free, it * NU + NU)
                dve.wait_ge(y_free, it + 1)
                for t in range(TT):
                    for j in range(2, 4):
                        src = ps[3 + t // 2][32 * j:32 * j + 32, 256 * (t % 2):256 * (t % 2) + 256]
                        cp(yrow[32 * t:32 * t + 32, 256 * j:256 * j + 256], src).then_inc(y_ev, 1)
            dve.sem_inc(prod_done, TT)
            dve.sem_inc(y_ev, 12)
            evict_x(0)
            find_tokens(1)
            with dve.Fori(0, NE - 2) as e:
                expert(e, False, e + 2)
            expert(NE - 2, False, None)
            expert(NE - 1, True, None)
            v = dve.value_load(cmaxi[0:1, 0:1], min_val=0, max_val=T)
            with dve.If(v > CAP):
                with dve.Fori(1, ROUNDS) as r:
                    ts(posm, posm, float(-CAP), None, ALU.add).then_inc(dve_round, 1)
                    dve.wait_ge(dve_round, r)
                    find_tokens(0)
                    evict_x(r * NE)
                    find_tokens(1)
                    with dve.Fori(0, NE - 2) as e:
                        expert(r * NE + e, False, e + 2)
                    expert(r * NE + NE - 2, False, None)
                    expert(r * NE + NE - 1, True, None)
            dve.nop()
            dve.wait_ge(ld_g2, 32)

            def combine(t):
                dve.wait_ge(act_mo, t + 1)
                step(stt(m_out[:, t, :], y2c[:, 1, t, :], cmb[:, 1, t:t + 1], m_out[:, t, :], ALU.mult, ALU.add))
                step(tt(m_out[:, t, :], m_out[:, t, :], gate_rows[:, 1 if t else 0, :], ALU.mult))
                tt(x1[:, t, :], x1[:, t, :], m_out[:, t, :], ALU.add).then_inc(dve_x2, 1)

            def mean_square(t):
                dve.wait_ge(act_sq, 2 * NT + t + 1)
                ts(stat[:, 4 + t:5 + t], stat[:, t:t + 1], 1.0 / D, EPS, ALU.mult, ALU.add).then_inc(dve_ms, 1)

            def final_norm(t):
                dve.wait_ge(act_rt, 2 + NT + t)
                step(dve.reciprocal(stat[:, 4 + t:5 + t], stat[:, 4 + t:5 + t]))
                stt(yo[:, t, :], x1[:, t, :], stat[:, 4 + t:5 + t], gfin, ALU.mult, ALU.mult).then_inc(dve_out, 1)
            combine(0)
            combine(1)
            mean_square(0)
            combine(2)
            mean_square(1)
            final_norm(0)
            mean_square(2)
            final_norm(1)
            final_norm(2)


_INS = ["x_prompt", "x_sample", "c", "state_ssm_re", "state_ssm_im", "c_ctx", "norm_mix", "norm_ffn",
        "w_ada", "b_ada", "ssm_w_in", "ssm_lam_re", "ssm_lam_im", "ssm_log_dt", "ssm_b_re", "ssm_b_im",
        "ssm_c_re", "ssm_c_im", "ssm_d", "ssm_w_glu", "router_w", "router_b", "moe_w_gate", "moe_w_up",
        "moe_w_down", "norm_final"]
_OUTS = [("y_prompt", (1, T_CTX, D)), ("y_sample", (1, T_LAT, D)),
         ("new_re", (1, 1, 2, G, NS)), ("new_im", (1, 1, 2, G, NS))]


def kernel(**inputs):
    import numpy as np
    import concourse.bacc as bacc
    from concourse.bass_utils import run_bass_kernel_spmd

    nc = bacc.Bacc("TRN2", target_bir_lowering=False, num_devices=1)
    arrays, args = {}, []
    for name in _INS:
        a = np.ascontiguousarray(inputs[name])
        arrays[f"in_{name}"] = a
        args.append(nc.dram_tensor(f"in_{name}", a.shape, mybir.dt.from_np(a.dtype), kind="ExternalInput").ap())
    for name, shape in _OUTS:
        args.append(nc.dram_tensor(f"out_{name}", shape, F32, kind="ExternalOutput").ap())
    build(nc, *args)
    r = run_bass_kernel_spmd(nc, [arrays], core_ids=[0])
    return tuple(r.results[0][f"out_{name}"] for name, _ in _OUTS)
```
